# Optimizing a Trainium2 kernel written in Bass

```python
import math
import jax
import jax.numpy as jnp
from jax import lax
import numpy as np
import jax, jax.numpy as jnp

D_MODEL = 1024
BATCH = 1
SEQ = 256
DEPTH = 2

GRID_W = 64
CTX_LEN = 256
D_CONV = 512
CONV_K = 31
D_SSD = 512
SSD_HEADDIM = 64
SSD_HEADS = D_SSD // SSD_HEADDIM
SSD_GROUPS = 2
SSD_STATE = 128
SSD_CONV_K = 5
SSD_CHUNK = 128
D_BC = SSD_GROUPS * SSD_STATE
D_XBC = D_SSD + 2 * D_BC
D_MIX = D_CONV + D_SSD
D_IN = 2 * D_CONV + D_SSD + D_XBC + 2 * SSD_HEADS
MOE_GROUPS = 4
MOE_PER_GROUP = 4
N_EXPERTS = MOE_GROUPS * MOE_PER_GROUP
MOE_TOPK = 2
EXPERT_FF = 256
RMS_EPS = 1e-6
LN_EPS = 1e-5


def rms_norm(x, g):
    xf = x.astype(jnp.float32)
    y = xf * lax.rsqrt(jnp.mean(jnp.square(xf), axis=-1, keepdims=True) + RMS_EPS)
    return (y * g.astype(jnp.float32)).astype(x.dtype)

def layer_norm(x, g, b):
    xf = x.astype(jnp.float32)
    mu = jnp.mean(xf, axis=-1, keepdims=True)
    var = jnp.mean(jnp.square(xf - mu), axis=-1, keepdims=True)
    y = (xf - mu) * lax.rsqrt(var + LN_EPS)
    return (y * g.astype(jnp.float32) + b.astype(jnp.float32)).astype(x.dtype)

def modulate(h, shift, scale):
    return h * (1.0 + scale) + shift

def ada_mod(cvec, w_ada, b_ada, n):
    m = jax.nn.silu(cvec) @ w_ada[:, :n * D_MODEL] + b_ada[:n * D_MODEL]
    return jnp.split(m, n, axis=-1)

def dwconv_seq(v, w):
    k, ch = w.shape
    return lax.conv_general_dilated(
        v, w[:, None, :].astype(v.dtype), (1,), [(k // 2, k // 2)],
        dimension_numbers=("NWC", "WIO", "NWC"), feature_group_count=ch)

def dwconv_grid(v, w, axis):
    k, ch = w.shape
    if axis == 1:
        taps, pad = w[:, None, None, :], [(k // 2, k // 2), (0, 0)]
    else:
        taps, pad = w[None, :, None, :], [(0, 0), (k // 2, k // 2)]
    return lax.conv_general_dilated(
        v, taps.astype(v.dtype), (1, 1), pad,
        dimension_numbers=("NHWC", "HWIO", "NHWC"), feature_group_count=ch)

def split_proj(proj):
    o1, o2, o3, o4 = D_CONV, 2 * D_CONV, 2 * D_CONV + D_SSD, 2 * D_CONV + D_SSD + D_XBC
    return proj[..., :o1], proj[..., o1:o2], proj[..., o2:o3], proj[..., o3:o4], proj[..., o4:]

def conformer_conv(u, gate, p, rows):
    v = u * jax.nn.sigmoid(gate)
    if rows is None:
        y = dwconv_seq(v, p["conv_w"])
    else:
        b, l, ch = v.shape
        half = ch // 2
        vg = v.reshape(b, rows, GRID_W, ch)
        y = jnp.concatenate([dwconv_grid(vg[..., :half], p["conv_w"][:, :half], 2),
                             dwconv_grid(vg[..., half:], p["conv_w"][:, half:], 1)],
                            axis=-1).reshape(b, l, ch)
    return jax.nn.silu(layer_norm(y + p["conv_b"], p["conv_ln_g"], p["conv_ln_b"]))

def group_to_heads(v):
    b, l, _ = v.shape
    return jnp.repeat(v.reshape(b, l, SSD_GROUPS, SSD_STATE), SSD_HEADS // SSD_GROUPS, axis=2)

def ssd_scan_inputs(xbc_raw, dt_raw, p):
    b, l, ch = xbc_raw.shape
    xbc = jax.nn.silu(dwconv_seq(xbc_raw, p["ssd_conv_w"][:, :ch]) + p["ssd_conv_b"][:ch])
    xs = xbc[..., :D_SSD].reshape(b, l, SSD_HEADS, SSD_HEADDIM)
    bm = group_to_heads(xbc[..., D_SSD:D_SSD + D_BC])
    cm = group_to_heads(xbc[..., D_SSD + D_BC:]) if ch == D_XBC else None
    dt = jax.nn.softplus(dt_raw.astype(jnp.float32).reshape(b, l, 2, SSD_HEADS)
                         + p["dt_bias"].astype(jnp.float32))
    return xs, bm, cm, dt

def flip_seq(t):
    return jnp.flip(t, axis=1)

def ssd_chunked(xs, dt, a, bm, cm, h0):
    b, l, nh, hp = xs.shape
    n = bm.shape[-1]
    nc = l // SSD_CHUNK
    a_cum = jnp.cumsum((dt * a).reshape(b, nc, SSD_CHUNK, nh), axis=2)
    xdt = (xs * dt[..., None]).reshape(b, nc, SSD_CHUNK, nh, hp)
    bc = bm.reshape(b, nc, SSD_CHUNK, nh, n)
    cc = cm.reshape(b, nc, SSD_CHUNK, nh, n)
    causal = jnp.tril(jnp.ones((SSD_CHUNK, SSD_CHUNK), dtype=bool))
    seg = a_cum[:, :, :, None, :] - a_cum[:, :, None, :, :]
    decay_ls = jnp.exp(jnp.where(causal[None, None, :, :, None], seg, -jnp.inf))
    scores = jnp.einsum("bclhn,bcshn->bclsh", cc, bc) * decay_ls
    y_diag = jnp.einsum("bclsh,bcshp->bclhp", scores, xdt)
    decay_to_end = jnp.exp(a_cum[:, :, -1:, :] - a_cum)
    chunk_states = jnp.einsum("bclh,bclhn,bclhp->bchpn", decay_to_end, bc, xdt)
    chunk_decay = jnp.exp(a_cum[:, :, -1, :])

    def step(h, inp):
        s, d = inp
        return h * d[:, :, None, None] + s, h

    _, h_prev = lax.scan(step, h0.astype(chunk_states.dtype),
                         (jnp.swapaxes(chunk_states, 0, 1), jnp.swapaxes(chunk_decay, 0, 1)))
    h_prev = jnp.swapaxes(h_prev, 0, 1)
    y_off = jnp.einsum("bclhn,bchpn,bclh->bclhp", cc, h_prev, jnp.exp(a_cum))
    return (y_diag + y_off).reshape(b, l, nh, hp)

def ssd_final_state(xs, dt, a, bm):
    la = jnp.cumsum(dt * a, axis=1)
    w = jnp.exp(la[:, -1:, :] - la) * dt
    return jnp.einsum("blh,blhn,blhp->bhpn", w, bm, xs)

def context_states(xs, bm, dt, a):
    hf = ssd_final_state(xs, dt[:, :, 0], a[0], bm)
    hb = ssd_final_state(flip_seq(xs), flip_seq(dt[:, :, 1]), a[1], flip_seq(bm))
    return hf, hb

def mixer_output(u, gate, z, xs, bm, cm, dt, a, h0_f, h0_b, p, rows):
    conv_out = conformer_conv(u, gate, p, rows)
    y_f = ssd_chunked(xs, dt[:, :, 0], a[0], bm, cm, h0_f)
    y_b = flip_seq(ssd_chunked(flip_seq(xs), flip_seq(dt[:, :, 1]), a[1],
                               flip_seq(bm), flip_seq(cm), h0_b))
    y = y_f + y_b + p["d_skip"][:, None] * xs
    b, l = xs.shape[:2]
    ssd_out = rms_norm(y.reshape(b, l, D_SSD) * jax.nn.silu(z), p["ssd_norm_g"])
    return jnp.concatenate([conv_out, ssd_out], axis=-1) @ p["w_out"]

def hier_moe(h, p):
    b, l, d = h.shape
    t = h.reshape(b * l, d)
    g_logits = (t @ p["w_rg"] + p["b_rg"]).astype(jnp.float32)
    g_sel = jnp.argmax(g_logits, axis=-1)
    g_prob = jnp.take_along_axis(jax.nn.softmax(g_logits, axis=-1), g_sel[:, None], axis=-1)
    e_logits = (t @ p["w_re"] + p["b_re"]).astype(jnp.float32).reshape(-1, MOE_GROUPS, MOE_PER_GROUP)
    e_logits = jnp.take_along_axis(e_logits, g_sel[:, None, None], axis=1)[:, 0]
    top_v, top_i = lax.top_k(jax.nn.softmax(e_logits, axis=-1), MOE_TOPK)
    w_sel = g_prob * top_v / jnp.sum(top_v, axis=-1, keepdims=True)
    e_id = g_sel[:, None] * MOE_PER_GROUP + top_i
    comb = jnp.einsum("tk,tke->et", w_sel, jax.nn.one_hot(e_id, N_EXPERTS, dtype=jnp.float32))

    def expert(acc, ew):
        wg, wu, wd, cw = ew
        hid = jax.nn.silu(t @ wg) * (t @ wu)
        return acc + (cw[:, None] * (hid @ wd)).astype(acc.dtype), None

    out, _ = lax.scan(expert, jnp.zeros(t.shape, jnp.float32),
                      (p["w_gate"], p["w_up"], p["w_down"], comb))
    return out.reshape(b, l, d)

def first_inputs(seed: int = 0) -> dict:
    key = jax.random.key(seed)
    ks = iter(jax.random.split(key, 40))
    f32 = jnp.float32

    def nrm(shape, scale):
        return scale * jax.random.normal(next(ks), shape, f32)

    def gain(shape):
        return 1.0 + nrm(shape, 0.02)

    dt0 = jnp.exp(jax.random.uniform(next(ks), (DEPTH, 2, SSD_HEADS), f32,
                                     math.log(1e-3), math.log(1e-1)))
    return {
        "x": nrm((BATCH, SEQ, D_MODEL), 1.0),
        "c": nrm((BATCH, D_MODEL), 1.0),
        "ctx": nrm((BATCH, CTX_LEN, D_MODEL), 1.0),
        "c_ctx": nrm((D_MODEL,), 1.0),
        "w_ada": nrm((DEPTH, D_MODEL, 6 * D_MODEL), 0.5 * D_MODEL ** -0.5),
        "b_ada": nrm((DEPTH, 6 * D_MODEL), 0.02),
        "g_mix": gain((DEPTH, D_MODEL)),
        "g_ffn": gain((DEPTH, D_MODEL)),
        "w_in": nrm((DEPTH, D_MODEL, D_IN), D_MODEL ** -0.5),
        "conv_w": nrm((DEPTH, CONV_K, D_CONV), CONV_K ** -0.5),
        "conv_b": nrm((DEPTH, D_CONV), 0.02),
        "conv_ln_g": gain((DEPTH, D_CONV)),
        "conv_ln_b": nrm((DEPTH, D_CONV), 0.02),
        "ssd_conv_w": nrm((DEPTH, SSD_CONV_K, D_XBC), SSD_CONV_K ** -0.5),
        "ssd_conv_b": nrm((DEPTH, D_XBC), 0.02),
        "dt_bias": dt0 + jnp.log(-jnp.expm1(-dt0)),
        "a_log": jnp.log(jax.random.uniform(next(ks), (DEPTH, 2, SSD_HEADS), f32, 1.0, 16.0)),
        "d_skip": gain((DEPTH, SSD_HEADS)),
        "ssd_norm_g": gain((DEPTH, D_SSD)),
        "w_out": nrm((DEPTH, D_MIX, D_MODEL), D_MIX ** -0.5),
        "w_router_group": nrm((DEPTH, D_MODEL, MOE_GROUPS), D_MODEL ** -0.5),
        "b_router_group": nrm((DEPTH, MOE_GROUPS), 0.01),
        "w_router_expert": nrm((DEPTH, D_MODEL, N_EXPERTS), D_MODEL ** -0.5),
        "b_router_expert": nrm((DEPTH, N_EXPERTS), 0.01),
        "w_gate": nrm((DEPTH, N_EXPERTS, D_MODEL, EXPERT_FF), D_MODEL ** -0.5),
        "w_up": nrm((DEPTH, N_EXPERTS, D_MODEL, EXPERT_FF), D_MODEL ** -0.5),
        "w_down": nrm((DEPTH, N_EXPERTS, EXPERT_FF, D_MODEL), EXPERT_FF ** -0.5),
        "g_final": gain((D_MODEL,)),
    }

def first_block(x, c, ctx, c_ctx, w_ada, b_ada, g_mix, g_ffn, w_in, conv_w, conv_b, conv_ln_g,
              conv_ln_b, ssd_conv_w, ssd_conv_b, dt_bias, a_log, d_skip, ssd_norm_g, w_out,
              w_router_group, b_router_group, w_router_expert, b_router_expert,
              w_gate, w_up, w_down, g_final):
    rows = x.shape[1] // GRID_W
    h_x, h_c = x, ctx
    lo = 2 * D_CONV + D_SSD
    for l in range(DEPTH):
        last = l == DEPTH - 1
        p = {"w_in": w_in[l], "conv_w": conv_w[l], "conv_b": conv_b[l], "conv_ln_g": conv_ln_g[l],
             "conv_ln_b": conv_ln_b[l], "ssd_conv_w": ssd_conv_w[l], "ssd_conv_b": ssd_conv_b[l],
             "dt_bias": dt_bias[l], "d_skip": d_skip[l], "ssd_norm_g": ssd_norm_g[l],
             "w_out": w_out[l], "w_rg": w_router_group[l], "b_rg": b_router_group[l],
             "w_re": w_router_expert[l], "b_re": b_router_expert[l],
             "w_gate": w_gate[l], "w_up": w_up[l], "w_down": w_down[l]}
        a = -jnp.exp(a_log[l].astype(jnp.float32))
        sh1, sc1, gt1, sh2, sc2, gt2 = [m[:, None, :] for m in ada_mod(c, w_ada[l], b_ada[l], 6)]

        if last:
            csh1, csc1 = ada_mod(c_ctx, w_ada[l], b_ada[l], 2)
            hc = modulate(rms_norm(h_c, g_mix[l]), csh1, csc1)
            w_xb_dt = jnp.concatenate([p["w_in"][:, lo:lo + D_SSD + D_BC], p["w_in"][:, lo + D_XBC:]], axis=1)
            proj_c = hc @ w_xb_dt
            xs_c, bm_c, _, dt_c = ssd_scan_inputs(proj_c[..., :D_SSD + D_BC], proj_c[..., D_SSD + D_BC:], p)
        else:
            csh1, csc1, cgt1, csh2, csc2, cgt2 = ada_mod(c_ctx, w_ada[l], b_ada[l], 6)
            hc = modulate(rms_norm(h_c, g_mix[l]), csh1, csc1)
            uc, gc, zc, xbc_c, dtr_c = split_proj(hc @ p["w_in"])
            xs_c, bm_c, cm_c, dt_c = ssd_scan_inputs(xbc_c, dtr_c, p)
        hf0, hb0 = context_states(xs_c, bm_c, dt_c, a)

        hx = modulate(rms_norm(h_x, g_mix[l]), sh1, sc1)
        u, gate, z, xbc, dt_raw = split_proj(hx @ p["w_in"])
        xs, bm, cm, dt = ssd_scan_inputs(xbc, dt_raw, p)
        h_x = h_x + gt1 * mixer_output(u, gate, z, xs, bm, cm, dt, a, hf0, hb0, p, rows)
        h_x = h_x + gt2 * hier_moe(modulate(rms_norm(h_x, g_ffn[l]), sh2, sc2), p)

        if not last:
            zero = jnp.zeros_like(hf0)
            h_c = h_c + cgt1 * mixer_output(uc, gc, zc, xs_c, bm_c, cm_c, dt_c, a, zero, zero, p, None)
            h_c = h_c + cgt2 * hier_moe(modulate(rms_norm(h_c, g_ffn[l]), csh2, csc2), p)

    return rms_norm(h_x, g_final).astype(x.dtype)


DEPTH_2 = 4

CHUNK = 64
N_MIXERS = 3
EPS = 1e-6
N_FOX = (DEPTH_2 + 2) // 3
N_S5 = (DEPTH_2 + 1) // 3
N_POOL = DEPTH_2 // 3
FOX_HEADS = 16
FOX_HEAD_DIM = D_MODEL // FOX_HEADS
Q_BLOCK = 128
FOX_IN = 3 * D_MODEL + FOX_HEADS
FORGET_BIAS_CENTER = 3.0
S5_GROUP = 16
S5_GROUPS = D_MODEL // S5_GROUP
S5_STATE = 64
S5_DT_MIN = 1e-3
S5_DT_MAX = 1e-1
POOL_WINDOWS = (2, 4, 8, 16)
POOL_GROUPS = len(POOL_WINDOWS)
POOL_WIDTH = D_MODEL // POOL_GROUPS
D_FF = -(-8 * D_MODEL // (3 * 256)) * 256


F32 = jnp.float32

def rms_norm_2(x, g):
    xf = x.astype(F32)
    y = xf * lax.rsqrt(jnp.mean(xf * xf, axis=-1, keepdims=True) + EPS)
    return (y * g.astype(F32)).astype(x.dtype)

def forgetting_attention(h, w_in, b_f, w_out):
    B, S, _ = h.shape
    proj = h @ w_in
    q, k, v, f_logit = jnp.split(proj, [D_MODEL, 2 * D_MODEL, 3 * D_MODEL], axis=-1)

    def heads(t):
        return t.reshape(B, S, FOX_HEADS, FOX_HEAD_DIM).transpose(0, 2, 1, 3).astype(F32)

    q, k, v = heads(q), heads(k), heads(v)
    log_f = jax.nn.log_sigmoid(f_logit.astype(F32) + b_f.astype(F32))
    c = jnp.cumsum(log_f, axis=1).transpose(0, 2, 1)
    n_blk = S // Q_BLOCK
    q_blocks = q.reshape(B, FOX_HEADS, n_blk, Q_BLOCK, FOX_HEAD_DIM).transpose(2, 0, 1, 3, 4)
    c_blocks = c.reshape(B, FOX_HEADS, n_blk, Q_BLOCK).transpose(2, 0, 1, 3)
    starts = jnp.arange(n_blk, dtype=jnp.int32) * Q_BLOCK
    key_pos = jnp.arange(S, dtype=jnp.int32)
    scale = FOX_HEAD_DIM ** -0.5

    def one_block(args):
        q_b, c_b, start = args
        logits = jnp.einsum('bhqd,bhkd->bhqk', q_b, k) * scale
        logits = logits + c_b[..., :, None] - c[..., None, :]
        q_pos = start + jnp.arange(Q_BLOCK, dtype=jnp.int32)
        mask = key_pos[None, :] <= q_pos[:, None]
        p = jax.nn.softmax(jnp.where(mask, logits, -jnp.inf), axis=-1)
        return jnp.einsum('bhqk,bhkd->bhqd', p, v)

    out = lax.map(one_block, (q_blocks, c_blocks, starts))
    out = out.transpose(1, 0, 3, 2, 4).reshape(B, S, D_MODEL).astype(h.dtype)
    return out @ w_out

def s5_layer(h, w_in, a_re, a_im, log_dt, b_re, b_im, c_re, c_im, d, w_glu):
    B, S, _ = h.shape
    u = (h @ w_in).astype(F32)
    u_g = u.reshape(B, S, S5_GROUPS, S5_GROUP).astype(jnp.complex64)
    lam = lax.complex(a_re.astype(F32), a_im.astype(F32))
    dt = jnp.exp(log_dt.astype(F32))[:, None]
    lam_bar = jnp.exp(lam * dt)
    b_mat = lax.complex(b_re.astype(F32), b_im.astype(F32))
    b_bar = ((lam_bar - 1.0) / lam)[..., None] * b_mat
    bu = jnp.einsum('gpc,bsgc->bsgp', b_bar, u_g)
    lam_seq = jnp.broadcast_to(lam_bar, bu.shape)

    def combine(left, right):
        a_l, s_l = left
        a_r, s_r = right
        return a_r * a_l, a_r * s_l + s_r

    _, states = lax.associative_scan(combine, (lam_seq, bu), axis=1)
    c_mat = lax.complex(c_re.astype(F32), c_im.astype(F32))
    y = jnp.einsum('gcp,bsgp->bsgc', c_mat, states).real.reshape(B, S, D_MODEL)
    y = y + d.astype(F32) * u
    g = jax.nn.gelu(y).astype(h.dtype)
    val, gate = jnp.split(g @ w_glu, 2, axis=-1)
    return val * jax.nn.sigmoid(gate)

def multiscale_pool(h, w_grp, b_grp, scale):
    B, S, _ = h.shape
    hf = h.astype(F32).reshape(B, S, POOL_GROUPS, POOL_WIDTH)
    count_base = jnp.arange(1, S + 1, dtype=F32)[None, :, None]
    outs = []
    for gi, w in enumerate(POOL_WINDOWS):
        xg = hf[:, :, gi]
        cs = jnp.cumsum(xg, axis=1)
        lag = jnp.pad(cs[:, :-w], ((0, 0), (w, 0), (0, 0)))
        mean = (cs - lag) / jnp.minimum(count_base, float(w))
        outs.append(jnp.einsum('bsc,cd->bsd', mean - xg, w_grp[gi].astype(F32)))
    y = jnp.concatenate(outs, axis=-1) + b_grp.astype(F32)
    return (y * scale.astype(F32)).astype(h.dtype)

def swiglu(h, w_gate_up, w_down):
    g, u = jnp.split(h @ w_gate_up, 2, axis=-1)
    return (jax.nn.silu(g) * u) @ w_down

def second_inputs(seed: int = 0) -> dict:
    key = jax.random.key(seed)
    ks = jax.random.split(key, 24)
    D, H, G, P, C = D_MODEL, FOX_HEADS, S5_GROUPS, S5_STATE, S5_GROUP
    nrm = jax.random.normal
    x = nrm(ks[0], (BATCH, SEQ, D), F32)
    mix_norm_g = 1.0 + 0.05 * nrm(ks[1], (DEPTH_2, D), F32)
    ffn_norm_g = 1.0 + 0.05 * nrm(ks[2], (DEPTH_2, D), F32)
    final_norm_g = 1.0 + 0.05 * nrm(ks[3], (D,), F32)
    fox_w_in = nrm(ks[4], (N_FOX, D, FOX_IN), F32) * D ** -0.5
    fox_b_f = FORGET_BIAS_CENTER + 0.5 * nrm(ks[5], (N_FOX, H), F32)
    fox_w_out = nrm(ks[6], (N_FOX, D, D), F32) * D ** -0.5
    s5_w_in = nrm(ks[7], (N_S5, D, D), F32) * D ** -0.5
    s5_a_re = -0.5 + 0.01 * nrm(ks[8], (N_S5, G, P), F32)
    s5_a_im = math.pi * jnp.arange(P, dtype=F32)[None, None, :] + 0.01 * nrm(ks[9], (N_S5, G, P), F32)
    s5_log_dt = jax.random.uniform(ks[10], (N_S5, G), F32, math.log(S5_DT_MIN), math.log(S5_DT_MAX))
    s5_b_re = nrm(ks[11], (N_S5, G, P, C), F32) * (2 * C) ** -0.5
    s5_b_im = nrm(ks[12], (N_S5, G, P, C), F32) * (2 * C) ** -0.5
    s5_c_re = nrm(ks[13], (N_S5, G, C, P), F32) * P ** -0.5
    s5_c_im = nrm(ks[14], (N_S5, G, C, P), F32) * P ** -0.5
    s5_d = nrm(ks[15], (N_S5, D), F32)
    s5_w_glu = nrm(ks[16], (N_S5, D, 2 * D), F32) * D ** -0.5
    pool_w = nrm(ks[17], (N_POOL, POOL_GROUPS, POOL_WIDTH, POOL_WIDTH), F32) * POOL_WIDTH ** -0.5
    pool_b = 0.01 * nrm(ks[18], (N_POOL, D), F32)
    pool_scale = 0.5 + 0.05 * nrm(ks[19], (N_POOL, D), F32)
    ffn_w_gate_up = nrm(ks[20], (DEPTH_2, D, 2 * D_FF), F32) * D ** -0.5
    ffn_w_down = nrm(ks[21], (DEPTH_2, D_FF, D), F32) * D_FF ** -0.5
    return {"x": x, "mix_norm_g": mix_norm_g, "ffn_norm_g": ffn_norm_g, "final_norm_g": final_norm_g,
            "fox_w_in": fox_w_in, "fox_b_f": fox_b_f, "fox_w_out": fox_w_out,
            "s5_w_in": s5_w_in, "s5_a_re": s5_a_re, "s5_a_im": s5_a_im, "s5_log_dt": s5_log_dt,
            "s5_b_re": s5_b_re, "s5_b_im": s5_b_im, "s5_c_re": s5_c_re, "s5_c_im": s5_c_im,
            "s5_d": s5_d, "s5_w_glu": s5_w_glu,
            "pool_w": pool_w, "pool_b": pool_b, "pool_scale": pool_scale,
            "ffn_w_gate_up": ffn_w_gate_up, "ffn_w_down": ffn_w_down}

def second_block(x, mix_norm_g, ffn_norm_g, final_norm_g, fox_w_in, fox_b_f, fox_w_out,
              s5_w_in, s5_a_re, s5_a_im, s5_log_dt, s5_b_re, s5_b_im, s5_c_re, s5_c_im,
              s5_d, s5_w_glu, pool_w, pool_b, pool_scale, ffn_w_gate_up, ffn_w_down):
    for i in range(DEPTH_2):
        h = rms_norm_2(x, mix_norm_g[i])
        kind, j = i % N_MIXERS, i // N_MIXERS
        if kind == 0:
            mix = forgetting_attention(h, fox_w_in[j], fox_b_f[j], fox_w_out[j])
        elif kind == 1:
            mix = s5_layer(h, s5_w_in[j], s5_a_re[j], s5_a_im[j], s5_log_dt[j], s5_b_re[j], s5_b_im[j],
                           s5_c_re[j], s5_c_im[j], s5_d[j], s5_w_glu[j])
        else:
            mix = multiscale_pool(h, pool_w[j], pool_b[j], pool_scale[j])
        x = x + mix.astype(x.dtype)
        x = x + swiglu(rms_norm_2(x, ffn_norm_g[i]), ffn_w_gate_up[i], ffn_w_down[i]).astype(x.dtype)
    return rms_norm_2(x, final_norm_g)


def setup_inputs(seed=0):
    out = dict(first_inputs(seed))
    for name, value in second_inputs(seed + 1).items():
        if name != "x":
            out[name + "_2"] = value
    return out


def reference(
    x, c, ctx, c_ctx, w_ada, b_ada, g_mix, g_ffn, w_in, conv_w, conv_b, conv_ln_g, conv_ln_b,
    ssd_conv_w, ssd_conv_b, dt_bias, a_log, d_skip, ssd_norm_g, w_out, w_router_group,
    b_router_group, w_router_expert, b_router_expert, w_gate, w_up, w_down, g_final,
    mix_norm_g_2, ffn_norm_g_2, final_norm_g_2, fox_w_in_2, fox_b_f_2, fox_w_out_2, s5_w_in_2,
    s5_a_re_2, s5_a_im_2, s5_log_dt_2, s5_b_re_2, s5_b_im_2, s5_c_re_2, s5_c_im_2, s5_d_2,
    s5_w_glu_2, pool_w_2, pool_b_2, pool_scale_2, ffn_w_gate_up_2, ffn_w_down_2,
):
    x = first_block(
        x, c, ctx, c_ctx, w_ada, b_ada, g_mix, g_ffn, w_in, conv_w, conv_b, conv_ln_g,
        conv_ln_b, ssd_conv_w, ssd_conv_b, dt_bias, a_log, d_skip, ssd_norm_g, w_out,
        w_router_group, b_router_group, w_router_expert, b_router_expert, w_gate, w_up, w_down,
        g_final,
    )
    return second_block(
        x, mix_norm_g_2, ffn_norm_g_2, final_norm_g_2, fox_w_in_2, fox_b_f_2, fox_w_out_2,
        s5_w_in_2, s5_a_re_2, s5_a_im_2, s5_log_dt_2, s5_b_re_2, s5_b_im_2, s5_c_re_2,
        s5_c_im_2, s5_d_2, s5_w_glu_2, pool_w_2, pool_b_2, pool_scale_2, ffn_w_gate_up_2,
        ffn_w_down_2,
    )


_drawn_inputs = setup_inputs


def setup_inputs(seed=0):
    import zlib

    import numpy as np

    out = dict(_drawn_inputs(seed))
    spreads = {}
    factors = {'g_mix': 3.019,
     'conv_ln_g': 5.606,
     'conv_ln_b': 5.427,
     'ssd_conv_b': 7.797,
     'd_skip': 64.0,
     'ssd_norm_g': 8.363,
     'b_router_group': 39.857,
     'b_router_expert': 27.828,
     's5_a_re_2': 64.0,
     's5_b_re_2': 2.92,
     's5_b_im_2': 2.849,
     's5_c_re_2': 2.9,
     's5_c_im_2': 2.858,
     'pool_b_2': 8.0,
     'g_ffn': 4.906,
     'conv_b': 2.727}
    for name, (base, spread) in spreads.items():
        noise = np.random.default_rng([zlib.crc32(name.encode()), seed]).standard_normal(out[name].shape)
        drawn = base * np.exp(spread * noise) if base else spread * noise
        out[name] = jnp.asarray(drawn.astype(out[name].dtype))
    for name, factor in factors.items():
        out[name] = (out[name] * factor).astype(out[name].dtype)
    return out
```

```python
import math
from contextlib import ExitStack

import numpy as np

import concourse.bass as bass
import concourse.mybir as mybir

ALU = mybir.AluOpType
ACT = mybir.ActivationFunctionType
AX = mybir.AxisListType
F32 = mybir.dt.float32
BF16 = mybir.dt.bfloat16
I32 = mybir.dt.int32

P = 128
D = 1024
KC = D // P
T = 256
TB = T // P
GRID_W = 64
ROWS = T // GRID_W
DEPTH = 2
TAPS = 31
HALF = TAPS // 2
STAPS = 5
HEADS = 8
HD = 64
EXPERTS = 16
FF = 256
FFN_SLICES = 11
FOX_HEADS = 16
S5_CH = 32
POOLS = 4
RING = 3
TILE = KC * 2 * FF + 2 * D
ADA_N = 768
BIG = 1.0e30

W_IN_ORDER = [[0, 4, 1, 5, 2, 6], [3, 7, 12, 13, 14, 15], [16, 17, 18, 19, 8, 9], [10, 11]]

VEC_SHAPES = (
    [("c2", (KC, 2))]
    + [(f"b_ada{l}", (48, 2)) for l in range(DEPTH)]
    + [(f"{n}{l}", (KC, 2)) for l in range(DEPTH) for n in ("g_mix", "g_ffn")]
    + [(f"conv_w{l}", (4, TAPS)) for l in range(DEPTH)]
    + [(f"{n}{l}", (4,)) for l in range(DEPTH) for n in ("conv_b", "ln_g", "ln_b", "d_skip", "ssd_g")]
    + [(f"sconv_w{l}", (8, STAPS)) for l in range(DEPTH)]
    + [(f"sconv_b{l}", (8,)) for l in range(DEPTH)]
    + [(f"{n}{l}", (16,)) for l in range(DEPTH) for n in ("dt_bias", "a_log", "fox_b")]
    + [(f"b_rt{l}", (20,)) for l in range(DEPTH)]
    + [(f"w_rt{l}", (KC, 20)) for l in range(DEPTH)]
    + [(f"{n}{l}", (KC, 16)) for l in range(DEPTH) for n in ("w_dt", "w_f")]
    + [(f"{n}{i}", (KC,)) for i in range(4) for n in ("mix_g", "ffn_g")]
    + [(n, (KC,)) for n in ("g_final", "fin_g", "s5_d", "pool_b", "pool_s")]
    + [(n, (S5_CH,)) for n in ("a_re", "a_im", "log_dt")]
)
VEC_AT = {}
_at = 0
for _n, _s in VEC_SHAPES:
    VEC_AT[_n] = (_at, _s)
    _at += int(np.prod(_s))
NVEC = _at

CONSTS = ([("ident", (P,)), ("fw4", (4, P)), ("bw4", (4, P)), ("mean1024", (P,)), ("mean512", (P,)),
           ("first4", (4,)), ("eps6", (1,)), ("eps5", (1,)), ("halfpi", (1,))])
CON_AT = {}
_at = 0
for _n, _s in CONSTS:
    CON_AT[_n] = (_at, _s)
    _at += int(np.prod(_s))
NCON = _at


def const_arrays():
    i = np.arange(P)
    up = (i[:, None] <= i[None, :]).astype(np.float32)
    lo = (i[:, None] >= i[None, :]).astype(np.float32)
    one = np.ones((P, P), np.float32)
    c = {
        "ident": np.eye(P, dtype=np.float32),
        "fw4": np.concatenate([up, up, one, one], 1),
        "bw4": np.concatenate([one, one, lo, lo], 1),
        "mean1024": one / D, "mean512": one / (D // 2),
        "first4": np.broadcast_to(np.arange(4, 0, -1, dtype=np.float32), (P, 4)),
        "eps6": np.full((P, 1), 1e-6, np.float32), "eps5": np.full((P, 1), 1e-5, np.float32),
        "halfpi": np.full((P, 1), math.pi / 2, np.float32),
    }
    con = np.concatenate([c[n].reshape(P, -1) for n, _ in CONSTS], 1).astype(np.float32)
    masks = np.concatenate([np.eye(P), (up - 1) * BIG, (lo - 1) * BIG, np.zeros((P, 512))], 1)
    counts = np.stack([1.0 / np.minimum(np.arange(1, T + 1), 2 << g) for g in range(POOLS)])
    pool = np.broadcast_to(counts.astype(np.float32)[None], (P, POOLS, T))
    return con, masks.astype(mybir.dt.np(BF16)), np.ascontiguousarray(pool)


def tile_plan():
    plan = []
    for l in range(DEPTH):
        plan += [(("ada", l), 8, 8 * l), (("win", l), 4, 0), (("wout", l), 2, 2 * l)]
        plan += [(("moe", l, s), EXPERTS, EXPERTS * l) for s in (range(2) if l == 0 else range(1))]
    for i in range(4):
        if i in (0, 3):
            plan += [(("foxin", i), 4, 4 * (i // 3)), (("foxout", i), 2, 2 * (i // 3))]
        elif i == 1:
            plan += [(("s5in", i), 2, 0), (("glu", i), 4, 0)]
        else:
            plan += [(("poolw", i), 1, 0)]
        plan += [(("ffn", i), FFN_SLICES, FFN_SLICES * i)]
    return plan


PLAN = tile_plan()
TILE_AT = {}
_at = 0
for _n, _k, _ in PLAN:
    TILE_AT[_n] = _at
    _at += _k


def program(nc, dram, out, known):
    ctx = ExitStack()
    seen, count, sems = {}, {}, {}

    def sem(name):
        if name not in sems:
            sems[name] = ctx.enter_context(nc.semaphore(name))
            count[name] = 0
        return sems[name]

    def done(name, key=None, by=1):
        s = sem(name)
        count[name] += by
        seen[name, key] = count[name]
        return s, by

    def at(name, key=None):
        return sem(name), known.get((name, key), 1)

    def loop_base(name, key, total):
        sem(name)
        seen[name, key] = count[name]
        count[name] += total
        return seen[name, key]

    def base(name, key):
        sem(name)
        return known.get((name, key), 0)

    with ctx:
        def sb(name, shape, dt=F32):
            return ctx.enter_context(nc.sbuf_tensor(name, [P] + list(shape), dt))

        ring = [sb(f"ring{i}", [TILE]) for i in range(RING)]
        vec = sb("vec", [NVEC])
        con = sb("con", [NCON])
        msk = sb("msk", [3 * P + 512], BF16)
        XT = sb("XT", [KC, 2 * T])
        HT = sb("HT", [KC, 2 * T])
        MIX = sb("MIX", [KC, 2 * T])
        wide = sb("wide", [4160])
        border = sb("border", [3176])
        zs_b = sb("zs_b", [4 * 2 * T])
        xtok = sb("xtok", [TB, 512])
        btok = sb("btok", [TB, 2, P])
        score = sb("score", [2, TB, T])
        h0 = sb("h0", [2, 2, T])
        sig = sb("sig", [2, 2 * T])
        rms = sb("rms", [2 * T])
        rstd = sb("rstd", [2 * T])
        mod = [sb(f"mod{l}", [48, 2]) for l in range(DEPTH)]
        gsc = [sb(f"gsc{l}", [2, KC, 2]) for l in range(DEPTH)]
        sc2 = sb("sc2", [KC, 2])
        arow = sb("arow", [4, ADA_N // 2])
        dts = sb("dts", [6, 4, 16])
        aneg = sb("aneg", [2, 16])
        nacum = sb("nacum", [TB, 16])
        wst = sb("wst", [2, TB, 16])
        rt = sb("rt", [4, 4, 20])
        rs1 = sb("rs1", [16, 4, 4])
        comb = sb("comb", [4, 16])
        s5p = sb("s5p", [20, S5_CH])

        ps = [ctx.enter_context(nc.psum_tensor(f"bank{b}", [P, 512], F32)) for b in range(8)]

        def v(name):
            o, s = VEC_AT[name]
            x = vec[:, o:o + int(np.prod(s))]
            return x if len(s) == 1 else x.rearrange("p (a b) -> p a b", a=s[0])

        def k(name):
            o, s = CON_AT[name]
            return con[:, o:o + int(np.prod(s))]

        identb, mask_f, mask_b, zeros = msk[:, 0:P], msk[:, P:2 * P], msk[:, 2 * P:3 * P], msk[:, 3 * P:]
        ident = k("ident")

        def view(buf, off, *shape):
            x = buf[:, off:off + int(np.prod(shape))]
            names = "abcd"[:len(shape)]
            if len(shape) == 1:
                return x
            return x.rearrange(f"p ({' '.join(names)}) -> p {' '.join(names)}",
                               **dict(zip(names[:-1], shape[:-1])))

        sq = view(wide, 0, KC, 2 * T)
        xbc = view(wide, 0, KC, 2, T + STAPS - 1)
        vrow = view(border, 0, 2, ROWS, GRID_W + 2 * HALF)
        vcol = view(border, 752, 2, ROWS + 6, GRID_W)
        vseq = view(border, 752 + 1280, 4, T + 2 * HALF)
        zs = view(zs_b, 0, 4, 2 * T)
        xw = view(border, 0, TB, 2, 512)
        dec_f0, dec_f1 = view(wide, 0, 2, T), view(wide, 512, 2, P)
        dec_b1, dec_b0 = view(wide, 768, 2, T), view(wide, 1280, 2, P)
        off_f, off_b = view(wide, 1536, 2, T), view(wide, 2048, 2, T)
        mix0, mix1 = view(wide, 2560, 2, T), view(wide, 3072, 2, T)
        part0, part1 = view(wide, 3584, 2, P), view(wide, 3840, 2, P)
        cw = view(wide, 0, EXPERTS, T)
        hid = view(border, 0, 2, T)
        gact = view(border, 512, 2, T)

        XT2 = XT[:, :, 0:T]
        HTf, MIXf = HT[:].rearrange("p a b -> p (a b)"), MIX[:].rearrange("p a b -> p (a b)")
        H2, Q2 = view(HTf, 0, KC, T), view(HTf, KC * T, KC, T)
        O2, K2 = view(MIXf, 0, KC, T), view(MIXf, KC * T, KC, T)
        vtok = view(zs_b, 0, TB, D)
        prob = view(wide, 0, 2, 384)
        probT = view(wide, 768, 2, 384)
        fx = view(wide, 1536, 6, TB, 16)
        stat = view(wide, 1536 + 192, 2, 4, 2)
        bT = view(MIXf, KC * T, 2, KC, P)
        cT = view(zs_b, 0, 2, S5_CH, S5_CH)
        bblk = view(border, 0, 2, S5_CH, S5_CH)
        pw = view(border, 2 * S5_CH * S5_CH, 8, 3, S5_CH)
        state = view(wide, 0, 2, 2, 2, P + T)
        hpad = [view(wide, i * 4 * (16 + T), 4, 16 + T) for i in range(2)]
        counts = view(border, 0, POOLS, T)

        block = ctx.enter_context(nc.Block())

        def tile_ready(t, eng, g=0):
            eng.wait_ge(sem(f"tile_loaded{t % RING}"), 16 * (t // RING + 1) + 16 * g)
            return ring[t % RING]

        @block.sync
        def _(sp):
            def load(t, src, width, g=0):
                if t + 1 > RING or not isinstance(g, int):
                    sp.wait_ge(sem("tile_free"), t - RING + 1 + RING * g)
                sp.dma_start(ring[t % RING][:, 0:width], src).then_inc(sem(f"tile_loaded{t % RING}"), 16)

            for name, n, first in PLAN:
                t0, src = TILE_AT[name], dram[name[0]]
                if name[0] == "win":
                    for j in range(3):
                        load(t0 + j, src[3 * name[1] + j], KC * 768)
                    load(t0 + 3, dram["win_z"][name[1]], KC * 256)
                    continue
                width = src.shape[2]
                turns = n // RING if n > 8 else 0
                if turns:
                    with sp.Fori(0, turns) as g:
                        for j in range(RING):
                            load(t0 + j, src[first + j + RING * g], width, g)
                for j in range(turns * RING, n):
                    load(t0 + j, src[first + j], width)
            sp.wait_ge(*at("x_ready", "end"))
            sp.dma_start(out.rearrange("p (a b) -> p a b", a=KC), H2).then_inc(sem("stored"), 16)
            sp.wait_ge(sem("stored"), 16)

        @block.gpsimd
        def _(pool):
            for l in range(DEPTH):
                if l > 0:
                    pool.wait_ge(*at("x_ready", ("moe", 0, 1)))
                nc.gpsimd.memset(border[:], 0.0).then_inc(*done("border_zero", l))
                pool.wait_ge(*at("normed", (("mix", l), KC - 1)))
                nc.gpsimd.memset(wide[:], 0.0).then_inc(*done("wide_zero", l))
            pool.wait_ge(*at("x_ready", ("ffn", 0)))
            pool.dma_start(bblk, dram["s5_b"]).then_inc(*done("s5_loaded", 0, 16))
            pool.dma_start(cT, dram["s5_c"]).then_inc(*done("s5_loaded", 1, 16))
            pool.wait_ge(*at("x_ready", ("ffn", 1)))
            pool.dma_start(counts, dram["pool_counts"]).then_inc(*done("counts_loaded", 0, 16))
            pool.wait_ge(*at("normed_plain", (("pool",), KC - 1)))
            nc.gpsimd.memset(wide[:], 0.0).then_inc(*done("wide_zero", "pool"))

        mm = nc.tensor.matmul

        @block.tensor
        def _(pe):
            def ada(l):
                t0 = TILE_AT["ada", l]
                pe.wait_ge(*at("c2_silu"))
                if l:
                    pe.wait_ge(*at("x_ready", ("moe", l - 1, 1)))
                n = ADA_N // 2

                def turn(j):
                    pe.wait_ge(*at("ada_row", (l, j)))
                    for c in range(3):
                        i = mm(ps[2][:, 6 * j + 2 * c:6 * j + 2 * c + 2], arow[0:2, j % 4, P * c:P * c + P],
                               ident[0:2, 0:2], start=True, stop=True)
                    i.then_inc(*done("ada_turned", (l, j)))

                for j in range(16):
                    w = tile_ready(t0 + j // 2, pe)[:].rearrange("p (a b) -> p a b", a=KC)
                    if j >= 2:
                        pe.wait_ge(*at("ada_row", (l, j - 2)))
                    for c in range(KC):
                        i = mm(ps[j % 2][0:2, 0:n], sc2[:, c, :], w[:, c, (j % 2) * n:(j % 2) * n + n],
                               start=c == 0, stop=c == KC - 1)
                    if j % 2:
                        i.then_inc(*done("tile_free"))
                        pe.drain().then_inc(*done("ada_prod", (l, j)))
                    else:
                        i.then_inc(*done("ada_prod", (l, j)))
                    if j:
                        turn(j - 1)
                turn(15)

            def mean_square(n, tok):
                for c in range(KC):
                    if c % 4 == 0:
                        pe.wait_ge(*at("squares", (n, c // 4)))
                    i = mm(ps[7][:, 0:tok.stop - tok.start], k("mean1024"), sq[:, c, tok],
                           start=c == 0, stop=c == KC - 1)
                i.then_inc(*done("mean_square", n))

            def project(name, groups, banks, ready, taken, frees):
                for j, (out_ap, pairs) in enumerate(groups):
                    if j >= len(banks):
                        pe.wait_ge(*taken(j - len(banks)))
                    t = frees(j)
                    w = tile_ready(t[0], pe)
                    for c, (lhs, rhs) in enumerate(pairs(w)):
                        if j == 0 and ready is not None:
                            pe.wait_ge(*ready(c))
                        i = mm(out_ap(ps[banks[j % len(banks)]]), lhs, rhs, start=c == 0, stop=c == KC - 1)
                    if t[1]:
                        i.then_inc(*done("tile_free"))
                        pe.drain().then_inc(*done("proj", (name, j)))
                    else:
                        i.then_inc(*done("proj", (name, j)))

            def win(l):
                t0, groups = TILE_AT["win", l], []
                flat = [(a, b) for a, tile in enumerate(W_IN_ORDER) for b in range(len(tile))]
                for a, b in flat:
                    ch, n = W_IN_ORDER[a][b], len(W_IN_ORDER[a]) * P
                    tok = slice(0, 2 * T) if l == 0 or 12 <= ch < 18 else slice(0, T)
                    groups.append((lambda bank, tok=tok: bank[:, tok],
                                   lambda w, b=b, n=n, tok=tok: [
                                       (w[:, c * n + b * P:c * n + b * P + P], HT[:, c, tok]) for c in range(KC)]))
                project(("win", l), groups, [0, 1, 2, 3, 4, 5], lambda c: at("normed", (("mix", l), c)),
                        lambda j: at(*win_taken(l, j)),
                        lambda j: (t0 + flat[j][0], flat[j][1] == len(W_IN_ORDER[flat[j][0]]) - 1))
                for b in range(4):
                    for c in range(KC):
                        i = mm(ps[6][:, 16 * b:16 * b + 16], HT[:, c, b * P:b * P + P], v(f"w_dt{l}")[:, c, :],
                               start=c == 0, stop=c == KC - 1)
                i.then_inc(*done("dt_raw", l))

            def ssd(l, s, full):
                o = s * T
                fw, bw = k("fw4"), k("bw4")
                up, one, lo = fw[:, 0:P], fw[:, 2 * P:3 * P], bw[:, 2 * P:3 * P]
                da = dts[:, 5, :, :]
                b0, b1 = 2 * s, 2 * s + 1
                for c in range(KC):
                    pe.wait_ge(*at("ssd_in", (l, c)))
                for b in range(TB):
                    for c in range(4):
                        i = nc.tensor.transpose(ps[6 + b][:, c * P:c * P + P],
                                                HT[:, c, o + b * P:o + b * P + P], ident)
                    i.then_inc(*done("x_tok", (l, s, b)))
                pe.wait_ge(*at("x_tok_sb", (l, s, 0)))
                for b in range(TB):
                    for g in range(2):
                        i = nc.tensor.transpose(ps[6][:, (2 * b + g) * P:(2 * b + g + 1) * P],
                                                HT[:, 4 + g, o + b * P:o + b * P + P], ident)
                i.then_inc(*done("b_tok", (l, s)))
                pe.wait_ge(*at("da", l))
                pe.wait_ge(*at("x_tok_sb", (l, s, 1)))
                ac = ps[7]
                mm(ac[:, 0:8], up, da[:, b0, 0:8], start=True, stop=True)
                mm(ac[:, 16:24], one, da[:, b0, 0:8], start=True, stop=False)
                mm(ac[:, 16:24], up, da[:, b1, 0:8], start=False, stop=True)
                mm(ac[:, 24:32], lo, da[:, b1, 8:16], start=True, stop=True)
                mm(ac[:, 8:16], lo, da[:, b0, 8:16], start=True, stop=False)
                mm(ac[:, 8:16], one, da[:, b1, 8:16], start=False, stop=True)
                mm(ac[:, 32:48], one, da[:, b0, :], start=True, stop=False)
                mm(ac[:, 32:48], one, da[:, b1, :], start=False, stop=True).then_inc(*done("acum", (l, s)))
                if full:
                    for g in range(2):
                        pe.wait_ge(*(at("b_tok_sb", (l, s)) if g == 0 else at("acum_sb", (l, s))))
                        for b in range(TB):
                            i = mm(ps[6 + g][:, b * T:b * T + T], HT[:, 4 + g, o + b * P:o + b * P + P],
                                   HT[:, 6 + g, o:o + T], start=True, stop=True)
                        i.then_inc(*done("scores", (l, s, g)))
                if s == 1:
                    pe.wait_ge(*at("xw", l))
                    pe.wait_ge(*at("b_tok_sb", (l, s)))
                    for g in range(2):
                        if full:
                            pe.wait_ge(*at("scores_sb", (l, s, g)))
                        for b in range(TB):
                            i = mm(ps[6 + g][:], btok[:, b, g, :], xw[:, b, :, g * T:g * T + T],
                                   start=b == 0, stop=b == TB - 1)
                        i.then_inc(*done("states", (l, g)))
                if not full:
                    return

                def decay(h):
                    f, b = ps[2 * (h % 2)], ps[2 * (h % 2) + 1]
                    if h >= 2:
                        pe.wait_ge(*at("decayed", (l, s, h - 2)))
                    mm(f[:], da[:, b0, h:h + 1].to_broadcast([P, P]), fw, start=True, stop=True, skip_group_check=True)
                    mm(f[:, 2 * P:], da[:, b1, h:h + 1].to_broadcast([P, P]), fw[:, 0:2 * P], start=False, stop=True, skip_group_check=True)
                    fm = f[:].rearrange("p (a m c) -> p a m c", a=2, m=2)[:, :, 1, :]
                    mm(fm, identb, mask_f.unsqueeze(1).to_broadcast([P, 2, P]), start=False, stop=True, skip_group_check=True)
                    mm(b[:], da[:, b1, 8 + h:9 + h].to_broadcast([P, P]), bw, start=True, stop=True, skip_group_check=True)
                    mm(b[:, 0:2 * P], da[:, b0, 8 + h:9 + h].to_broadcast([P, P]), bw[:, 2 * P:], start=False, stop=True, skip_group_check=True)
                    bm = b[:].rearrange("p (a m c) -> p a m c", a=2, m=2)[:, :, 0, :]
                    mm(bm, identb, mask_b.unsqueeze(1).to_broadcast([P, 2, P]), start=False, stop=True, skip_group_check=True)\
                        .then_inc(*done("decay", (l, s, h)))

                def outputs(h):
                    c, q = h // 2, (h % 2) * HD
                    if h % 2 == 0 and c >= 2:
                        pe.wait_ge(*at("y_taken", (l, s, c - 2)))
                    pe.wait_ge(*at("mix_sb", (l, s, h)))
                    y = ps[4 + c % 2][q:q + HD, 0:T]
                    mm(y, xtok[:, 0, h * HD:h * HD + HD], mix0[:, h % 2, :], start=True, stop=False)
                    i = mm(y, xtok[:, 1, h * HD:h * HD + HD], mix1[:, h % 2, :], start=False, stop=s == 1)
                    if s == 0:
                        g, w = h // 4, (h % 4) * HD
                        mm(y, h0[:, g, 0, w:w + HD], off_f[:, h % 2, :], start=False, stop=False)
                        i = mm(y, h0[:, g, 1, w:w + HD], off_b[:, h % 2, :], start=False, stop=True)
                    i.then_inc(*done("y", (l, s, h)))

                decay(0)
                for h in range(HEADS):
                    if h + 1 < HEADS:
                        decay(h + 1)
                    outputs(h)

            def mean4(name, src, bank, tok, ready):
                for c in range(4):
                    pe.wait_ge(*ready(c))
                    i = mm(ps[bank][:, 0:tok.stop - tok.start], k("mean512"), src(c), start=c == 0, stop=c == 3)
                i.then_inc(*done("mean4", name))

            def wout(l, tok):
                t0 = TILE_AT["wout", l]
                n = 4 * P
                groups = [(lambda bank: bank[:, 0:tok.stop], lambda w, j=j: [
                    (w[:, c * n + (j % 4) * P:c * n + (j % 4) * P + P], MIX[:, c, tok]) for c in range(KC)])
                    for j in range(KC)]
                project(("wout", l), groups, [0, 1, 2, 3],
                        lambda c: at("conv_out", (l, c)) if c < 4 else at("ssd_out", (l, c - 4)),
                        lambda j: at("res_dve", (("wout", l), j)), lambda j: (t0 + j // 4, j % 4 == 3))

            def router(l, blocks):
                for c in range(KC):
                    pe.wait_ge(*at("normed", (("ffn", l), c)))
                for b in range(blocks):
                    for c in range(KC):
                        i = mm(ps[6][:, 20 * b:20 * b + 20], HT[:, c, b * P:b * P + P], v(f"w_rt{l}")[:, c, :],
                               start=c == 0, stop=c == KC - 1)
                i.then_inc(*done("logits", l))

            def comb_rows(l, s):
                pe.wait_ge(*at("comb", l))
                for j in range(EXPERTS // 2):
                    if j >= 2:
                        pe.wait_ge(*at("cw_sb", (l, s, j - 2)))
                    for e in range(2):
                        for b in range(TB):
                            at_e = comb[:, 2 * s + b, 2 * j + e:2 * j + e + 1]
                            i = mm(ps[6 + j % 2][:, e * T + b * P:e * T + b * P + P],
                                   at_e.to_broadcast([P, P]), ident, start=True, stop=True)
                    i.then_inc(*done("cw", (l, s, j)))

            def swiglu(name, slices, src, ready):
                if name == ("moe", 0, 1):
                    pe.wait_ge(*at("x_ready", ("moe", 0, 0)))
                t0 = TILE_AT[name]
                gu0 = loop_base("gate_up", name, 2 * slices)
                hid0 = base("hidden", name)
                loop_base("tile_free", name, slices)
                for b in range(4):
                    mm(ps[b][:], zeros[:, 0:P], zeros, start=True, stop=True)
                for c in range(KC):
                    pe.wait_ge(*ready(c))

                def one_slice(j, g):
                    w = tile_ready(t0 + j, pe, g)
                    gu = w[:, 0:KC * 2 * FF].rearrange("p (a m n) -> p a m n", a=KC, m=4)
                    dn = w[:, KC * 2 * FF:].rearrange("p (a n) -> p a n", a=2)
                    for m in range(2):
                        for half in range(2):
                            for c in range(KC):
                                i = mm(ps[4 + m][:, half * T:half * T + T], gu[:, c, 2 * m + half, :],
                                       src(c), start=c == 0, stop=c == KC - 1)
                        i.then_inc(sem("gate_up"), 1)
                    for m in range(2):
                        pe.wait_ge(sem("hidden"), hid0 + 2 * j + m + 1 + 2 * RING * g)
                        for c in range(KC):
                            i = mm(ps[c // 2][:, (c % 2) * T:(c % 2) * T + T], dn[:, m, c * P:c * P + P],
                                   hid[:, m, :], start=False, stop=True, skip_group_check=True)
                    i.then_inc(sem("tile_free"), 1)

                turns = slices // RING
                with pe.Fori(0, turns) as g:
                    for j in range(RING):
                        one_slice(j, g)
                for j in range(turns * RING, slices):
                    one_slice(j, 0)

            def fox(i_layer):
                j_fox = i_layer // 3
                name = ("fox", i_layer)
                t0 = TILE_AT["foxin", i_layer]
                for c in range(KC):
                    pe.wait_ge(*at("normed_plain", (name, c)))
                for b in range(TB):
                    for c in range(KC):
                        i = mm(ps[7][:, 256 + 16 * b:272 + 16 * b], H2[:, c, b * P:b * P + P], v(f"w_f{j_fox}")[:, c, :],
                               start=c == 0, stop=c == KC - 1)
                i.then_inc(*done("f_raw", i_layer))
                groups = []
                for b in range(TB):
                    for lo_c, n in ((0, 384), (384, 384)):
                        groups.append((lambda bank, n=n: bank[:, 0:n], lambda w, b=b, lo_c=lo_c, n=n: [
                            (H2[:, c, b * P:b * P + P], w[:, c * 768 + lo_c:c * 768 + lo_c + n]) for c in range(KC)]))
                for b in range(TB):
                    groups.append((lambda bank: bank[:, 0:T], lambda w, b=b: [
                        (H2[:, c, b * P:b * P + P], w[:, c * 768:c * 768 + T]) for c in range(KC)]))
                for col in [2, 3, 4, 5] + list(range(6)) * 2:
                    groups.append((lambda bank: bank[:, 0:T], lambda w, col=col: [
                        (w[:, c * 768 + col * P:c * 768 + col * P + P], H2[:, c, :]) for c in range(KC)]))
                tile_of = [0] * 4 + [1] * 6 + [2] * 6 + [3] * 6
                project(name, groups, [0, 1, 2, 3], None, lambda j: at("fox_sb", (i_layer, j)),
                        lambda j: (t0 + tile_of[j], j in (3, 9, 15, 21)))

                fw = k("fw4")
                spl = fx[:, 5, :, :]

                def logits(h):
                    c, q = h // 2, (h % 2) * HD
                    L = ps[h % 2]
                    if h >= 2:
                        pe.wait_ge(*at("prob", (i_layer, h - 2)))
                    else:
                        pe.wait_ge(*at("fox_sb", (i_layer, 21)))
                        pe.wait_ge(*at("f_sp", i_layer))
                    mm(L[:, 0:384], spl[:, 0, h:h + 1].to_broadcast([P, P]), fw[:, 0:384], start=True, stop=True, skip_group_check=True)
                    mm(L[:, 256:384], spl[:, 1, h:h + 1].to_broadcast([P, P]), fw[:, 0:P], start=False, stop=True, skip_group_check=True)
                    diag = L[:].rearrange("p (a m c) -> p a m c", a=2, m=2)[:, :, 0, :]
                    mm(diag, identb, mask_b.unsqueeze(1).to_broadcast([P, 2, P]), start=False, stop=True, skip_group_check=True)
                    mm(L[:, 0:P], Q2[q:q + HD, c, 0:P], K2[q:q + HD, c, 0:P], start=False, stop=True, skip_group_check=True)
                    mm(L[:, P:384], Q2[q:q + HD, c, P:T], K2[q:q + HD, c, 0:T], start=False, stop=True, skip_group_check=True)\
                        .then_inc(*done("att", (i_layer, h)))

                def turn(h):
                    pe.wait_ge(*at("prob_n", (i_layer, h)))
                    if h >= 2:
                        pe.wait_ge(*at("probT", (i_layer, h - 2)))
                    for blk, to in ((0, 0), (1, 1), (2, 2)):
                        i = nc.tensor.transpose(ps[2 + h % 2][:, to * P:to * P + P],
                                                prob[:, h % 2, blk * P:blk * P + P], ident)
                    i.then_inc(*done("att_turned", (i_layer, h)))

                def values(h):
                    c, q = h // 2, (h % 2) * HD
                    pe.wait_ge(*at("probT", (i_layer, h)))
                    if h % 2 == 0 and c >= 2:
                        pe.wait_ge(*at("o_sb", (i_layer, c - 2)))
                    o = ps[4 + c % 2]
                    mm(o[q:q + HD, 0:T], vtok[:, 0, h * HD:h * HD + HD], probT[:, h % 2, 0:T], start=True, stop=False)
                    mm(o[q:q + HD, P:T], vtok[:, 1, h * HD:h * HD + HD], probT[:, h % 2, T:384],
                       start=False, stop=True).then_inc(*done("o", (i_layer, h)))

                for h in range(FOX_HEADS + 2):
                    if h < FOX_HEADS:
                        logits(h)
                    if 1 <= h <= FOX_HEADS:
                        turn(h - 1)
                    if h >= 2:
                        values(h - 2)
                t1 = TILE_AT["foxout", i_layer]
                n = 4 * P
                groups = [(lambda bank: bank[:, 0:T], lambda w, j=j: [
                    (w[:, c * n + (j % 4) * P:c * n + (j % 4) * P + P], O2[:, c, :]) for c in range(KC)])
                    for j in range(KC)]
                project(("foxout", i_layer), groups, [0, 1, 2, 3], lambda c: at("o_sb", (i_layer, c)),
                        lambda j: at("res_dve", (("foxout", i_layer), j)), lambda j: (t1 + j // 4, j % 4 == 3))

            def s5():
                t0, n = TILE_AT["s5in", 1], 4 * P
                groups = [(lambda bank: bank[:, 0:T], lambda w, j=j: [
                    (w[:, c * n + (j % 4) * P:c * n + (j % 4) * P + P], H2[:, c, :]) for c in range(KC)])
                    for j in range(KC)]
                project(("s5in",), groups, [0, 1, 2, 3], lambda c: at("normed_plain", (("s5",), c)),
                        lambda j: at("u_sb", j), lambda j: (t0 + j // 4, j % 4 == 3))
                pe.wait_ge(*at("b_bar"))
                for c in range(KC):
                    for r in range(2):
                        if c >= 2:
                            pe.wait_ge(*at("bT", c - 2))
                        i = nc.tensor.transpose(
                            ps[4 + c % 2][:, r * P:r * P + P],
                            bblk[:, r, 4 * c:4 * c + 4, :].rearrange("p a b -> p (a b)"), ident)
                    i.then_inc(*done("b_turned", c))
                pe.wait_ge(*at("bT", KC - 1))
                pe.wait_ge(*at("u_sb", KC - 1))
                pe.wait_ge(*at("c_neg"))

                def inputs(j):
                    q, c = 32 * (j % 4), j // 4
                    if j >= 2:
                        pe.wait_ge(*at("bu_sb", j - 2))
                    for r in range(2):
                        i = mm(ps[j % 2][:, r * T:r * T + T], bT[q:q + 32, r, c, :], Q2[q:q + 32, c, :],
                               start=True, stop=True, tile_position=(q, 0))
                    i.then_inc(*done("bu", j))

                def outputs(j):
                    q, c = 32 * (j % 4), j // 4
                    if j % 4 == 0 and c >= 2:
                        pe.wait_ge(*at("s5_y", c - 2))
                    pe.wait_ge(*at("states_done", j))
                    y = ps[2 + c % 2][q:q + 32, 0:T]
                    st = state[:, j % 2, 0, :, :]
                    mm(y, cT[:, 0, j, :], st[:, 0, P:], start=True, stop=False, tile_position=(0, q))
                    mm(y, cT[:, 1, j, :], st[:, 1, P:], start=False, stop=True, tile_position=(0, q))\
                        .then_inc(*done("s5_out", j))

                inputs(0)
                for j in range(S5_CH):
                    if j + 1 < S5_CH:
                        inputs(j + 1)
                    outputs(j)
                t1 = TILE_AT["glu", 1]
                groups = [(lambda bank: bank[:, 0:T], lambda w, j=j: [
                    (w[:, c * n + (j % 4) * P:c * n + (j % 4) * P + P], O2[:, c, :]) for c in range(KC)])
                    for j in range(2 * KC)]
                project(("glu",), groups, [4, 5, 6, 7], lambda c: at("gelu", c),
                        lambda j: at("glu_val", j // 2) if j % 2 == 0 else at("glu_gate", j // 2),
                        lambda j: (t1 + j // 4, j % 4 == 3))

            def pooling():
                t0 = TILE_AT["poolw", 2]
                w = tile_ready(t0, pe)[:, 0:8 * T].rearrange("p (g a n) -> p g a n", g=POOLS, a=2)
                for j in range(KC):
                    g, m = j // 2, j % 2
                    if j >= 4:
                        pe.wait_ge(*at("res_dve", (("pool",), j - 4)))
                    if m == 0:
                        pe.wait_ge(*at("pooled", g))
                    for a in range(2):
                        i = mm(ps[j % 4][:, 0:T], w[:, g, a, m * P:m * P + P], O2[:, 2 * g + a, :],
                               start=a == 0, stop=a == 1)
                    if j == KC - 1:
                        i.then_inc(*done("tile_free"))
                        pe.drain().then_inc(*done("proj", (("pool",), j)))
                    else:
                        i.then_inc(*done("proj", (("pool",), j)))

            pe.wait_ge(sem("small_loaded"), 16 * 4)
            for l in range(DEPTH):
                both, last = slice(0, 2 * T), l == DEPTH - 1
                tok = slice(0, T) if last else both
                ada(l)
                mean_square(("mix", l), both)
                win(l)
                ssd(l, 1, not last)
                pe.wait_ge(*at("h0", (l, 1)))
                ssd(l, 0, True)
                mean4(("ln_mean", l), lambda c: MIX[:, c, tok], 6, tok, lambda c: at("conv_y", l))
                mean4(("ln_var", l), lambda c: sq[:, c, tok], 7, tok, lambda c: at("ln_sq", l))
                mean4(("ssd_ms", l), lambda c: sq[:, 4 + c, tok], 6, tok, lambda c: at("ssd_sq", l))
                wout(l, tok)
                mean_square(("ffn", l), tok)
                router(l, 2 if last else 4)
                for s in range(1 if last else 2):
                    comb_rows(l, s)
                    swiglu(("moe", l, s), EXPERTS, lambda c, s=s: HT[:, c, s * T:s * T + T],
                           lambda c: at("cw_sb", (l, s, EXPERTS // 2 - 1)))
            mean_square(("final1",), slice(0, T))
            for i_layer in range(4):
                name = (("fox", 0), ("s5",), ("pool",), ("fox", 3))[i_layer]
                mean_square(name, slice(0, T))
                if i_layer in (0, 3):
                    fox(i_layer)
                elif i_layer == 1:
                    s5()
                else:
                    pooling()
                mean_square(("ffn2", i_layer), slice(0, T))
                swiglu(("ffn", i_layer), FFN_SLICES, lambda c: H2[:, c, :],
                       lambda c: at("normed_plain", (("ffn2", i_layer), c)))
            mean_square(("final2",), slice(0, T))

        act_fn = nc.scalar.activation

        @block.scalar
        def _(act):
            act.dma_start(vec[:], dram["vec"]).then_inc(sem("small_loaded"), 16)
            act.dma_start(con[:], dram["con"]).then_inc(sem("small_loaded"), 16)
            act.dma_start(msk[:], dram["msk"]).then_inc(sem("small_loaded"), 16)
            act.dma_start(XT[:], dram["xt"]).then_inc(sem("small_loaded"), 16)
            act.wait_ge(sem("small_loaded"), 16 * 4)
            act_fn(sc2[:], v("c2"), ACT.Silu).then_inc(*done("c2_silu"))

            def ada(l):
                for j in range(16):
                    act.wait_ge(*at("ada_prod", (l, j)))
                    if j >= 4:
                        act.wait_ge(*at("ada_turned", (l, j - 4)))
                    nc.scalar.copy(arow[0:2, j % 4, :], ps[j % 2][0:2, 0:ADA_N // 2]).then_inc(*done("ada_row", (l, j)))

            def squares(n, tok, ready):
                if ready is not None:
                    act.wait_ge(*ready)
                for half in range(2):
                    act_fn(sq[:, 4 * half:4 * half + 4, tok], XT[:, 4 * half:4 * half + 4, tok], ACT.Square)\
                        .then_inc(*done("squares", (n, half)))
                act.wait_ge(*at("mean_square", n))
                act_fn(rms[:, 0:tok.stop], ps[7][:, 0:tok.stop], ACT.Sqrt, bias=k("eps6")).then_inc(*done("root", n))

            def shift(l, which, n, streams):
                for c in range(KC):
                    for s in range(streams):
                        act.wait_ge(*at("scaled", (n, c, s)))
                        h = HT[:, c, s * T:s * T + T]
                        i = act_fn(h, h, ACT.Identity, bias=mod[l][:, 24 * which + c, s:s + 1])
                    i.then_inc(*done("normed", (n, c)))

            def win(l):
                flat = [ch for tile in W_IN_ORDER for ch in tile]
                streams = 1 if l == DEPTH - 1 else 2
                for j, ch in enumerate(flat):
                    if ch < 4:
                        continue
                    act.wait_ge(*at("proj", (("win", l), j)))
                    if ch < 8:
                        if ch >= 6:
                            act.wait_ge(*at("gated", (l, ch - 6)))
                        act_fn(sig[:, ch % 2, 0:streams * T], ps[j % 6][:, 0:streams * T], ACT.Sigmoid)\
                            .then_inc(*done("win_act", (l, j)))
                    elif ch < 12:
                        act_fn(zs[:, ch - 8, 0:streams * T], ps[j % 6][:, 0:streams * T], ACT.Silu)\
                            .then_inc(*done("win_act", (l, j)))
                    else:
                        if ch == 12:
                            act.wait_ge(*at("wide_zero", l))
                        n = 2 if ch < 18 else streams
                        act_fn(xbc[:, ch - 12, 0:n, 2:2 + T],
                               ps[j % 6][:, 0:n * T].rearrange("p (a b) -> p a b", a=n), ACT.Copy)\
                            .then_inc(*done("win_act", (l, j)))

            def softplus_log(name, key, e, src):
                act.wait_ge(*at(name + "_abs", key))
                act_fn(e, src, ACT.Exp, scale=-1.0)
                act.drain()
                act_fn(e, e, ACT.Ln, bias=1.0).then_inc(*done(name + "_log", key))

            def ssd_in(l):
                streams = 1 if l == DEPTH - 1 else 2
                for c in range(8):
                    act.wait_ge(*at("sconv", l))
                    n = 2 * T if c < 6 else streams * T
                    act_fn(HT[:, c, 0:n], HT[:, c, 0:n], ACT.Silu).then_inc(*done("ssd_in", (l, c)))

            def ssd(l, s, full):
                for b in range(TB):
                    act.wait_ge(*at("x_tok", (l, s, b)))
                    nc.scalar.copy(xtok[:, b, :], ps[6 + b][:]).then_inc(*done("x_tok_sb", (l, s, b)))
                act.wait_ge(*at("b_tok", (l, s)))
                nc.scalar.copy(btok[:].rearrange("p a b c -> p (a b c)"), ps[6][:]).then_inc(*done("b_tok_sb", (l, s)))
                if full:
                    for g in range(2):
                        act.wait_ge(*at("scores", (l, s, g)))
                        nc.scalar.copy(score[:, g, :, :].rearrange("p a b -> p (a b)"), ps[6 + g][:])\
                            .then_inc(*done("scores_sb", (l, s, g)))
                if s == 1:
                    act.wait_ge(*at("to_end", l))
                    act_fn(wst[:, 1, :, :], wst[:, 0, :, :], ACT.Exp).then_inc(*done("end_decay", l))
                    for g in range(2):
                        act.wait_ge(*at("states", (l, g)))
                        nc.scalar.copy(h0[:, g, :, :].rearrange("p a b -> p (a b)"), ps[6 + g][:]).then_inc(*done("h0", (l, g)))
                if not full:
                    return
                act.wait_ge(*at("acum_sb", (l, s)))
                for h in range(HEADS):
                    p = h % 2
                    f, b = ps[2 * p], ps[2 * p + 1]
                    act.wait_ge(*at("decay", (l, s, h)))
                    if h >= 2:
                        act.wait_ge(*at("mix_sb", (l, s, h - 2)))
                    act_fn(dec_f0[:, p, :], f[:, P:3 * P], ACT.Exp, bias=nacum[:, 0, h:h + 1])
                    act_fn(dec_f1[:, p, :], f[:, 3 * P:], ACT.Exp, bias=nacum[:, 1, h:h + 1])
                    act_fn(dec_b1[:, p, :], b[:, P:3 * P], ACT.Exp, bias=nacum[:, 1, 8 + h:9 + h])
                    i = act_fn(dec_b0[:, p, :], b[:, 0:P], ACT.Exp, bias=nacum[:, 0, 8 + h:9 + h])
                    if s == 0:
                        act_fn(off_f[:, p, :].rearrange("p (a c) -> p a c", a=2),
                               f[:].rearrange("p (a m c) -> p a m c", a=2, m=2)[:, :, 0, :], ACT.Exp)
                        i = act_fn(off_b[:, p, :].rearrange("p (a c) -> p a c", a=2),
                                   b[:].rearrange("p (a m c) -> p a m c", a=2, m=2)[:, :, 1, :], ACT.Exp)
                    i.then_inc(*done("decayed", (l, s, h)))

            def mixer_norms(l, tok):
                act.wait_ge(*at("centred", l))
                act_fn(sq[:, 0:4, tok], MIX[:, 0:4, tok], ACT.Square).then_inc(*done("ln_sq", l))
                act.wait_ge(*at("y_done", l))
                act_fn(sq[:, 4:8, tok], MIX[:, 4:8, tok], ACT.Square).then_inc(*done("ssd_sq", l))
                act.wait_ge(*at("mean4", ("ln_var", l)))
                act_fn(rms[:, tok], ps[7][:, tok], ACT.Sqrt, bias=k("eps5")).then_inc(*done("ln_root", l))
                act.wait_ge(*at("mean4", ("ssd_ms", l)))
                act.wait_ge(*at("ln_rstd", l))
                act_fn(rms[:, tok], ps[6][:, tok], ACT.Sqrt, bias=k("eps6")).then_inc(*done("ssd_root", l))
                for c in range(4):
                    act.wait_ge(*at("ln_scaled", l))
                    act_fn(MIX[:, c, tok], MIX[:, c, tok], ACT.Silu, bias=v(f"ln_b{l}")[:, c:c + 1],
                           scale=v(f"ln_g{l}")[:, c:c + 1]).then_inc(*done("conv_out", (l, c)))

            def router(l):
                act.wait_ge(*at("rt_shift", l))
                act_fn(rt[:, 2, :, 0:4], rt[:, 1, :, 0:4], ACT.Exp)
                act_fn(rt[:, 2, :, 4:8], rt[:, 1, :, 4:8], ACT.Exp).then_inc(*done("rt_exp", l))

            def comb_rows(l, s):
                for j in range(EXPERTS // 2):
                    act.wait_ge(*at("cw", (l, s, j)))
                    nc.scalar.copy(cw[:, 2 * j:2 * j + 2, :].rearrange("p a b -> p (a b)"), ps[6 + j % 2][:])\
                        .then_inc(*done("cw_sb", (l, s, j)))

            def swiglu(name, slices):
                gu0 = base("gate_up", name)
                loop_base("gate_act", name, 2 * slices)

                def one_slice(j, g):
                    for m in range(2):
                        act.wait_ge(sem("gate_up"), gu0 + 2 * j + m + 1 + 2 * RING * g)
                        act_fn(gact[:, m, :], ps[4 + m][:, 0:T], ACT.Silu).then_inc(sem("gate_act"), 1)

                turns = slices // RING
                with act.Fori(0, turns) as g:
                    for j in range(RING):
                        one_slice(j, g)
                for j in range(turns * RING, slices):
                    one_slice(j, 0)

            def fox(i_layer):
                softplus_log("f", i_layer, fx[:, 3, :, :], fx[:, 1, :, :])
                for j in range(22):
                    act.wait_ge(*at("proj", (("fox", i_layer), j)))
                    bank = ps[j % 4]
                    if j < 4:
                        i = nc.scalar.copy(vtok[:, j // 2, 384 * (j % 2):384 * (j % 2) + 384], bank[:, 0:384])
                    elif j < 6:
                        i = nc.scalar.copy(vtok[:, j - 4, 768:1024], bank[:, 0:T])
                    elif j < 14:
                        i = nc.scalar.mul(Q2[:, j - 6, :], bank[:, 0:T], HD ** -0.5)
                    else:
                        i = nc.scalar.copy(K2[:, j - 14, :], bank[:, 0:T])
                    i.then_inc(*done("fox_sb", (i_layer, j)))
                for h in range(FOX_HEADS + 2):
                    p = h % 2
                    if h < FOX_HEADS:
                        act.wait_ge(*at("att_max", (i_layer, h)))
                        if h >= 2:
                            act.wait_ge(*at("att_turned", (i_layer, h - 2)))
                        L = ps[p]
                        act_fn(prob[:, p, 0:P], L[:, 0:P], ACT.Exp, bias=stat[:, p, 0, 0:1], accum_out=stat[:, p, 1, 0:1])
                        act_fn(prob[:, p, P:384], L[:, P:384], ACT.Exp, bias=stat[:, p, 0, 1:2],
                               accum_out=stat[:, p, 1, 1:2]).then_inc(*done("prob", (i_layer, h)))
                    if 1 <= h <= FOX_HEADS:
                        q = (h - 1) % 2
                        act.wait_ge(*at("att_turned", (i_layer, h - 1)))
                        if h >= 3:
                            act.wait_ge(*at("o", (i_layer, h - 3)))
                        nc.scalar.copy(probT[:, q, :], ps[2 + q][:, 0:384]).then_inc(*done("probT", (i_layer, h - 1)))
                    if h >= 2 and h % 2 == 1:
                        c = (h - 2) // 2
                        act.wait_ge(*at("o", (i_layer, h - 2)))
                        nc.scalar.copy(O2[:, c, :], ps[4 + c % 2][:, 0:T]).then_inc(*done("o_sb", (i_layer, c)))

            def s5():
                act_fn(s5p[:, 0, :], v("log_dt"), ACT.Exp).then_inc(*done("s5_dt"))
                act.wait_ge(*at("s5_ang"))
                act_fn(s5p[:, 3, :], s5p[:, 1, :], ACT.Exp)
                act_fn(s5p[:, 6, :], s5p[:, 4, :], ACT.Sin)
                act_fn(s5p[:, 7, :], s5p[:, 5, :], ACT.Sin).then_inc(*done("s5_trig"))
                for j in range(KC):
                    act.wait_ge(*at("proj", (("s5in",), j)))
                    nc.scalar.copy(Q2[:, j, :], ps[j % 4][:, 0:T]).then_inc(*done("u_sb", j))
                for c in range(KC):
                    act.wait_ge(*at("b_turned", c))
                    nc.scalar.copy(bT[:, :, c, :], ps[4 + c % 2][:, 0:2 * P].rearrange("p (a b) -> p a b", a=2))\
                        .then_inc(*done("bT", c))
                for j in range(S5_CH):
                    act.wait_ge(*at("bu", j))
                    if j >= 2:
                        act.wait_ge(*at("s5_out", j - 2))
                    nc.scalar.copy(state[:, j % 2, 0, :, P:], ps[j % 2][:].rearrange("p (a b) -> p a b", a=2))\
                        .then_inc(*done("bu_sb", j))
                for c in range(KC):
                    act.wait_ge(*at("s5_y", c))
                    act_fn(O2[:, c, :], O2[:, c, :], ACT.Gelu_apprx_tanh).then_inc(*done("gelu", c))
                for j in range(KC):
                    act.wait_ge(*at("proj", (("glu",), 2 * j + 1)))
                    if j >= 2:
                        act.wait_ge(*at("res_dve", (("glu",), j - 2)))
                    act_fn(sig[:, j % 2, 0:T], ps[4 + (2 * j + 1) % 4][:, 0:T], ACT.Sigmoid).then_inc(*done("glu_gate", j))

            for l in range(DEPTH):
                last = l == DEPTH - 1
                tok = slice(0, T) if last else slice(0, 2 * T)
                act_fn(aneg[:, 0, :], v(f"a_log{l}"), ACT.Exp).then_inc(*done("a_exp", l))
                ada(l)
                squares(("mix", l), slice(0, 2 * T), at("x_ready", ("moe", l - 1, 1)) if l else None)
                shift(l, 0, ("mix", l), 2)
                win(l)
                softplus_log("dt", l, dts[:, 3, :, :], dts[:, 1, :, :])
                ssd_in(l)
                ssd(l, 1, not last)
                ssd(l, 0, True)
                mixer_norms(l, tok)
                squares(("ffn", l), tok, at("res_dve", (("wout", l), KC - 1)))
                shift(l, 1, ("ffn", l), 1 if last else 2)
                router(l)
                for s in range(1 if last else 2):
                    comb_rows(l, s)
                    swiglu(("moe", l, s), EXPERTS)
            squares(("final1",), slice(0, T), at("x_ready", ("moe", 1, 0)))
            for i_layer in range(4):
                name = (("fox", 0), ("s5",), ("pool",), ("fox", 3))[i_layer]
                squares(name, slice(0, T), at("x_ready", ("ffn", i_layer - 1) if i_layer else "first"))
                if i_layer in (0, 3):
                    fox(i_layer)
                elif i_layer == 1:
                    s5()
                last_res = (("foxout", 0), ("glu",), ("pool",), ("foxout", 3))[i_layer]
                squares(("ffn2", i_layer), slice(0, T), at("res_dve", (last_res, KC - 1)))
                swiglu(("ffn", i_layer), FFN_SLICES)
            squares(("final2",), slice(0, T), at("x_ready", ("ffn", 3)))

        stt, tt, ts = nc.vector.scalar_tensor_tensor, nc.vector.tensor_tensor, nc.vector.tensor_scalar
        tss = nc.vector.tensor_single_scalar

        @block.vector
        def _(dve):
            dve.wait_ge(sem("small_loaded"), 16 * 4)

            def ada(l):
                dve.wait_ge(*at("ada_turned", (l, 15)))
                tt(mod[l][:], ps[2][:, 0:96].rearrange("p (a b) -> p a b", a=48), v(f"b_ada{l}"), ALU.add)
                dve.drain()
                for which, g in ((0, "g_mix"), (1, "g_ffn")):
                    stt(gsc[l][:, which, :, :], mod[l][:, 24 * which + 8:24 * which + 16, :], 1.0, v(f"{g}{l}"),
                        ALU.add, ALU.mult)
                dve.drain()

            def scale(n, streams, gain, plain=None):
                dve.wait_ge(*at("root", n))
                nc.vector.reciprocal(rstd[:, 0:streams * T], rms[:, 0:streams * T])
                dve.drain()
                for c in range(KC):
                    for s in range(streams):
                        dst = plain[:, c, :] if plain is not None else HT[:, c, s * T:s * T + T]
                        stt(dst, XT[:, c, s * T:s * T + T], gain(c, s), rstd[:, s * T:s * T + T], ALU.mult, ALU.mult)\
                            .then_inc(*done("normed_plain", (n, c)) if plain is not None else done("scaled", (n, c, s)))

            def gate(l):
                flat = [ch for tile in W_IN_ORDER for ch in tile]
                dve.wait_ge(*at("border_zero", l))
                for c in range(4):
                    ju, jg = flat.index(c), flat.index(4 + c)
                    dve.wait_ge(*at("proj", (("win", l), ju)))
                    dve.wait_ge(*at("win_act", (l, jg)))
                    bank = ps[ju % 6]
                    if c < 2:
                        dst = vrow[:, c, :, HALF:HALF + GRID_W]
                    else:
                        dst = vcol[:, c - 2, 3:3 + ROWS, :]
                    i = tt(dst, bank[:, 0:T].rearrange("p (a b) -> p a b", a=ROWS),
                           sig[:, c % 2, 0:T].rearrange("p (a b) -> p a b", a=ROWS), ALU.mult)
                    if l < DEPTH - 1:
                        i = tt(vseq[:, c, HALF:HALF + T], bank[:, T:2 * T], sig[:, c % 2, T:2 * T], ALU.mult)
                    i.then_inc(*done("gated", (l, c)))
                dve.drain()

            def conformer(l):
                w, b = v(f"conv_w{l}"), v(f"conv_b{l}")

                def grid(c):
                    return MIX[:, c, 0:T].rearrange("p (a b) -> p a b", a=ROWS)

                first = HALF - (ROWS - 1)
                for c in range(4):
                    src = vrow[:, c, :, 0:GRID_W] if c < 2 else vcol[:, c - 2, 0:ROWS, :]
                    tap = 0 if c < 2 else first
                    ts(grid(c), src, w[:, c, tap:tap + 1], b[:, c:c + 1], ALU.mult, ALU.add)
                    if l < DEPTH - 1:
                        ts(MIX[:, c, T:2 * T], vseq[:, c, 0:T], w[:, c, 0:1], b[:, c:c + 1], ALU.mult, ALU.add)
                dve.drain()
                with dve.Fori(1, TAPS) as tap:
                    for c in range(2):
                        stt(grid(c), vrow[:, c, :, bass.ds(tap, GRID_W)], w[:, c, bass.ds(tap, 1)], grid(c), ALU.mult, ALU.add)
                    if l < DEPTH - 1:
                        for c in range(4):
                            y = MIX[:, c, T:2 * T]
                            stt(y, vseq[:, c, bass.ds(tap, T)], w[:, c, bass.ds(tap, 1)], y, ALU.mult, ALU.add)
                    dve.drain()
                for r in range(1, 2 * ROWS - 1):
                    for c in range(2, 4):
                        i = stt(grid(c), vcol[:, c - 2, r:r + ROWS, :], w[:, c, first + r:first + r + 1], grid(c), ALU.mult, ALU.add)
                    if r < 2 * ROWS - 2:
                        dve.drain()
                i.then_inc(*done("conv_y", l))

            def sconv(l):
                w, b = v(f"sconv_w{l}"), v(f"sconv_b{l}")
                flat = [ch for tile in W_IN_ORDER for ch in tile]
                dve.wait_ge(*at("win_act", (l, flat.index(19))))
                dve.wait_ge(*at("dt_raw", l))
                streams = 1 if l == DEPTH - 1 else 2
                for tap in range(STAPS):
                    for c in range(8):
                        n = 2 if c < 6 else streams
                        y = HT[:, c, 0:n * T].rearrange("p (a b) -> p a b", a=n)
                        src = xbc[:, c, 0:n, tap:tap + T]
                        if tap == 0:
                            i = ts(y, src, w[:, c, 0:1], b[:, c:c + 1], ALU.mult, ALU.add)
                        else:
                            i = stt(y, src, w[:, c, tap:tap + 1], y, ALU.mult, ALU.add)
                    if tap == STAPS - 1:
                        i.then_inc(*done("sconv", l))
                    else:
                        dve.drain()

            def softplus(name, key, raw, bias, x, ab, mx, lp, res, sign):
                tt(x, raw, bias, ALU.add)
                dve.drain()
                tss(lp, x, -1.0, ALU.mult)
                ts(mx, x, sign, 0.0, ALU.mult, ALU.max)
                dve.drain()
                tt(ab, x, lp, ALU.max).then_inc(*done(name + "_abs", key))
                dve.wait_ge(*at(name + "_log", key))
                tt(res, mx, lp, ALU.add)
                dve.drain()

            def steps(l):
                dve.wait_ge(*at("dt_raw", l))
                raw = ps[6][:, 0:64].rearrange("p (a b) -> p a b", a=4)
                bias = v(f"dt_bias{l}").unsqueeze(1).to_broadcast([P, 4, 16])
                softplus("dt", l, raw, bias, dts[:, 0, :, :], dts[:, 1, :, :], dts[:, 2, :, :], dts[:, 3, :, :],
                         dts[:, 4, :, :], 1.0)
                dve.wait_ge(*at("a_exp", l))
                tss(aneg[:, 1, :], aneg[:, 0, :], -1.0, ALU.mult)
                dve.drain()
                tt(dts[:, 5, :, :], dts[:, 4, :, :], aneg[:, 1, :].unsqueeze(1).to_broadcast([P, 4, 16]), ALU.mult)\
                    .then_inc(*done("da", l))

            def ssd(l, s, full):
                o = s * T
                dt = dts[:, 4, :, :]
                dve.wait_ge(*at("acum", (l, s)))
                if s == 1:
                    tss(nacum[:], ps[7][:, 0:32].rearrange("p (a b) -> p a b", a=2), -1.0, ALU.mult)
                    dve.drain()
                    tt(wst[:, 0, :, :], nacum[:], ps[7][:, 32:48].unsqueeze(1).to_broadcast([P, 2, 16]), ALU.add)\
                        .then_inc(*done("to_end", l))
                    dve.drain()
                    dve.drain().then_inc(*done("acum_sb", (l, s)))
                    dve.wait_ge(*at("end_decay", l))
                    tt(wst[:, 0, :, :], wst[:, 1, :, :], dt[:, 2:4, :], ALU.mult)
                    dve.wait_ge(*at("x_tok_sb", (l, s, 1)))
                    dve.drain()
                    for b in range(TB):
                        for d in range(2):
                            i = tt(xw[:, b, d, :].rearrange("p (h c) -> p h c", h=HEADS),
                                   xtok[:, b, :].rearrange("p (h c) -> p h c", h=HEADS),
                                   wst[:, 0, b, 8 * d:8 * d + 8].unsqueeze(2).to_broadcast([P, HEADS, HD]), ALU.mult)
                    i.then_inc(*done("xw", l))
                else:
                    tss(nacum[:], ps[7][:, 0:32].rearrange("p (a b) -> p a b", a=2), -1.0, ALU.mult)\
                        .then_inc(*done("acum_sb", (l, s)))
                if not full:
                    return
                b0, b1 = 2 * s, 2 * s + 1

                def take(c):
                    dve.wait_ge(*at("y", (l, s, 2 * c + 1)))
                    y = MIX[:, 4 + c, o:o + T]
                    stt(y, HT[:, c, o:o + T], v(f"d_skip{l}")[:, c:c + 1], ps[4 + c % 2][:, 0:T], ALU.mult, ALU.add)\
                        .then_inc(*done("y_taken", (l, s, c)))
                    dve.drain()
                    return tt(y, y, zs[:, c, o:o + T], ALU.mult)

                dve.wait_ge(*at("scores_sb", (l, s, 1)))
                for h in range(HEADS):
                    p, g = h % 2, h // 4
                    dve.wait_ge(*at("decayed", (l, s, h)))
                    if h >= 2:
                        dve.wait_ge(*at("y", (l, s, h - 2)))
                    stt(mix0[:, p, :], dec_f0[:, p, :], dt[:, b0, h:h + 1], score[:, g, 0, :], ALU.mult, ALU.mult)
                    stt(part0[:, p, :], dec_b0[:, p, :], dt[:, b0, 8 + h:9 + h], score[:, g, 0, 0:P], ALU.mult, ALU.mult)
                    stt(mix1[:, p, :], dec_b1[:, p, :], dt[:, b1, 8 + h:9 + h], score[:, g, 1, :], ALU.mult, ALU.mult)
                    stt(part1[:, p, :], dec_f1[:, p, :], dt[:, b1, h:h + 1], score[:, g, 1, P:T], ALU.mult, ALU.mult)
                    if s == 0:
                        tt(off_f[:, p, :], off_f[:, p, :], HT[:, 6 + g, o:o + T], ALU.mult)
                        tt(off_b[:, p, :], off_b[:, p, :], HT[:, 6 + g, o:o + T], ALU.mult)
                    dve.drain()
                    tt(mix0[:, p, 0:P], mix0[:, p, 0:P], part0[:, p, :], ALU.add)
                    tt(mix1[:, p, P:T], mix1[:, p, P:T], part1[:, p, :], ALU.add).then_inc(*done("mix_sb", (l, s, h)))
                    if h >= 3 and h % 2:
                        take((h - 3) // 2)
                take(3).then_inc(*done("y_stream", (l, s)))

            def mixer_norms(l, tok):
                n = tok.stop
                dve.drain()
                dve.drain().then_inc(*done("y_done", l))
                y = MIX[:, 0:4, tok]
                dve.wait_ge(*at("mean4", ("ln_mean", l)))
                tt(y, y, ps[6][:, 0:n].unsqueeze(1).to_broadcast([P, 4, n]), ALU.subtract).then_inc(*done("centred", l))
                dve.wait_ge(*at("ln_root", l))
                nc.vector.reciprocal(rstd[:, 0:n], rms[:, 0:n]).then_inc(*done("ln_rstd", l))
                dve.drain()
                tt(y, y, rstd[:, 0:n].unsqueeze(1).to_broadcast([P, 4, n]), ALU.mult).then_inc(*done("ln_scaled", l))
                dve.wait_ge(*at("ssd_root", l))
                dve.drain()
                nc.vector.reciprocal(rstd[:, 0:n], rms[:, 0:n])
                dve.drain()
                for c in range(4):
                    y = MIX[:, 4 + c, tok]
                    stt(y, y, v(f"ssd_g{l}")[:, c:c + 1], rstd[:, 0:n], ALU.mult, ALU.mult).then_inc(*done("ssd_out", (l, c)))

            def residual(name, taken, gates=None, streams=1):
                for j in range(KC):
                    dve.wait_ge(*at("proj", (name, j)))
                    for s in range(streams):
                        x = XT[:, j, s * T:s * T + T]
                        p = ps[taken[j % len(taken)]][:, s * T:s * T + T]
                        i = tt(x, p, x, ALU.add) if gates is None else stt(x, p, gates(j, s), x, ALU.mult, ALU.add)
                    i.then_inc(*done("res_dve", (name, j)))

            def first_max(hot, score_, x, mx, n):
                tt(hot, x, mx.to_broadcast([P, n, 4]), ALU.is_equal)
                dve.drain()
                tt(score_, hot, k("first4").unsqueeze(1).to_broadcast([P, n, 4]), ALU.mult)
                dve.drain()
                nc.vector.tensor_reduce(mx, score_, AX.X, ALU.max)
                dve.drain()
                tt(hot, score_, mx.to_broadcast([P, n, 4]), ALU.is_equal)
                dve.drain()

            def router(l, n):
                dve.wait_ge(*at("logits", l))
                lg = rt[:, 0, 0:n, :]
                tt(lg, ps[6][:, 0:20 * n].rearrange("p (a b) -> p a b", a=n),
                   v(f"b_rt{l}").unsqueeze(1).to_broadcast([P, n, 20]), ALU.add)
                dve.drain()
                a = lambda i: rs1[:, i, 0:n, :]
                one = lambda i: rs1[:, 12 + i // 4, 0:n, i % 4:i % 4 + 1]
                mx, gs, e2, wsum, w1, w2, m2 = (one(i) for i in range(7))
                nc.vector.tensor_reduce(mx, lg[:, :, 0:4], AX.X, ALU.max)
                dve.drain()
                tt(rt[:, 1, 0:n, 0:4], lg[:, :, 0:4], mx.to_broadcast([P, n, 4]), ALU.subtract)
                first_max(a(0), a(1), lg[:, :, 0:4], mx, n)
                tt(a(2), lg[:, :, 4:8], a(0)[:, :, 0:1].to_broadcast([P, n, 4]), ALU.mult)
                dve.drain()
                for g in range(1, 4):
                    tt(a(3), lg[:, :, 4 + 4 * g:8 + 4 * g], a(0)[:, :, g:g + 1].to_broadcast([P, n, 4]), ALU.mult)
                    dve.drain()
                    tt(a(2), a(2), a(3), ALU.add)
                    dve.drain()
                nc.vector.tensor_reduce(mx, a(2), AX.X, ALU.max)
                dve.drain()
                tt(rt[:, 1, 0:n, 4:8], a(2), mx.to_broadcast([P, n, 4]), ALU.subtract).then_inc(*done("rt_shift", l))
                first_max(a(4), a(5), a(2), mx, n)
                stt(a(6), a(4), -BIG, a(2), ALU.mult, ALU.add)
                dve.drain()
                nc.vector.tensor_reduce(m2, a(6), AX.X, ALU.max)
                dve.drain()
                first_max(a(7), a(8), a(6), m2, n)
                dve.wait_ge(*at("rt_exp", l))
                nc.vector.tensor_reduce(gs, rt[:, 2, 0:n, 0:4], AX.X, ALU.add)
                tt(a(9), rt[:, 2, 0:n, 4:8], a(4), ALU.mult)
                tt(a(10), rt[:, 2, 0:n, 4:8], a(7), ALU.mult)
                dve.drain()
                nc.vector.tensor_reduce(w1, a(9), AX.X, ALU.add)
                nc.vector.tensor_reduce(w2, a(10), AX.X, ALU.add)
                dve.drain()
                tt(wsum, w1, w2, ALU.add)
                dve.drain()
                tt(wsum, wsum, gs, ALU.mult)
                dve.drain()
                nc.vector.reciprocal(wsum, wsum)
                tt(a(9), a(9), a(10), ALU.add)
                dve.drain()
                tt(a(9), a(9), wsum.to_broadcast([P, n, 4]), ALU.mult)
                dve.drain()
                for g in range(4):
                    i = tt(comb[:, 0:n, 4 * g:4 * g + 4], a(9), a(0)[:, :, g:g + 1].to_broadcast([P, n, 4]), ALU.mult)
                i.then_inc(*done("comb", l))

            def swiglu(name, slices, weighted):
                act0 = base("gate_act", name)
                loop_base("hidden", name, 2 * slices)

                def one_slice(j, g, e):
                    for m in range(2):
                        dve.wait_ge(sem("gate_act"), act0 + 2 * j + m + 1 + 2 * RING * g)
                        h = hid[:, m, :]
                        i = tt(h, gact[:, m, :], ps[4 + m][:, T:2 * T], ALU.mult)
                        if weighted:
                            dve.drain()
                            i = tt(h, h, cw[:, e, :], ALU.mult)
                        i.then_inc(sem("hidden"), 1)

                turns = slices // RING
                with dve.Fori(0, turns) as g:
                    for j in range(RING):
                        one_slice(j, g, j + RING * g)
                for j in range(turns * RING, slices):
                    one_slice(j, 0, j)

            def add_sum(name, gates=None, stream=0):
                slices = EXPERTS if gates is not None else FFN_SLICES
                dve.wait_ge(sem("tile_free"), TILE_AT[name] + slices)
                for c in range(KC):
                    x = XT[:, c, stream * T:stream * T + T]
                    p = ps[c // 2][:, (c % 2) * T:(c % 2) * T + T]
                    i = tt(x, p, x, ALU.add) if gates is None else stt(x, p, gates(c), x, ALU.mult, ALU.add)
                i.then_inc(*done("x_ready", name))
                dve.drain()

            def fox(i_layer):
                j_fox = i_layer // 3
                dve.wait_ge(*at("f_raw", i_layer))
                softplus("f", i_layer, ps[7][:, 256:288].rearrange("p (a b) -> p a b", a=TB),
                         v(f"fox_b{j_fox}").unsqueeze(1).to_broadcast([P, TB, 16]),
                         fx[:, 0, :, :], fx[:, 1, :, :], fx[:, 2, :, :], fx[:, 3, :, :], fx[:, 5, :, :], -1.0)
                dve.drain().then_inc(*done("f_sp", i_layer))
                for h in range(FOX_HEADS):
                    p = h % 2
                    L = ps[p]
                    dve.wait_ge(*at("att", (i_layer, h)))
                    nc.vector.reduce_max(stat[:, p, 0, 0:1], L[:, 0:P], AX.X, negate=True)
                    nc.vector.reduce_max(stat[:, p, 0, 1:2], L[:, P:384], AX.X, negate=True)\
                        .then_inc(*done("att_max", (i_layer, h)))
                    dve.wait_ge(*at("prob", (i_layer, h)))
                    nc.vector.reciprocal(stat[:, p, 2, :], stat[:, p, 1, :])
                    dve.drain()
                    tss(prob[:, p, 0:P], prob[:, p, 0:P], stat[:, p, 2, 0:1], ALU.mult)
                    tss(prob[:, p, P:384], prob[:, p, P:384], stat[:, p, 2, 1:2], ALU.mult)\
                        .then_inc(*done("prob_n", (i_layer, h)))
                residual(("foxout", i_layer), [0, 1, 2, 3])

            def s5():
                dve.wait_ge(*at("s5_dt"))
                pv = lambda i: s5p[:, i, :]
                tt(pv(1), v("a_re"), pv(0), ALU.mult)
                tt(pv(2), v("a_im"), pv(0), ALU.mult)
                dve.drain()
                tss(pv(9), pv(2), math.pi / 2, ALU.add)
                dve.drain()
                for src, dst in ((2, 4), (9, 5)):
                    tss(pv(8), pv(src), 1 / (2 * math.pi), ALU.mult)
                    dve.drain()
                    nc.vector.tensor_copy(pv(10).bitcast(I32), pv(8))
                    dve.drain()
                    nc.vector.tensor_copy(pv(8), pv(10).bitcast(I32))
                    dve.drain()
                    stt(pv(dst), pv(8), -6.28125, pv(src), ALU.mult, ALU.add)
                    dve.drain()
                    stt(pv(dst), pv(8), -(2 * math.pi - 6.28125), pv(dst), ALU.mult, ALU.add)
                    dve.drain()
                    ts(pv(dst), pv(dst), 3.1415925, -3.1415925, ALU.min, ALU.max)
                    dve.drain()
                dve.drain().then_inc(*done("s5_ang"))
                dve.wait_ge(*at("s5_trig"))
                tt(pw[:, 0, 0, :], pv(3), pv(7), ALU.mult)
                tt(pw[:, 0, 1, :], pv(3), pv(6), ALU.mult)
                dve.drain()
                tss(pv(11), pw[:, 0, 0, :], -1.0, ALU.add)
                tt(pv(12), v("a_re"), v("a_re"), ALU.mult)
                tt(pv(13), v("a_im"), v("a_im"), ALU.mult)
                dve.drain()
                tt(pv(12), pv(12), pv(13), ALU.add)
                dve.drain()
                nc.vector.reciprocal(pv(12), pv(12))
                tt(pv(13), pv(11), v("a_re"), ALU.mult)
                tt(pv(14), pw[:, 0, 1, :], v("a_im"), ALU.mult)
                tt(pv(15), pw[:, 0, 1, :], v("a_re"), ALU.mult)
                tt(pv(16), pv(11), v("a_im"), ALU.mult)
                dve.drain()
                tt(pv(13), pv(13), pv(14), ALU.add)
                tt(pv(15), pv(15), pv(16), ALU.subtract)
                dve.drain()
                tt(pv(13), pv(13), pv(12), ALU.mult)
                tt(pv(15), pv(15), pv(12), ALU.mult)
                for n in range(8):
                    if n:
                        tt(pv(17), pw[:, n - 1, 0, :], pw[:, n - 1, 0, :], ALU.mult)
                        tt(pv(18), pw[:, n - 1, 1, :], pw[:, n - 1, 1, :], ALU.mult)
                        stt(pw[:, n, 1, :], pw[:, n - 1, 0, :], 2.0, pw[:, n - 1, 1, :], ALU.mult, ALU.mult)
                        dve.drain()
                        tt(pw[:, n, 0, :], pv(17), pv(18), ALU.subtract)
                    tss(pw[:, n, 2, :], pw[:, n, 1, :], -1.0, ALU.mult)
                    dve.drain()
                dve.wait_ge(sem("s5_loaded"), 32)
                dve.wait_ge(*at("normed_plain", (("s5",), KC - 1)))
                br, bi = bblk[:, 0, :, :], bblk[:, 1, :, :]
                f_re = pv(13).unsqueeze(2).to_broadcast([P, S5_CH, S5_CH])
                f_im = pv(15).unsqueeze(2).to_broadcast([P, S5_CH, S5_CH])
                tmp = [view(wide, i * 1024, S5_CH, S5_CH) for i in range(4)]
                tt(tmp[0], br, f_re, ALU.mult)
                tt(tmp[1], bi, f_im, ALU.mult)
                tt(tmp[2], br, f_im, ALU.mult)
                tt(tmp[3], bi, f_re, ALU.mult)
                dve.drain()
                tt(br, tmp[0], tmp[1], ALU.subtract)
                tt(bi, tmp[2], tmp[3], ALU.add).then_inc(*done("b_bar"))
                dve.drain()
                nc.vector.memset(wide[:], 0.0)
                tss(cT[:, 1, :, :], cT[:, 1, :, :], -1.0, ALU.mult).then_inc(*done("c_neg"))
                dve.drain()
                for j in range(S5_CH):
                    dve.wait_ge(*at("bu_sb", j))
                    for n in range(8):
                        d = 1 << n
                        a, b = state[:, j % 2, n % 2, :, :], state[:, j % 2, 1 - n % 2, :, :]
                        re, im, nim = (pw[:, n, i, j:j + 1] for i in range(3))
                        stt(b[:, 0, P:], a[:, 0, P - d:P - d + T], re, a[:, 0, P:], ALU.mult, ALU.add)
                        stt(b[:, 1, P:], a[:, 1, P - d:P - d + T], re, a[:, 1, P:], ALU.mult, ALU.add)
                        dve.drain()
                        stt(b[:, 0, P:], a[:, 1, P - d:P - d + T], nim, b[:, 0, P:], ALU.mult, ALU.add)
                        i = stt(b[:, 1, P:], a[:, 0, P - d:P - d + T], im, b[:, 1, P:], ALU.mult, ALU.add)
                        if n < 7:
                            dve.drain()
                    i.then_inc(*done("states_done", j))
                    if j % 4 == 3:
                        c = j // 4
                        dve.wait_ge(*at("s5_out", j))
                        stt(O2[:, c, :], Q2[:, c, :], v("s5_d")[:, c:c + 1], ps[2 + c % 2][:, 0:T], ALU.mult, ALU.add)\
                            .then_inc(*done("s5_y", c))
                for j in range(KC):
                    dve.wait_ge(*at("proj", (("glu",), 2 * j)))
                    dve.wait_ge(*at("glu_gate", j))
                    g = sig[:, j % 2, 0:T]
                    tt(g, g, ps[4 + (2 * j) % 4][:, 0:T], ALU.mult).then_inc(*done("glu_val", j))
                    dve.drain()
                    tt(XT2[:, j, :], XT2[:, j, :], g, ALU.add).then_inc(*done("res_dve", (("glu",), j)))

            def pooling():
                dve.wait_ge(*at("wide_zero", "pool"))
                dve.wait_ge(sem("counts_loaded"), 16)
                dve.drain()

                for half in range(2):
                    a, b = hpad
                    c0 = 4 * half
                    nc.vector.tensor_copy(a[:, :, 16:], H2[:, c0:c0 + 4, :])
                    dve.drain()
                    n, lo_c = 0, 0
                    for step in range(2 * half + 2):
                        d = 1 << step
                        if step == 2 * half + 1:
                            lo_c = 2
                        src, dst = (a, b) if n % 2 == 0 else (b, a)
                        tt(dst[:, lo_c:4, 16:], src[:, lo_c:4, 16:], src[:, lo_c:4, 16 - d:16 - d + T], ALU.add)
                        n += 1
                        dve.drain()
                        if step == 2 * half or step == 2 * half + 1:
                            g = step
                            res, r0 = dst, (0 if step == 2 * half else 2)
                            o = O2[:, 2 * g:2 * g + 2, :]
                            tt(o, res[:, r0:r0 + 2, 16:], counts[:, g, :].unsqueeze(1).to_broadcast([P, 2, T]), ALU.mult)
                            dve.drain()
                            tt(o, o, H2[:, 2 * g:2 * g + 2, :], ALU.subtract).then_inc(*done("pooled", g))
                for j in range(KC):
                    dve.wait_ge(*at("proj", (("pool",), j)))
                    t = sig[:, j % 2, 0:T]
                    ts(t, ps[j % 4][:, 0:T], v("pool_b")[:, j:j + 1], v("pool_s")[:, j:j + 1], ALU.add, ALU.mult)
                    dve.drain()
                    tt(XT2[:, j, :], XT2[:, j, :], t, ALU.add).then_inc(*done("res_dve", (("pool",), j)))

            for l in range(DEPTH):
                last = l == DEPTH - 1
                streams = 1 if last else 2
                tok = slice(0, streams * T)
                ada(l)
                scale(("mix", l), 2, lambda c, s: gsc[l][:, 0, c, s:s + 1])
                gate(l)
                conformer(l)
                sconv(l)
                steps(l)
                ssd(l, 1, not last)
                ssd(l, 0, True)
                mixer_norms(l, tok)
                residual(("wout", l), [0, 1, 2, 3], lambda j, s: mod[l][:, 16 + j, s:s + 1], streams)
                dve.drain()
                scale(("ffn", l), streams, lambda c, s: gsc[l][:, 1, c, s:s + 1])
                router(l, 2 * streams)
                for s in range(streams):
                    swiglu(("moe", l, s), EXPERTS, True)
                    add_sum(("moe", l, s), lambda c: mod[l][:, 40 + c, s:s + 1], s)
            dve.wait_ge(*at("root", ("final1",)))
            nc.vector.reciprocal(rstd[:, 0:T], rms[:, 0:T])
            dve.drain()
            for c in range(KC):
                i = stt(XT2[:, c, :], XT2[:, c, :], v("g_final")[:, c:c + 1], rstd[:, 0:T], ALU.mult, ALU.mult)
            i.then_inc(*done("x_ready", "first"))
            dve.drain()
            for i_layer in range(4):
                name = (("fox", 0), ("s5",), ("pool",), ("fox", 3))[i_layer]
                scale(name, 1, lambda c, s: v(f"mix_g{i_layer}")[:, c:c + 1], H2)
                if i_layer in (0, 3):
                    fox(i_layer)
                elif i_layer == 1:
                    s5()
                else:
                    pooling()
                dve.drain()
                scale(("ffn2", i_layer), 1, lambda c, s: v(f"ffn_g{i_layer}")[:, c:c + 1], H2)
                swiglu(("ffn", i_layer), FFN_SLICES, False)
                add_sum(("ffn", i_layer))
            scale(("final2",), 1, lambda c, s: v("fin_g")[:, c:c + 1], H2)
            dve.drain()
            dve.drain().then_inc(*done("x_ready", "end"))

    return seen


def win_taken(l, j):
    ch = [c for tile in W_IN_ORDER for c in tile][j]
    return ("gated", (l, ch)) if ch < 4 else ("win_act", (l, j))


def lay_out(a):
    def cols(w, idx=None):
        w = w if idx is None else w[:, idx]
        return w.reshape(KC, P, -1).transpose(1, 0, 2).reshape(P, -1)

    def chunks(ids):
        return np.concatenate([np.arange(P) + P * i for i in ids])

    def feat(x):
        return x.reshape(-1, P).T

    def rep(x):
        return np.broadcast_to(x.reshape(1, -1), (P, x.size))

    def expert(g, u, d):
        gu = np.stack([g[:, :P], u[:, :P], g[:, P:], u[:, P:]], 1).reshape(D, 4 * P)
        return np.concatenate([cols(gu), d.reshape(2, P, D).transpose(1, 0, 2).reshape(P, -1)], 1)

    d = {}
    d["ada"] = np.stack([cols(a["w_ada"][l][:, ADA_N * i:ADA_N * i + ADA_N]) for l in range(DEPTH) for i in range(8)])
    d["win"] = np.stack([cols(a["w_in"][l], chunks(W_IN_ORDER[i])) for l in range(DEPTH) for i in range(3)])
    d["win_z"] = np.stack([cols(a["w_in"][l], chunks(W_IN_ORDER[3])) for l in range(DEPTH)])
    halves = lambda w, n=2: [cols(w[:, 512 * i:512 * i + 512]) for i in range(n)]
    d["wout"] = np.stack([t for l in range(DEPTH) for t in halves(a["w_out"][l])])
    d["moe"] = np.stack([expert(a["w_gate"][l, e], a["w_up"][l, e], a["w_down"][l, e])
                         for l in range(DEPTH) for e in range(EXPERTS)])
    fin = lambda w: [cols(w, np.concatenate([np.arange(768) + 2048])),
                     cols(w, np.concatenate([np.arange(256) + 2816, np.arange(512)])),
                     cols(w, np.arange(768) + 512), cols(w, np.arange(768) + 1280)]
    d["foxin"] = np.stack([t for j in range(2) for t in fin(a["fox_w_in_2"][j])])
    d["foxout"] = np.stack([t for j in range(2) for t in halves(a["fox_w_out_2"][j])])
    d["s5in"] = np.stack(halves(a["s5_w_in_2"][0]))
    pairs = np.concatenate([chunks([j, KC + j]) for j in range(KC)])
    d["glu"] = np.stack(halves(a["s5_w_glu_2"][0][:, pairs], 4))
    d["poolw"] = a["pool_w_2"][0].reshape(POOLS, 2, P, 2 * P).transpose(2, 0, 1, 3).reshape(1, P, -1)
    f = FFN_SLICES * FF
    d["ffn"] = np.stack([expert(a["ffn_w_gate_up_2"][i][:, FF * j:FF * j + FF],
                                a["ffn_w_gate_up_2"][i][:, f + FF * j:f + FF * j + FF],
                                a["ffn_w_down_2"][i][FF * j:FF * j + FF]) for i in range(4) for j in range(FFN_SLICES)])

    def by_state(re, im):
        o = np.zeros((P, 2, S5_CH, 2, 16), np.float32)
        for r, m in enumerate((re, im)):
            x = m.reshape(S5_CH, 2, 64, 16)
            for g in range(2):
                o[64 * g:64 * g + 64, r, :, g, :] = x[:, g].transpose(1, 0, 2)
        return o.reshape(P, -1)

    d["s5_b"] = by_state(a["s5_b_re_2"][0], a["s5_b_im_2"][0])
    d["s5_c"] = by_state(a["s5_c_re_2"][0].transpose(0, 2, 1), a["s5_c_im_2"][0].transpose(0, 2, 1))

    vec = {"c2": np.stack([feat(a["c"][0]), feat(a["c_ctx"])], 2)}
    two = lambda x: np.stack([feat(x), feat(x)], 2)
    state = lambda x: x.reshape(S5_CH, P).T
    for l in range(DEPTH):
        vec[f"b_ada{l}"] = two(a["b_ada"][l])
        vec[f"g_mix{l}"], vec[f"g_ffn{l}"] = two(a["g_mix"][l]), two(a["g_ffn"][l])
        vec[f"conv_w{l}"] = a["conv_w"][l].T.reshape(4, P, TAPS).transpose(1, 0, 2)
        vec[f"conv_b{l}"], vec[f"ln_g{l}"] = feat(a["conv_b"][l]), feat(a["conv_ln_g"][l])
        vec[f"ln_b{l}"], vec[f"ssd_g{l}"] = feat(a["conv_ln_b"][l]), feat(a["ssd_norm_g"][l])
        vec[f"d_skip{l}"] = feat(np.repeat(a["d_skip"][l], HD))
        vec[f"sconv_w{l}"] = a["ssd_conv_w"][l].T.reshape(8, P, STAPS).transpose(1, 0, 2)
        vec[f"sconv_b{l}"] = feat(a["ssd_conv_b"][l])
        vec[f"dt_bias{l}"], vec[f"a_log{l}"] = rep(a["dt_bias"][l]), rep(a["a_log"][l])
        vec[f"fox_b{l}"] = rep(a["fox_b_f_2"][l])
        vec[f"b_rt{l}"] = rep(np.concatenate([a["b_router_group"][l], a["b_router_expert"][l]]))
        vec[f"w_rt{l}"] = cols(np.concatenate([a["w_router_group"][l], a["w_router_expert"][l]], 1))
        vec[f"w_dt{l}"] = cols(a["w_in"][l][:, 2560:])
        vec[f"w_f{l}"] = cols(a["fox_w_in_2"][l][:, 3 * D:])
    for i in range(4):
        vec[f"mix_g{i}"], vec[f"ffn_g{i}"] = feat(a["mix_norm_g_2"][i]), feat(a["ffn_norm_g_2"][i])
    vec["g_final"], vec["fin_g"], vec["s5_d"] = feat(a["g_final"]), feat(a["final_norm_g_2"]), feat(a["s5_d_2"][0])
    vec["pool_b"], vec["pool_s"] = feat(a["pool_b_2"][0]), feat(a["pool_scale_2"][0])
    vec["a_re"], vec["a_im"] = state(a["s5_a_re_2"][0]), state(a["s5_a_im_2"][0])
    vec["log_dt"] = state(np.repeat(a["s5_log_dt_2"][0], 64))
    d["vec"] = np.concatenate([vec[n].reshape(P, -1) for n, _ in VEC_SHAPES], 1)
    xt = np.concatenate([a["x"][0], a["ctx"][0]], 0)
    d["xt"] = xt.T.reshape(KC, P, 2 * T).transpose(1, 0, 2).reshape(P, -1)
    d["con"], d["msk"], pool = const_arrays()
    d["pool_counts"] = pool.reshape(P, -1)
    return {n: np.ascontiguousarray(x) for n, x in d.items()}


def shaped(dram):
    r = dict(dram)
    r["xt"] = dram["xt"].rearrange("p (a b) -> p a b", a=KC)
    for n in ("s5_b", "s5_c"):
        r[n] = dram[n].rearrange("p (a b c) -> p a b c", a=2, b=S5_CH)
    r["pool_counts"] = dram["pool_counts"].rearrange("p (a b) -> p a b", a=POOLS)
    return r


def declare(nc, arrays):
    dram = {n: nc.dram_tensor(f"in_{n}", x.shape, mybir.dt.from_np(x.dtype), kind="ExternalInput").ap()
            for n, x in arrays.items()}
    return shaped(dram), nc.dram_tensor("out_0", (P, KC * T), F32, kind="ExternalOutput").ap()


def kernel(**inputs):
    import concourse.bacc as _bacc
    from concourse.bass_utils import run_bass_kernel_spmd as _run

    arrays = lay_out({n: np.asarray(x) for n, x in inputs.items()})
    counting = _bacc.Bacc("TRN2", target_bir_lowering=False, num_devices=1)
    known = program(counting, *declare(counting, arrays), {})
    nc = _bacc.Bacc("TRN2", target_bir_lowering=False, num_devices=1)
    program(nc, *declare(nc, arrays), known)
    r = _run(nc, [{f"in_{n}": x for n, x in arrays.items()}], core_ids=[0])
    o = np.asarray(r.results[0]["out_0"]).reshape(P, KC, T)
    return o.transpose(2, 1, 0).reshape(1, T, D)
```

```python
import math
from contextlib import ExitStack

import numpy as np

import concourse.bass as bass
import concourse.mybir as mybir

ALU = mybir.AluOpType
ACT = mybir.ActivationFunctionType
AX = mybir.AxisListType
F32 = mybir.dt.float32
BF16 = mybir.dt.bfloat16
F32R = mybir.dt.float32r
I32 = mybir.dt.int32

P = 128
D = 1024
KC = D // P
T = 256
TB = T // P
GRID_W = 64
ROWS = T // GRID_W
DEPTH = 2
TAPS = 31
HALF = TAPS // 2
STAPS = 5
HEADS = 8
HD = 64
EXPERTS = 16
FF = P
EXPERT_FF = 256
SLICES = EXPERTS * EXPERT_FF // FF
FFN_SLICES = 2816 // FF
FOX_HEADS = 16
S5_CH = 32
S5_LEVELS = 8
BATCH = 4
POOLS = 4
RING = 4
HIGH = 2
TCOLS = 2 * P
TILE = KC * TCOLS
BIG = 1.0e30

W_IN_ORDER = [0, 4, 1, 5, 2, 6, 3, 7, 12, 13, 14, 15, 16, 17, 18, 19, 8, 9, 10, 11]

VEC_SHAPES = (
    [("c2", (KC, 2))]
    + [(f"b_ada{l}", (48, 2)) for l in range(DEPTH)]
    + [(f"{n}{l}", (KC, 2)) for l in range(DEPTH) for n in ("g_mix", "g_ffn")]
    + [(f"conv_w{l}", (4, TAPS)) for l in range(DEPTH)]
    + [(f"{n}{l}", (4,)) for l in range(DEPTH) for n in ("conv_b", "ln_g", "ln_b", "d_skip", "ssd_g")]
    + [(f"sconv_w{l}", (8, STAPS)) for l in range(DEPTH)]
    + [(f"sconv_b{l}", (8,)) for l in range(DEPTH)]
    + [(f"{n}{l}", (16,)) for l in range(DEPTH) for n in ("dt_bias", "a_log", "fox_b")]
    + [(f"b_rt{l}", (20,)) for l in range(DEPTH)]
    + [(f"w_rt{l}", (KC, 20)) for l in range(DEPTH)]
    + [(f"{n}{l}", (KC, 16)) for l in range(DEPTH) for n in ("w_dt", "w_f")]
    + [(f"{n}{i}", (KC,)) for i in range(4) for n in ("mix_g", "ffn_g")]
    + [(n, (KC,)) for n in ("g_final", "fin_g", "s5_d", "pool_b", "pool_s")]
    + [(n, (S5_CH,)) for n in ("a_re", "a_im", "log_dt")]
)
VEC_AT = {}
_at = 0
for _n, _s in VEC_SHAPES:
    VEC_AT[_n] = (_at, _s)
    _at += int(np.prod(_s))
NVEC = _at

CONSTS = ([("ident", (P,)), ("fw4", (4, P)), ("bw4", (4, P)), ("mean1024", (P,)), ("mean512", (P,)),
           ("first4", (4,)), ("eps6", (1,)), ("eps5", (1,)), ("halfpi", (1,))])
CON_AT = {}
_at = 0
for _n, _s in CONSTS:
    CON_AT[_n] = (_at, _s)
    _at += int(np.prod(_s))
NCON = _at


def const_arrays():
    i = np.arange(P)
    up = (i[:, None] <= i[None, :]).astype(np.float32)
    lo = (i[:, None] >= i[None, :]).astype(np.float32)
    one = np.ones((P, P), np.float32)
    c = {
        "ident": np.eye(P, dtype=np.float32),
        "fw4": np.concatenate([up, up, one, one], 1),
        "bw4": np.concatenate([one, one, lo, lo], 1),
        "mean1024": one / D, "mean512": one / (D // 2),
        "first4": np.broadcast_to(np.arange(4, 0, -1, dtype=np.float32), (P, 4)),
        "eps6": np.full((P, 1), 1e-6, np.float32), "eps5": np.full((P, 1), 1e-5, np.float32),
        "halfpi": np.full((P, 1), math.pi / 2, np.float32),
    }
    con = np.concatenate([c[n].reshape(P, -1) for n, _ in CONSTS], 1).astype(np.float32)
    masks = np.concatenate([np.eye(P), (up - 1) * BIG, (lo - 1) * BIG, np.zeros((P, 512))], 1)
    counts = np.stack([1.0 / np.minimum(np.arange(1, T + 1), 2 << g) for g in range(POOLS)])
    pool = np.broadcast_to(counts.astype(np.float32)[None], (P, POOLS, T))
    return con, masks.astype(mybir.dt.np(BF16)), np.ascontiguousarray(pool)


ADA_TILES = 6 * D // TCOLS
WIN_TILES = len(W_IN_ORDER) // 2
HALF_D = D // TCOLS
RAW = ("ada", "poolw")
WITH_DVE = ("moe", "ffn", "foxin", "foxout", "s5in", "glu")


def tile_plan():
    plan = [(("ada", 0), ADA_TILES, 0)]
    for l in range(DEPTH):
        plan += [(("win", l), WIN_TILES, WIN_TILES * l)]
        if l + 1 < DEPTH:
            plan += [(("ada", l + 1), ADA_TILES, ADA_TILES * (l + 1))]
        plan += [(("wout", l), HALF_D, HALF_D * l)]
        plan += [(("moe", l, s), SLICES, SLICES * l) for s in (range(2) if l == 0 else range(1))]
    for i in range(4):
        if i in (0, 3):
            plan += [(("foxin", i), 3 * HALF_D, 3 * HALF_D * (i // 3)), (("foxout", i), HALF_D, HALF_D * (i // 3))]
        elif i == 1:
            plan += [(("s5in", i), HALF_D, 0), (("glu", i), 2 * HALF_D, 0)]
        else:
            plan += [(("poolw", i), 1, 0)]
        plan += [(("ffn", i), FFN_SLICES, FFN_SLICES * i)]
    return plan


PLAN = tile_plan()
TILE_AT, SPLIT_AT, DOWN_AT = {}, {}, {}
SPLIT, SHARED, DOWNS = [], [], 0
_at = 0
for _n, _k, _ in PLAN:
    TILE_AT[_n], SPLIT_AT[_n] = _at, len(SPLIT)
    for _i in range(_k):
        if _n[0] not in RAW:
            SPLIT.append(_at + _i)
            SHARED.append((SHARED[-1] if SHARED else 0) + (_n[0] in WITH_DVE))
    if _n[0] in ("moe", "ffn"):
        DOWN_AT[_n] = DOWNS
        DOWNS += _k
    _at += _k


def shared(c):
    return SHARED[c] > (SHARED[c - 1] if c else 0)


def program(nc, dram, out, known):
    ctx = ExitStack()
    seen, count, sems = {}, {}, {}

    def sem(name):
        if name not in sems:
            sems[name] = ctx.enter_context(nc.semaphore(name))
            count[name] = 0
        return sems[name]

    def done(name, key=None, by=1):
        s = sem(name)
        count[name] += by
        seen[name, key] = count[name]
        return s, by

    def at(name, key=None):
        return sem(name), known.get((name, key), 1)

    def loop_base(name, key, total):
        sem(name)
        seen[name, key] = count[name]
        count[name] += total
        return seen[name, key]

    def base(name, key):
        sem(name)
        return known.get((name, key), 0)

    with ctx:
        def sb(name, shape, dt=F32):
            return ctx.enter_context(nc.sbuf_tensor(name, [P] + list(shape), dt))

        def shared_sb(name, shape):
            with nc.sbuf_tensor(name + "_halves", [P] + list(shape), F32) as halves:
                pass
            return sb(name, shape), halves

        ring, ring_r = zip(*(shared_sb(f"ring{i}", [TILE]) for i in range(RING)))
        high = [sb(f"high{i}", [TILE]) for i in range(HIGH)]
        dring, dring_r = zip(*(shared_sb(f"dring{i}", [D]) for i in range(RING)))
        dhigh = [sb(f"dhigh{i}", [D]) for i in range(HIGH)]
        vec = sb("vec", [NVEC])
        con = sb("con", [NCON])
        msk = sb("msk", [3 * P + 512], BF16)
        XT = sb("XT", [KC, 2 * T])
        HT, HT_r = shared_sb("HT", [KC, 2 * T])
        MIX, MIX_r = shared_sb("MIX", [KC, 2 * T])
        wide = sb("wide", [4160])
        border, border_r = shared_sb("border", [3176])
        zs_b = sb("zs_b", [4 * 2 * T])
        ssdb, ssdb_r = shared_sb("ssdb", [KC * 2 * T])
        sig = sb("sig", [2, 2 * T])
        rms = sb("rms", [2 * T])
        rstd = sb("rstd", [2 * T])
        mod = [sb(f"mod{l}", [48, 2]) for l in range(DEPTH)]
        gsc = [sb(f"gsc{l}", [2, KC, 2]) for l in range(DEPTH)]
        sc2 = sb("sc2", [KC, 2])
        arow = sb("arow", [4, TCOLS])
        dts = sb("dts", [6, 4, 16])
        aneg = sb("aneg", [2, 16])
        nacum = sb("nacum", [TB, 16])
        wst = sb("wst", [2, TB, 16])
        rt = sb("rt", [4, 4, 20])
        rs1 = sb("rs1", [16, 4, 4])
        comb = sb("comb", [4, 16])
        s5p = sb("s5p", [20, S5_CH])

        ps = [ctx.enter_context(nc.psum_tensor(f"bank{b}", [P, 512], F32)) for b in range(8)]

        def v(name):
            o, s = VEC_AT[name]
            x = vec[:, o:o + int(np.prod(s))]
            return x if len(s) == 1 else x.rearrange("p (a b) -> p a b", a=s[0])

        def k(name):
            o, s = CON_AT[name]
            return con[:, o:o + int(np.prod(s))]

        identb, mask_f, mask_b, zeros = msk[:, 0:P], msk[:, P:2 * P], msk[:, 2 * P:3 * P], msk[:, 3 * P:]
        ident = k("ident")

        def view(buf, off, *shape):
            x = buf[:, off:off + int(np.prod(shape))]
            names = "abcd"[:len(shape)]
            if len(shape) == 1:
                return x
            return x.rearrange(f"p ({' '.join(names)}) -> p {' '.join(names)}",
                               **dict(zip(names[:-1], shape[:-1])))

        sq = view(wide, 0, KC, 2 * T)
        xbc = view(wide, 0, KC, 2, T + STAPS - 1)
        vrow = view(border, 0, 2, ROWS, GRID_W + 2 * HALF)
        vcol = view(border, 752, 2, ROWS + 6, GRID_W)
        vseq = view(border, 752 + 1280, 4, T + 2 * HALF)
        zs = view(zs_b, 0, 4, 2 * T)
        xw = view(border, 0, TB, 2, 512)
        dec_f0, dec_f1 = view(wide, 0, 2, T), view(wide, 512, 2, P)
        dec_b1, dec_b0 = view(wide, 768, 2, T), view(wide, 1280, 2, P)
        off_f, off_b = view(wide, 1536, 2, T), view(wide, 2048, 2, T)
        mix0, mix1 = view(wide, 2560, 2, T), view(wide, 3072, 2, T)
        part0, part1 = view(wide, 3584, 2, P), view(wide, 3840, 2, P)
        cw = view(wide, 0, EXPERTS, T)
        hid = view(border_r, 0, 2, 2, T)
        gact = view(border, 1024, 2, T)
        hraw = view(border, 1536, T)
        xtok, btok = view(ssdb, 0, TB, 512), view(ssdb, 1024, TB, 2, P)
        score, h0 = view(ssdb, 1536, 2, TB, T), view(ssdb, 2560, 2, 2, T)
        SB3 = view(ssdb_r, 0, KC, 2 * T)
        r = lambda x: x.bitcast(F32R)

        XT2 = XT[:, :, 0:T]
        H2r, O2r = (x[:].rearrange("p a b -> p (a b)")[:, 0:KC * T].rearrange("p (a b) -> p a b", a=KC)
                    for x in (HT_r, MIX_r))
        HTf, MIXf = HT[:].rearrange("p a b -> p (a b)"), MIX[:].rearrange("p a b -> p (a b)")
        H2, Q2 = view(HTf, 0, KC, T), view(HTf, KC * T, KC, T)
        H2h = view(ssdb_r, 0, KC, T)
        O2, K2 = view(MIXf, 0, KC, T), view(MIXf, KC * T, KC, T)
        vtok = view(zs_b, 0, TB, D)
        prob = view(wide, 0, 2, 384)
        probT = view(wide, 768, 2, 384)
        fx = view(wide, 1536, 6, TB, 16)
        stat = view(wide, 1536 + 192, 2, 4, 2)
        bT = view(MIXf, KC * T, 2, KC, P)
        cT = view(zs_b, 0, 2, S5_CH, S5_CH)
        bblk = view(border, 0, 2, S5_CH, S5_CH)
        pw = view(arow[:].rearrange("p a b -> p (a b)"), 0, S5_LEVELS, 2, S5_CH)
        table = [XT[:, :, T:2 * T].rearrange("p (a b) t -> p a b t", a=2), view(ssdb, KC * T, 2, BATCH, T)]
        table_tmp = sig[:].rearrange("p a (b t) -> p a b t", b=BATCH)
        s5_a, s5_b, s5_z = (view(wide, i * 2 * T, 2, T) for i in range(3))
        s5_q = view(wide, 3 * 2 * T, 2, 2, 2, T)
        s5_dmat = view(dring[0], 0, KC, P)
        hpad = [view(wide, i * 4 * (16 + T), 4, 16 + T) for i in range(2)]
        counts = view(border, 0, POOLS, T)

        def proj_at(name, j):
            return at("proj", (name, j)) if j % 2 == 0 else (sem("tile_free"), TILE_AT[name] + j // 2 + 1)

        block = ctx.enter_context(nc.Block())

        def low_ready(c, g=0):
            if shared(c):
                nc.tensor.wait_ge(sem("low_dve"), SHARED[c] + RING * g)
            nc.tensor.wait_ge(sem("low_pool"), c + 1 + RING * g)
            return r(high[c % HIGH][:]), r(ring_r[SPLIT[c] % RING][:])

        def make_low(eng, engine, c, g=0):
            if engine == "dve" and not shared(c):
                return
            cut = TILE // 2 if shared(c) else 0
            at_ = slice(0, cut) if engine == "dve" else slice(cut, TILE)
            w, h = ring[SPLIT[c] % RING][:, at_], high[c % HIGH][:, at_]
            eng.wait_ge(sem("high"), c + 1 + RING * g)
            low = r(ring_r[SPLIT[c] % RING][:, at_])
            eng.tensor_tensor(low, w, h, ALU.subtract).then_inc(sem(f"low_{engine}"), 1)

        def make_down_low(eng, engine, d, g=0):
            at_ = slice(0, D // 2) if engine == "dve" else slice(D // 2, D)
            w, h = dring[d % RING][:, at_], dhigh[d % HIGH][:, at_]
            eng.wait_ge(sem("down_high"), d + 1 + RING * g)
            low = r(dring_r[d % RING][:, at_])
            eng.tensor_tensor(low, w, h, ALU.subtract).then_inc(sem(f"down_low_{engine}"), 1)

        def slices_loop(eng, slices, one, apart=0):
            turns = (slices - 1) // RING
            for j in range(apart * RING):
                one(j, 0)
            with eng.Fori(apart, turns) as g:
                for j in range(RING):
                    one(j, g)
            for j in range(turns * RING, slices):
                one(j, 0)

        @block.sync
        def _(sp):
            def load(t, src, g=0):
                if t >= RING:
                    sp.wait_ge(sem("tile_free"), t - RING + 1 + RING * g)
                sp.dma_start(ring[t % RING][:], src).then_inc(sem(f"tile_loaded{t % RING}"), 16)

            def load_down(d, src, g=0):
                if d >= RING:
                    sp.wait_ge(sem("down_free"), d - RING + 1 + RING * g)
                sp.dma_start(dring[d % RING][:], src).then_inc(sem(f"down_loaded{d % RING}"), 16)

            for name, n, first in PLAN:
                t0, src = TILE_AT[name], dram[name[0]]
                if name in DOWN_AT:
                    downs = dram[name[0] + "_down"]
                    d0 = DOWN_AT[name]
                    if t0 + 0 < RING or d0 < RING:
                        for j in range(RING):
                            load(t0 + j, src[first + j])
                            load_down(d0 + j, downs[first + j])
                        start = 1
                    else:
                        start = 0
                    with sp.Fori(start, n // RING) as g:
                        for j in range(RING):
                            load(t0 + j, src[first + j + RING * g], g)
                            load_down(d0 + j + (RING if start else 0), downs[first + j + RING * g], g - start)
                    for j in range(n // RING * RING, n):
                        load(t0 + j, src[first + j])
                        load_down(d0 + j, downs[first + j])
                else:
                    for j in range(n):
                        load(t0 + j, src[first + j])
            sp.wait_ge(*at("x_ready", "end"))
            sp.dma_start(out.rearrange("p (a b) -> p a b", a=KC), H2).then_inc(sem("stored"), 16)
            sp.wait_ge(sem("stored"), 16)

        @block.gpsimd
        def _(pool):
            def tiles(name, before=None):
                n = dict((a, b) for a, b, _ in PLAN)[name]
                for a in range(n):
                    if before is not None and a == 0:
                        before()
                    make_low(pool, "pool", SPLIT_AT[name] + a + 2)

            def swiglu(name, slices):
                c0, d0 = SPLIT_AT[name], DOWN_AT[name]

                def one(j, g):
                    if c0 + j + 2 < len(SPLIT):
                        make_low(pool, "pool", c0 + j + 2, g)
                    if j + 1 < slices:
                        make_down_low(pool, "pool", d0 + j + 1, g)

                make_down_low(pool, "pool", d0)
                slices_loop(pool, slices, one)

            def rotations(b, batch):
                tab = table[b]
                ptt = nc.gpsimd.tensor_tensor
                for n in range(S5_LEVELS):
                    d = 1 << n
                    low, new = tab[:, :, :, 0:d], tab[:, :, :, d:2 * d]
                    cos, sin = (pw[:, n, i, bass.ds(BATCH * batch, BATCH)].unsqueeze(1).unsqueeze(3)
                                .to_broadcast([P, 2, BATCH, d]) for i in range(2))
                    tmp = table_tmp[:, :, :, 0:d]
                    ptt(new, low, cos, ALU.mult)
                    ptt(tmp, low, sin, ALU.mult)
                    pool.drain()
                    ptt(new[:, 0], new[:, 0], tmp[:, 1], ALU.subtract)
                    i = ptt(new[:, 1], new[:, 1], tmp[:, 0], ALU.add)
                    if n == S5_LEVELS - 1:
                        i.then_inc(sem("tables"), 1)
                    pool.drain()

            def clear_wide(key, after):
                pool.wait_ge(*after)
                nc.gpsimd.memset(wide[:], 0.0).then_inc(*done("wide_zero", key))

            nc.gpsimd.memset(border[:], 0.0).then_inc(*done("border_zero", 0))
            make_low(pool, "pool", 0)
            make_low(pool, "pool", 1)
            for l in range(DEPTH):
                tiles(("win", l), lambda: clear_wide(l, at("mean_square", ("mix", l))))
                tiles(("wout", l))
                for s in range(2 if l == 0 else 1):
                    swiglu(("moe", l, s), SLICES)
                if l == 0:
                    pool.wait_ge(*at("x_ready", (("moe", 0, 1), KC - 1)))
                    nc.gpsimd.memset(border[:], 0.0).then_inc(*done("border_zero", 1))
            tiles(("foxin", 0))
            pool.wait_ge(*at("f_sp", 0))
            for b in range(2):
                nc.gpsimd.memset(table[b][:, 0, :, 0:1], 1.0)
                nc.gpsimd.memset(table[b][:, 1, :, 0:1], 0.0)
            pool.drain()
            for b in range(2):
                rotations(b, b)
            tiles(("foxout", 0))
            swiglu(("ffn", 0), FFN_SLICES)
            pool.wait_ge(*at("x_ready", (("ffn", 0), KC - 1)))
            pool.dma_start(bblk, dram["s5_b"]).then_inc(*done("s5_loaded", 0, 16))
            pool.dma_start(cT, dram["s5_c"]).then_inc(*done("s5_loaded", 1, 16))
            tiles(("s5in", 1))
            with pool.Fori(1, S5_CH // BATCH // 2) as g:
                for b in range(2):
                    pool.wait_ge(sem("states_done"), BATCH * (b - 1) + 2 * BATCH * g)
                    rotations(b, b + 2 * g)
            tiles(("glu", 1))
            swiglu(("ffn", 1), FFN_SLICES)
            pool.wait_ge(*at("x_ready", (("ffn", 1), KC - 1)))
            pool.dma_start(counts, dram["pool_counts"]).then_inc(*done("counts_loaded", 0, 16))
            clear_wide("pool", at("mean_square", ("pool",)))
            swiglu(("ffn", 2), FFN_SLICES)
            tiles(("foxin", 3))
            tiles(("foxout", 3))
            swiglu(("ffn", 3), FFN_SLICES)

        mm = nc.tensor.matmul

        @block.tensor
        def _(pe):
            def mm3(o, a, b, first, last, **kw):
                mm(o, a[0], b[0], start=first, stop=last and bool(kw), **kw)
                mm(o, a[0], b[1], start=False, stop=last and bool(kw), **kw)
                return mm(o, a[1], b[0], start=False, stop=last, **kw)

            def ada(l):
                t0 = TILE_AT["ada", l]

                def turn(j):
                    pe.wait_ge(*at("ada_row", (l, j)))
                    for c in range(2):
                        i = mm(ps[2][:, 4 * j + 2 * c:4 * j + 2 * c + 2], arow[0:2, j % 4, P * c:P * c + P],
                               ident[0:2, 0:2], start=True, stop=True)
                    i.then_inc(*done("ada_turned", (l, j)))

                for j in range(ADA_TILES):
                    t = t0 + j
                    pe.wait_ge(sem(f"tile_loaded{t % RING}"), 16 * (t // RING + 1))
                    w = ring[t % RING][:].rearrange("p (a b) -> p a b", a=KC)
                    if j >= 2:
                        pe.wait_ge(*at("ada_row", (l, j - 2)))
                    for c in range(KC):
                        i = mm(ps[j % 2][0:2, 0:TCOLS], sc2[:, c, :], w[:, c, :], start=c == 0, stop=c == KC - 1)
                    i.then_inc(sem("tile_free"), 1)
                    if j:
                        turn(j - 1)
                turn(ADA_TILES - 1)

            def mean_square(n, tok):
                for c in range(KC):
                    if c % 2 == 0:
                        pe.wait_ge(*at("squares", (n, c // 2)))
                    i = mm(ps[7][:, 0:tok.stop - tok.start], k("mean1024"), sq[:, c, tok],
                           start=c == 0, stop=c == KC - 1)
                i.then_inc(*done("mean_square", n))

            def project(name, groups, banks, ready, taken):
                for j, (out_ap, pairs) in enumerate(groups):
                    if j >= len(banks):
                        pe.wait_ge(*taken(j - len(banks)))
                    c0 = SPLIT_AT[name] + j // 2
                    for c, (a, b) in enumerate(pairs(*low_ready(c0))):
                        if j == 0:
                            pe.wait_ge(*ready(c))
                        i = mm3(out_ap(ps[banks[j % len(banks)]]), a, b, c == 0, c == KC - 1)
                    i.then_inc(*done("proj", (name, j))) if j % 2 == 0 else i.then_inc(sem("tile_free"), 1)

            def by_column(xh, xl, tok, m):
                def pairs(wh, wl):
                    for c in range(KC):
                        a = slice(c * TCOLS + m * P, c * TCOLS + m * P + P)
                        yield (wh[:, a], wl[:, a]), (r(xh[:, c, tok]), r(xl[:, c, tok]))
                return pairs

            def small_rows(bank, off, n, w, xh, xl, blocks):
                for b in range(blocks):
                    for c in range(KC):
                        for x in (xh, xl):
                            i = mm(ps[bank][:, off + n * b:off + n * b + n], x[:, c, b * P:b * P + P], w[:, c, :],
                                   start=c == 0 and x is xh, stop=c == KC - 1 and x is xl)
                return i

            def win(l):
                groups = []
                for j, ch in enumerate(W_IN_ORDER):
                    tok = slice(0, 2 * T) if l == 0 or 12 <= ch < 18 else slice(0, T)
                    groups.append((lambda bank, tok=tok: bank[:, tok], by_column(SB3, HT_r, tok, j % 2)))
                project(("win", l), groups, [0, 1, 2, 3, 4, 5], lambda c: at("normed", (("mix", l), c)),
                        lambda j: at(*win_taken(l, j)))
                small_rows(6, 0, 16, v(f"w_dt{l}"), SB3, HT_r, 4).then_inc(*done("dt_raw", l))

            def ssd(l, s, full):
                o = s * T
                fw, bw = k("fw4"), k("bw4")
                up, one, lo = fw[:, 0:P], fw[:, 2 * P:3 * P], bw[:, 2 * P:3 * P]
                da = dts[:, 5, :, :]
                b0, b1 = 2 * s, 2 * s + 1
                for c in range(KC):
                    pe.wait_ge(*at("ssd_in", (l, c)))
                for b in range(TB):
                    for c in range(4):
                        i = nc.tensor.transpose(ps[6 + b][:, c * P:c * P + P],
                                                HT[:, c, o + b * P:o + b * P + P], ident)
                    i.then_inc(*done("x_tok", (l, s, b)))
                pe.wait_ge(*at("x_tok_sb", (l, s, 0)))
                for b in range(TB):
                    for g in range(2):
                        i = nc.tensor.transpose(ps[6][:, (2 * b + g) * P:(2 * b + g + 1) * P],
                                                HT[:, 4 + g, o + b * P:o + b * P + P], ident)
                i.then_inc(*done("b_tok", (l, s)))
                pe.wait_ge(*at("da", l))
                pe.wait_ge(*at("x_tok_sb", (l, s, 1)))
                ac = ps[7]
                mm(ac[:, 0:8], up, da[:, b0, 0:8], start=True, stop=True)
                mm(ac[:, 16:24], one, da[:, b0, 0:8], start=True, stop=False)
                mm(ac[:, 16:24], up, da[:, b1, 0:8], start=False, stop=True)
                mm(ac[:, 24:32], lo, da[:, b1, 8:16], start=True, stop=True)
                mm(ac[:, 8:16], lo, da[:, b0, 8:16], start=True, stop=False)
                mm(ac[:, 8:16], one, da[:, b1, 8:16], start=False, stop=True)
                mm(ac[:, 32:48], one, da[:, b0, :], start=True, stop=False)
                mm(ac[:, 32:48], one, da[:, b1, :], start=False, stop=True).then_inc(*done("acum", (l, s)))
                if full:
                    for g in range(2):
                        pe.wait_ge(*(at("b_tok_sb", (l, s)) if g == 0 else at("acum_sb", (l, s))))
                        for b in range(TB):
                            i = mm(ps[6 + g][:, b * T:b * T + T], HT[:, 4 + g, o + b * P:o + b * P + P],
                                   HT[:, 6 + g, o:o + T], start=True, stop=True)
                        i.then_inc(*done("scores", (l, s, g)))
                if s == 1:
                    pe.wait_ge(*at("xw", l))
                    pe.wait_ge(*at("b_tok_sb", (l, s)))
                    for g in range(2):
                        if full:
                            pe.wait_ge(*at("scores_sb", (l, s, g)))
                        for b in range(TB):
                            i = mm(ps[6 + g][:], btok[:, b, g, :], xw[:, b, :, g * T:g * T + T],
                                   start=b == 0, stop=b == TB - 1)
                        i.then_inc(*done("states", (l, g)))
                if not full:
                    return

                def decay(h):
                    f, b = ps[2 * (h % 2)], ps[2 * (h % 2) + 1]
                    if h >= 2:
                        pe.wait_ge(*at("decayed", (l, s, h - 2)))
                    mm(f[:], da[:, b0, h:h + 1].to_broadcast([P, P]), fw, start=True, stop=True, skip_group_check=True)
                    mm(f[:, 2 * P:], da[:, b1, h:h + 1].to_broadcast([P, P]), fw[:, 0:2 * P], start=False, stop=True, skip_group_check=True)
                    fm = f[:].rearrange("p (a m c) -> p a m c", a=2, m=2)[:, :, 1, :]
                    mm(fm, identb, mask_f.unsqueeze(1).to_broadcast([P, 2, P]), start=False, stop=True, skip_group_check=True)
                    mm(b[:], da[:, b1, 8 + h:9 + h].to_broadcast([P, P]), bw, start=True, stop=True, skip_group_check=True)
                    mm(b[:, 0:2 * P], da[:, b0, 8 + h:9 + h].to_broadcast([P, P]), bw[:, 2 * P:], start=False, stop=True, skip_group_check=True)
                    bm = b[:].rearrange("p (a m c) -> p a m c", a=2, m=2)[:, :, 0, :]
                    mm(bm, identb, mask_b.unsqueeze(1).to_broadcast([P, 2, P]), start=False, stop=True, skip_group_check=True)\
                        .then_inc(*done("decay", (l, s, h)))

                def outputs(h):
                    c, q = h // 2, (h % 2) * HD
                    if h % 2 == 0 and c >= 2:
                        pe.wait_ge(*at("y_taken", (l, s, c - 2)))
                    pe.wait_ge(*at("mix_sb", (l, s, h)))
                    y = ps[4 + c % 2][q:q + HD, 0:T]
                    mm(y, xtok[:, 0, h * HD:h * HD + HD], mix0[:, h % 2, :], start=True, stop=False)
                    i = mm(y, xtok[:, 1, h * HD:h * HD + HD], mix1[:, h % 2, :], start=False, stop=s == 1)
                    if s == 0:
                        g, w = h // 4, (h % 4) * HD
                        mm(y, h0[:, g, 0, w:w + HD], off_f[:, h % 2, :], start=False, stop=False)
                        i = mm(y, h0[:, g, 1, w:w + HD], off_b[:, h % 2, :], start=False, stop=True)
                    i.then_inc(*done("y", (l, s, h)))

                decay(0)
                for h in range(HEADS):
                    if h + 1 < HEADS:
                        decay(h + 1)
                    outputs(h)

            def mean4(name, src, bank, tok, ready):
                for c in range(4):
                    pe.wait_ge(*ready(c))
                    i = mm(ps[bank][:, 0:tok.stop - tok.start], k("mean512"), src(c), start=c == 0, stop=c == 3)
                i.then_inc(*done("mean4", name))

            def wout(l, tok):
                groups = [(lambda bank: bank[:, 0:tok.stop], by_column(HT_r, MIX_r, tok, j % 2)) for j in range(KC)]
                project(("wout", l), groups, [0, 1, 2, 3], lambda c: at("mixed", (l, c)),
                        lambda j: at("res_dve", (("wout", l), j)))

            def router(l, blocks):
                for c in range(KC):
                    pe.wait_ge(*at("normed", (("ffn", l), c)))
                small_rows(6, 0, 20, v(f"w_rt{l}"), MIX_r, HT_r, blocks).then_inc(*done("logits", l))

            def comb_rows(l, s):
                pe.wait_ge(*at("comb", l))
                for j in range(EXPERTS // 2):
                    if j >= 2:
                        pe.wait_ge(*at("cw_sb", (l, s, j - 2)))
                    for e in range(2):
                        for b in range(TB):
                            at_e = comb[:, 2 * s + b, 2 * j + e:2 * j + e + 1]
                            i = mm(ps[6 + j % 2][:, e * T + b * P:e * T + b * P + P],
                                   at_e.to_broadcast([P, P]), ident, start=True, stop=True)
                    i.then_inc(*done("cw", (l, s, j)))

            def swiglu(name, slices, xh, xl, ready):
                if name == ("moe", 0, 1):
                    pe.wait_ge(*at("x_ready", (("moe", 0, 0), KC - 1)))
                c0, d0, hid0 = SPLIT_AT[name], DOWN_AT[name], base("hidden", name)
                for b in range(4):
                    mm(ps[b][:], zeros[:, 0:P], zeros, start=True, stop=True)
                for c in range(KC):
                    pe.wait_ge(*ready(c))

                def gate_up(j, g):
                    wh, wl = low_ready(c0 + j, g)
                    for m in range(2):
                        for c in range(KC):
                            a = slice(c * TCOLS + m * P, c * TCOLS + m * P + P)
                            i = mm3(ps[4 + j % 2][:, m * T:m * T + T], (wh[:, a], wl[:, a]), (r(xh(c)), r(xl(c))),
                                    c == 0, c == KC - 1)
                    i.then_inc(sem("tile_free"), 1)

                def down(j, g):
                    d = d0 + j
                    pe.wait_ge(sem("down_low_dve"), d + 1 + RING * g)
                    pe.wait_ge(sem("down_low_pool"), d + 1 + RING * g)
                    pe.wait_ge(sem("hidden"), hid0 + j + 1 + RING * g)
                    dh, dl = r(dhigh[d % HIGH][:]), r(dring_r[d % RING][:])
                    for c in range(KC):
                        a = slice(c * P, c * P + P)
                        i = mm3(ps[c // 2][:, (c % 2) * T:(c % 2) * T + T], (dh[:, a], dl[:, a]),
                                (r(hid[:, j % 2, 0, :]), r(hid[:, j % 2, 1, :])), False, True, skip_group_check=True)
                    i.then_inc(sem("down_free"), 1)

                gate_up(0, 0)
                turns = (slices - 1) // RING
                with pe.Fori(0, turns) as g:
                    for j in range(RING):
                        gate_up(j + 1, g)
                        down(j, g)
                for j in range(turns * RING, slices):
                    if j + 1 < slices:
                        gate_up(j + 1, 0)
                    down(j, 0)

            def fox(i_layer):
                j_fox = i_layer // 3
                name = ("fox", i_layer)
                groups = []
                for j in range(4):
                    for b in range(TB):
                        def pairs(wh, wl, b=b):
                            for c in range(KC):
                                t, a = slice(b * P, b * P + P), slice(c * TCOLS, c * TCOLS + TCOLS)
                                yield (r(H2h[:, c, t]), r(H2r[:, c, t])), (wh[:, a], wl[:, a])
                        groups.append((lambda bank: bank[:, 0:TCOLS], pairs))
                for j in range(16):
                    groups.append((lambda bank: bank[:, 0:T], by_column(H2h, H2r, slice(0, T), j % 2)))
                project(("foxin", i_layer), groups, [0, 1, 2, 3], lambda c: at("normed", (name, c)),
                        lambda j: at("fox_sb", (i_layer, j)))
                small_rows(7, 256, 16, v(f"w_f{j_fox}"), H2h, H2r, TB).then_inc(*done("f_raw", i_layer))

                fw = k("fw4")
                spl = fx[:, 5, :, :]

                def logits(h):
                    c, q = h // 2, (h % 2) * HD
                    L = ps[h % 2]
                    if h >= 2:
                        pe.wait_ge(*at("prob", (i_layer, h - 2)))
                    else:
                        pe.wait_ge(*at("fox_sb", (i_layer, 23)))
                        pe.wait_ge(*at("f_sp", i_layer))
                    mm(L[:, 0:384], spl[:, 0, h:h + 1].to_broadcast([P, P]), fw[:, 0:384], start=True, stop=True, skip_group_check=True)
                    mm(L[:, 256:384], spl[:, 1, h:h + 1].to_broadcast([P, P]), fw[:, 0:P], start=False, stop=True, skip_group_check=True)
                    diag = L[:].rearrange("p (a m c) -> p a m c", a=2, m=2)[:, :, 0, :]
                    mm(diag, identb, mask_b.unsqueeze(1).to_broadcast([P, 2, P]), start=False, stop=True, skip_group_check=True)
                    mm(L[:, 0:P], Q2[q:q + HD, c, 0:P], K2[q:q + HD, c, 0:P], start=False, stop=True, skip_group_check=True)
                    mm(L[:, P:384], Q2[q:q + HD, c, P:T], K2[q:q + HD, c, 0:T], start=False, stop=True, skip_group_check=True)\
                        .then_inc(*done("att", (i_layer, h)))

                def turn(h):
                    pe.wait_ge(*at("prob_n", (i_layer, h)))
                    if h >= 2:
                        pe.wait_ge(*at("probT", (i_layer, h - 2)))
                    for blk, to in ((0, 0), (1, 1), (2, 2)):
                        i = nc.tensor.transpose(ps[2 + h % 2][:, to * P:to * P + P],
                                                prob[:, h % 2, blk * P:blk * P + P], ident)
                    i.then_inc(*done("att_turned", (i_layer, h)))

                def values(h):
                    c, q = h // 2, (h % 2) * HD
                    pe.wait_ge(*at("probT", (i_layer, h)))
                    if h % 2 == 0 and c >= 2:
                        pe.wait_ge(*at("o_high", (i_layer, c - 2)))
                    o = ps[4 + c % 2]
                    mm(o[q:q + HD, 0:T], vtok[:, 0, h * HD:h * HD + HD], probT[:, h % 2, 0:T], start=True, stop=False)
                    mm(o[q:q + HD, P:T], vtok[:, 1, h * HD:h * HD + HD], probT[:, h % 2, T:384],
                       start=False, stop=True).then_inc(*done("o", (i_layer, h)))

                for h in range(FOX_HEADS + 2):
                    if h < FOX_HEADS:
                        logits(h)
                    if 1 <= h <= FOX_HEADS:
                        turn(h - 1)
                    if h >= 2:
                        values(h - 2)
                groups = [(lambda bank: bank[:, 0:T], by_column(H2r, O2r, slice(0, T), j % 2)) for j in range(KC)]
                project(("foxout", i_layer), groups, [0, 1, 2, 3], lambda c: at("o_split", (i_layer, c)),
                        lambda j: at("res_dve", (("foxout", i_layer), j)))

            def s5():
                groups = [(lambda bank: bank[:, 0:T], by_column(H2h, H2r, slice(0, T), j % 2)) for j in range(KC)]
                project(("s5in", 1), groups, [0, 1, 2, 3], lambda c: at("normed", (("s5",), c)),
                        lambda j: at("u_sb", j))
                pe.wait_ge(*at("b_bar"))
                for c in range(KC):
                    for r in range(2):
                        if c >= 2:
                            pe.wait_ge(*at("bT", c - 2))
                        i = nc.tensor.transpose(
                            ps[4 + c % 2][:, r * P:r * P + P],
                            bblk[:, r, 4 * c:4 * c + 4, :].rearrange("p a b -> p (a b)"), ident)
                    i.then_inc(*done("b_turned", c))
                pe.wait_ge(*at("bT", KC - 1))
                pe.wait_ge(*at("u_sb", KC - 1))
                pe.wait_ge(*at("c_neg"))
                pe.wait_ge(*at("s5_dmat"))

                def inputs(j):
                    q, c = 32 * (j % 4), j // 4
                    if j >= 2:
                        pe.wait_ge(sem("bu_used"), j - 1)
                    for i in range(2):
                        mm_ = mm(ps[j % 2][:, i * T:i * T + T], bT[q:q + 32, i, c, :], Q2[q:q + 32, c, :],
                                 start=True, stop=True, tile_position=(q, 0))
                    mm_.then_inc(sem("bu"), 1)

                def outputs(j):
                    q, c = 32 * (j % 4), j // 4
                    bank = ps[2 + c % 2]
                    if j % 4 == 0:
                        if c >= 2:
                            pe.wait_ge(*at("s5_y", c - 2))
                        mm(bank[:, 0:T], s5_dmat[:, c, :], Q2[:, c, :], start=True, stop=False, skip_group_check=True)
                    pe.wait_ge(sem("states_done"), j + 1)
                    y = bank[q:q + 32, 0:T]
                    for n, (part, z) in enumerate(((0, s5_q[:, j % 2, 0, 0, :]), (0, s5_q[:, j % 2, 1, 0, :]),
                                                   (1, s5_q[:, j % 2, 0, 1, :]), (1, s5_q[:, j % 2, 1, 1, :]))):
                        i = mm(y, cT[:, part, j, :], z, start=False, stop=n == 3, skip_group_check=True, tile_position=(0, q))
                    i.then_inc(sem("s5_out"), 1)

                inputs(0)
                for j in range(S5_CH):
                    if j + 1 < S5_CH:
                        inputs(j + 1)
                    outputs(j)
                groups = [(lambda bank: bank[:, 0:T], by_column(H2r, O2r, slice(0, T), j % 2)) for j in range(2 * KC)]
                project(("glu", 1), groups, [4, 5, 6, 7], lambda c: at("gelu_split", c),
                        lambda j: at("glu_val", j // 2) if j % 2 == 0 else at("glu_gate", j // 2))

            def pooling():
                t0 = TILE_AT["poolw", 2]
                pe.wait_ge(sem(f"tile_loaded{t0 % RING}"), 16 * (t0 // RING + 1))
                w = ring[t0 % RING][:].rearrange("p (g a n) -> p g a n", g=POOLS, a=2)
                for j in range(KC):
                    g, m = j // 2, j % 2
                    if j >= 4:
                        pe.wait_ge(*at("res_dve", (("poolw", 2), j - 4)))
                    if m == 0:
                        pe.wait_ge(*at("pooled", g))
                    for a in range(2):
                        i = mm(ps[j % 4][:, 0:T], w[:, g, a, m * P:m * P + P], O2[:, 2 * g + a, :],
                               start=a == 0, stop=a == 1)
                    i.then_inc(*done("proj", (("poolw", 2), j)))
                pe.wait_ge(*at("res_dve", (("poolw", 2), KC - 1)))
                nc.tensor.sem_inc(sem("tile_free"), 1)

            pe.wait_ge(*at("c2_silu"))
            pe.wait_ge(sem("con_loaded"), 16)
            ada(0)
            pe.wait_ge(sem("vec_loaded"), 16 * 2)
            for l in range(DEPTH):
                both, last = slice(0, 2 * T), l == DEPTH - 1
                tok = slice(0, T) if last else both
                mean_square(("mix", l), both)
                win(l)
                if not last:
                    for j in (0, 1):
                        pe.wait_ge(*at(*win_taken(l, 18 + j)))
                    pe.wait_ge(*at(*win_taken(l, 14)))
                    ada(l + 1)
                ssd(l, 1, not last)
                pe.wait_ge(*at("h0", (l, 1)))
                ssd(l, 0, True)
                mean4(("ln_mean", l), lambda c: MIX[:, c, tok], 6, tok, lambda c: at("conv_y", l))
                mean4(("ln_var", l), lambda c: sq[:, c, tok], 7, tok, lambda c: at("ln_sq", l))
                mean4(("ssd_ms", l), lambda c: sq[:, 4 + c, tok], 6, tok, lambda c: at("ssd_sq", l))
                wout(l, tok)
                mean_square(("ffn", l), tok)
                router(l, 2 if last else 4)
                for s in range(1 if last else 2):
                    comb_rows(l, s)
                    swiglu(("moe", l, s), SLICES, lambda c, s=s: MIX_r[:, c, s * T:s * T + T],
                           lambda c, s=s: HT_r[:, c, s * T:s * T + T], lambda c: at("cw_sb", (l, s, EXPERTS // 2 - 1)))
            mean_square(("final1",), slice(0, T))
            for i_layer in range(4):
                name = (("fox", 0), ("s5",), ("pool",), ("fox", 3))[i_layer]
                mean_square(name, slice(0, T))
                if i_layer in (0, 3):
                    fox(i_layer)
                elif i_layer == 1:
                    s5()
                else:
                    pooling()
                mean_square(("ffn2", i_layer), slice(0, T))
                swiglu(("ffn", i_layer), FFN_SLICES, lambda c: H2h[:, c, :], lambda c: H2r[:, c, :],
                       lambda c: at("normed", (("ffn2", i_layer), c)))
            mean_square(("final2",), slice(0, T))

        act_fn = nc.scalar.activation

        @block.scalar
        def _(act):
            c2_at, c2_end = VEC_AT["c2"][0], VEC_AT["c2"][0] + 2 * KC
            act.dma_start(vec[:, c2_at:c2_end], dram["vec"][:, c2_at:c2_end]).then_inc(sem("c2_loaded"), 16)
            act.dma_start(con[:], dram["con"]).then_inc(sem("con_loaded"), 16)
            act.dma_start(XT[:], dram["xt"]).then_inc(sem("x_loaded"), 16)
            act.dma_start(vec[:, c2_end:], dram["vec"][:, c2_end:]).then_inc(sem("vec_loaded"), 16)
            act.dma_start(msk[:], dram["msk"]).then_inc(sem("vec_loaded"), 16)
            act.wait_ge(sem("c2_loaded"), 16)
            act_fn(sc2[:], v("c2"), ACT.Silu).then_inc(*done("c2_silu"))

            def make_high(c, g=0):
                if c >= len(SPLIT):
                    return
                t = SPLIT[c]
                act.wait_ge(sem(f"tile_loaded{t % RING}"), 16 * (t // RING + 1) + 16 * g)
                if c >= HIGH:
                    act.wait_ge(sem("tile_free"), SPLIT[c - HIGH] + 1 + RING * g)
                nc.scalar.copy(r(high[c % HIGH][:]), ring[t % RING][:]).then_inc(sem("high"), 1)

            def make_down_high(d, g=0):
                act.wait_ge(sem(f"down_loaded{d % RING}"), 16 * (d // RING + 1) + 16 * g)
                if d >= HIGH or not isinstance(g, int):
                    act.wait_ge(sem("down_free"), d - HIGH + 1 + RING * g)
                nc.scalar.copy(r(dhigh[d % HIGH][:]), dring[d % RING][:]).then_inc(sem("down_high"), 1)

            def ada(l):
                for j in range(ADA_TILES):
                    act.wait_ge(sem("tile_free"), TILE_AT["ada", l] + j + 1)
                    if j >= 4:
                        act.wait_ge(*at("ada_turned", (l, j - 4)))
                    nc.scalar.copy(arow[0:2, j % 4, :], ps[j % 2][0:2, 0:TCOLS]).then_inc(*done("ada_row", (l, j)))
                    if l == 0 and j == ADA_TILES // 2:
                        act.wait_ge(sem("vec_loaded"), 32)
                        act_fn(s5p[:, 0, :], v("log_dt"), ACT.Exp).then_inc(*done("s5_dt"))
                    if l == 0 and j == ADA_TILES // 2 + 6:
                        act.wait_ge(*at("s5_ang"))
                        act_fn(s5p[:, 3, :], s5p[:, 1, :], ACT.Exp)
                        act_fn(s5p[:, 6, :], s5p[:, 4, :], ACT.Sin)
                        act_fn(s5p[:, 7, :], s5p[:, 5, :], ACT.Sin).then_inc(*done("s5_trig"))

            def squares(n, tok, ready):
                for p in range(KC // 2):
                    act.wait_ge(*ready(2 * p + 1))
                    act_fn(sq[:, 2 * p:2 * p + 2, tok], XT[:, 2 * p:2 * p + 2, tok], ACT.Square)\
                        .then_inc(*done("squares", (n, p)))
                act.wait_ge(*at("mean_square", n))
                act_fn(rms[:, 0:tok.stop], ps[7][:, 0:tok.stop], ACT.Sqrt, bias=k("eps6")).then_inc(*done("root", n))

            def split_high(n, dst, src, bias, streams):
                for c in range(KC):
                    for s in range(streams):
                        act.wait_ge(*at("scaled", (n, c, s)))
                        o, i = r(dst[:, c, s * T:s * T + T]), src[:, c, s * T:s * T + T]
                        i = nc.scalar.copy(o, i) if bias is None else act_fn(o, i, ACT.Identity, bias=bias(c, s))
                        i.then_inc(*done("norm_high", (n, c, s)))

            def win(l):
                streams = 1 if l == DEPTH - 1 else 2
                for j, ch in enumerate(W_IN_ORDER):
                    if ch >= 4:
                        act.wait_ge(*proj_at(("win", l), j))
                    if ch < 4:
                        pass
                    elif ch < 8:
                        if ch >= 6:
                            act.wait_ge(*at("gated", (l, ch - 6)))
                        act_fn(sig[:, ch % 2, 0:streams * T], ps[j % 6][:, 0:streams * T], ACT.Sigmoid)\
                            .then_inc(*done("win_act", (l, j)))
                    elif ch < 12:
                        act_fn(zs[:, ch - 8, 0:streams * T], ps[j % 6][:, 0:streams * T], ACT.Silu)\
                            .then_inc(*done("win_act", (l, j)))
                    else:
                        if ch == 12:
                            act.wait_ge(*at("wide_zero", l))
                        n = 2 if ch < 18 else streams
                        act_fn(xbc[:, ch - 12, 0:n, 2:2 + T],
                               ps[j % 6][:, 0:n * T].rearrange("p (a b) -> p a b", a=n), ACT.Copy)\
                            .then_inc(*done("win_act", (l, j)))
                    if j % 2 and j // 2 + 2 < WIN_TILES:
                        make_high(SPLIT_AT["win", l] + j // 2 + 2)

            def softplus_log(name, key, e, src):
                act.wait_ge(*at(name + "_abs", key))
                act_fn(e, src, ACT.Exp, scale=-1.0)
                act.drain()
                act_fn(e, e, ACT.Ln, bias=1.0).then_inc(*done(name + "_log", key))

            def ssd_in(l):
                streams = 1 if l == DEPTH - 1 else 2
                for c in range(8):
                    act.wait_ge(*at("sconv", l))
                    n = 2 * T if c < 6 else streams * T
                    act_fn(HT[:, c, 0:n], HT[:, c, 0:n], ACT.Silu).then_inc(*done("ssd_in", (l, c)))

            def ssd(l, s, full):
                for b in range(TB):
                    act.wait_ge(*at("x_tok", (l, s, b)))
                    nc.scalar.copy(xtok[:, b, :], ps[6 + b][:]).then_inc(*done("x_tok_sb", (l, s, b)))
                act.wait_ge(*at("b_tok", (l, s)))
                nc.scalar.copy(btok[:].rearrange("p a b c -> p (a b c)"), ps[6][:]).then_inc(*done("b_tok_sb", (l, s)))
                if full:
                    for g in range(2):
                        act.wait_ge(*at("scores", (l, s, g)))
                        nc.scalar.copy(score[:, g, :, :].rearrange("p a b -> p (a b)"), ps[6 + g][:])\
                            .then_inc(*done("scores_sb", (l, s, g)))
                if s == 1:
                    act.wait_ge(*at("to_end", l))
                    act_fn(wst[:, 1, :, :], wst[:, 0, :, :], ACT.Exp).then_inc(*done("end_decay", l))
                    for g in range(2):
                        act.wait_ge(*at("states", (l, g)))
                        nc.scalar.copy(h0[:, g, :, :].rearrange("p a b -> p (a b)"), ps[6 + g][:]).then_inc(*done("h0", (l, g)))
                if not full:
                    return
                act.wait_ge(*at("acum_sb", (l, s)))
                for h in range(HEADS):
                    p = h % 2
                    f, b = ps[2 * p], ps[2 * p + 1]
                    act.wait_ge(*at("decay", (l, s, h)))
                    if h >= 2:
                        act.wait_ge(*at("mix_sb", (l, s, h - 2)))
                    act_fn(dec_f0[:, p, :], f[:, P:3 * P], ACT.Exp, bias=nacum[:, 0, h:h + 1])
                    act_fn(dec_f1[:, p, :], f[:, 3 * P:], ACT.Exp, bias=nacum[:, 1, h:h + 1])
                    act_fn(dec_b1[:, p, :], b[:, P:3 * P], ACT.Exp, bias=nacum[:, 1, 8 + h:9 + h])
                    i = act_fn(dec_b0[:, p, :], b[:, 0:P], ACT.Exp, bias=nacum[:, 0, 8 + h:9 + h])
                    if s == 0:
                        act_fn(off_f[:, p, :].rearrange("p (a c) -> p a c", a=2),
                               f[:].rearrange("p (a m c) -> p a m c", a=2, m=2)[:, :, 0, :], ACT.Exp)
                        i = act_fn(off_b[:, p, :].rearrange("p (a c) -> p a c", a=2),
                                   b[:].rearrange("p (a m c) -> p a m c", a=2, m=2)[:, :, 1, :], ACT.Exp)
                    i.then_inc(*done("decayed", (l, s, h)))

            def mixer_norms(l, tok):
                act.wait_ge(*at("centred", l))
                act_fn(sq[:, 0:4, tok], MIX[:, 0:4, tok], ACT.Square).then_inc(*done("ln_sq", l))
                act.wait_ge(*at("y_done", l))
                act_fn(sq[:, 4:8, tok], MIX[:, 4:8, tok], ACT.Square).then_inc(*done("ssd_sq", l))
                act.wait_ge(*at("mean4", ("ln_var", l)))
                act_fn(rms[:, tok], ps[7][:, tok], ACT.Sqrt, bias=k("eps5")).then_inc(*done("ln_root", l))
                act.wait_ge(*at("mean4", ("ssd_ms", l)))
                act.wait_ge(*at("ln_rstd", l))
                act_fn(rms[:, tok], ps[6][:, tok], ACT.Sqrt, bias=k("eps6")).then_inc(*done("ssd_root", l))
                for c in range(4):
                    act.wait_ge(*at("ln_scaled", l))
                    act_fn(MIX[:, c, tok], MIX[:, c, tok], ACT.Silu, bias=v(f"ln_b{l}")[:, c:c + 1],
                           scale=v(f"ln_g{l}")[:, c:c + 1])
                act.drain()
                for c in range(KC):
                    if c >= 4:
                        act.wait_ge(*at("ssd_out", (l, c - 4)))
                    nc.scalar.copy(r(HT_r[:, c, tok]), MIX[:, c, tok]).then_inc(*done("mix_high", (l, c)))

            def router(l):
                act.wait_ge(*at("rt_shift", l))
                act_fn(rt[:, 2, :, 0:4], rt[:, 1, :, 0:4], ACT.Exp)
                act_fn(rt[:, 2, :, 4:8], rt[:, 1, :, 4:8], ACT.Exp).then_inc(*done("rt_exp", l))

            def comb_rows(l, s):
                for j in range(EXPERTS // 2):
                    act.wait_ge(*at("cw", (l, s, j)))
                    nc.scalar.copy(cw[:, 2 * j:2 * j + 2, :].rearrange("p a b -> p (a b)"), ps[6 + j % 2][:])\
                        .then_inc(*done("cw_sb", (l, s, j)))

            def swiglu(name, slices):
                t0, c0, d0 = TILE_AT[name], SPLIT_AT[name], DOWN_AT[name]
                loop_base("gate_act", name, slices)

                def one(j, g):
                    act.wait_ge(sem("tile_free"), t0 + j + 1 + RING * g)
                    act_fn(gact[:, j % 2, :], ps[4 + j % 2][:, 0:T], ACT.Silu).then_inc(sem("gate_act"), 1)
                    make_high(c0 + j + 2, g)
                    if j + 1 < slices:
                        make_down_high(d0 + j + 1, g)

                make_down_high(d0)
                slices_loop(act, slices, one, 1 if d0 == 0 else 0)

            def tiles_after(name, j):
                if j % 2:
                    make_high(SPLIT_AT[name] + j // 2 + 2)

            def fox(i_layer):
                for j in range(24):
                    act.wait_ge(*proj_at(("foxin", i_layer), j))
                    bank = ps[j % 4]
                    if j < 8:
                        i = nc.scalar.copy(vtok[:, j % 2, TCOLS * (j // 2):TCOLS * (j // 2) + TCOLS], bank[:, 0:TCOLS])
                    elif j < 16:
                        i = nc.scalar.mul(Q2[:, j - 8, :], bank[:, 0:T], HD ** -0.5)
                    else:
                        i = nc.scalar.copy(K2[:, j - 16, :], bank[:, 0:T])
                    i.then_inc(*done("fox_sb", (i_layer, j)))
                    tiles_after(("foxin", i_layer), j)
                softplus_log("f", i_layer, fx[:, 3, :, :], fx[:, 1, :, :])
                for h in range(FOX_HEADS + 2):
                    p = h % 2
                    if h < FOX_HEADS:
                        act.wait_ge(*at("att_max", (i_layer, h)))
                        if h >= 2:
                            act.wait_ge(*at("att_turned", (i_layer, h - 2)))
                        L = ps[p]
                        act_fn(prob[:, p, 0:P], L[:, 0:P], ACT.Exp, bias=stat[:, p, 0, 0:1], accum_out=stat[:, p, 1, 0:1])
                        act_fn(prob[:, p, P:384], L[:, P:384], ACT.Exp, bias=stat[:, p, 0, 1:2],
                               accum_out=stat[:, p, 1, 1:2]).then_inc(*done("prob", (i_layer, h)))
                    if 1 <= h <= FOX_HEADS:
                        q = (h - 1) % 2
                        act.wait_ge(*at("att_turned", (i_layer, h - 1)))
                        if h >= 3:
                            act.wait_ge(*at("o", (i_layer, h - 3)))
                        nc.scalar.copy(probT[:, q, :], ps[2 + q][:, 0:384]).then_inc(*done("probT", (i_layer, h - 1)))
                    if h >= 2 and h % 2 == 1:
                        c = (h - 2) // 2
                        act.wait_ge(*at("o", (i_layer, h - 2)))
                        nc.scalar.copy(O2[:, c, :], ps[4 + c % 2][:, 0:T]).then_inc(*done("o_sb", (i_layer, c)))
                        act_fn(r(H2r[:, c, :]), ps[4 + c % 2][:, 0:T], ACT.Copy).then_inc(*done("o_high", (i_layer, c)))

            def s5():
                for j in range(KC):
                    act.wait_ge(*proj_at(("s5in", 1), j))
                    nc.scalar.copy(Q2[:, j, :], ps[j % 4][:, 0:T]).then_inc(*done("u_sb", j))
                    tiles_after(("s5in", 1), j)
                for c in range(KC):
                    act.wait_ge(*at("b_turned", c))
                    nc.scalar.copy(bT[:, :, c, :], ps[4 + c % 2][:, 0:2 * P].rearrange("p (a b) -> p a b", a=2))\
                        .then_inc(*done("bT", c))
                for c in range(KC):
                    act.wait_ge(sem("s5_out"), 2 + 4 * c + 4)
                    act_fn(O2[:, c, :], ps[2 + c % 2][:, 0:T], ACT.Gelu_apprx_tanh).then_inc(*done("s5_y", c))
                    act.drain()
                    nc.scalar.copy(r(H2r[:, c, :]), O2[:, c, :]).then_inc(*done("gelu_high", c))
                for j in range(KC):
                    act.wait_ge(*proj_at(("glu", 1), 2 * j + 1))
                    if j >= 2:
                        act.wait_ge(*at("res_dve", (("glu", 1), j - 2)))
                    act_fn(sig[:, j % 2, 0:T], ps[4 + (2 * j + 1) % 4][:, 0:T], ACT.Sigmoid).then_inc(*done("glu_gate", j))
                    tiles_after(("glu", 1), 2 * j + 1)

            ada(0)
            make_high(0)
            make_high(1)
            act.wait_ge(sem("x_loaded"), 16)
            act.wait_ge(sem("con_loaded"), 16)
            act.wait_ge(sem("vec_loaded"), 32)
            for l in range(DEPTH):
                last = l == DEPTH - 1
                tok = slice(0, T) if last else slice(0, 2 * T)
                bias = lambda which: lambda c, s: mod[l][:, 24 * which + c, s:s + 1]
                act_fn(aneg[:, 0, :], v(f"a_log{l}"), ACT.Exp).then_inc(*done("a_exp", l))
                squares(("mix", l), slice(0, 2 * T),
                        (lambda c: at("x_ready", (("moe", l - 1, 1), c))) if l else lambda c: (sem("x_loaded"), 16))
                split_high(("mix", l), SB3, HT, bias(0), 2)
                win(l)
                if not last:
                    ada(l + 1)
                softplus_log("dt", l, dts[:, 3, :, :], dts[:, 1, :, :])
                ssd_in(l)
                for j in (0, 1):
                    make_high(SPLIT_AT["wout", l] + j)
                ssd(l, 1, not last)
                ssd(l, 0, True)
                mixer_norms(l, tok)
                for a in range(HALF_D):
                    tiles_after(("wout", l), 2 * a + 1)
                squares(("ffn", l), tok, lambda c: at("res_dve", (("wout", l), c)))
                split_high(("ffn", l), MIX_r, HT, bias(1), 1 if last else 2)
                router(l)
                for s in range(1 if last else 2):
                    comb_rows(l, s)
                    swiglu(("moe", l, s), SLICES)
            squares(("final1",), slice(0, T), lambda c: at("x_ready", (("moe", 1, 0), c)))
            for i_layer in range(4):
                name = (("fox", 0), ("s5",), ("pool",), ("fox", 3))[i_layer]
                squares(name, slice(0, T), lambda c: at("x_ready", (("ffn", i_layer - 1), c) if i_layer else ("first", c)))
                if i_layer != 2:
                    split_high(name, H2h, H2, None, 1)
                last_res = (("foxout", 0), ("glu", 1), ("poolw", 2), ("foxout", 3))[i_layer]
                if i_layer in (0, 3):
                    fox(i_layer)
                    for a in range(HALF_D):
                        tiles_after(last_res, 2 * a + 1)
                elif i_layer == 1:
                    s5()
                squares(("ffn2", i_layer), slice(0, T), lambda c: at("res_dve", (last_res, c)))
                split_high(("ffn2", i_layer), H2h, H2, None, 1)
                swiglu(("ffn", i_layer), FFN_SLICES)
            squares(("final2",), slice(0, T), lambda c: at("x_ready", (("ffn", 3), c)))

        stt, tt, ts = nc.vector.scalar_tensor_tensor, nc.vector.tensor_tensor, nc.vector.tensor_scalar
        tss = nc.vector.tensor_single_scalar

        @block.vector
        def _(dve):
            dve.wait_ge(sem("con_loaded"), 16)
            dve.wait_ge(sem("vec_loaded"), 32)
            dve.wait_ge(sem("x_loaded"), 16)

            def ada(l):
                dve.wait_ge(*at("ada_turned", (l, ADA_TILES - 1)))
                tt(mod[l][:], ps[2][:, 0:96].rearrange("p (a b) -> p a b", a=48), v(f"b_ada{l}"), ALU.add)
                dve.drain()
                for which, g in ((0, "g_mix"), (1, "g_ffn")):
                    stt(gsc[l][:, which, :, :], mod[l][:, 24 * which + 8:24 * which + 16, :], 1.0, v(f"{g}{l}"),
                        ALU.add, ALU.mult)
                dve.drain()

            def scale(n, streams, gain, bias=None, xh=None):
                dve.wait_ge(*at("root", n))
                nc.vector.reciprocal(rstd[:, 0:streams * T], rms[:, 0:streams * T])
                dve.drain()

                def low(c):
                    for s in range(streams):
                        h, hh = HT_(c, s), xh[:, c, s * T:s * T + T]
                        dve.wait_ge(*at("norm_high", (n, c, s)))
                        to = r(H2r[:, c, :] if bias is None else HT_r[:, c, s * T:s * T + T])
                        i = tt(to, h, hh, ALU.subtract) if bias is None else \
                            stt(to, h, bias(c, s), hh, ALU.add, ALU.subtract)
                    i.then_inc(*done("normed", (n, c)))

                HT_ = lambda c, s: HT[:, c, s * T:s * T + T] if bias is not None else H2[:, c, :]
                for c in range(KC):
                    for s in range(streams):
                        stt(HT_(c, s), XT[:, c, s * T:s * T + T], gain(c, s), rstd[:, s * T:s * T + T], ALU.mult, ALU.mult)\
                            .then_inc(*done("scaled", (n, c, s)))
                    if xh is not None and c:
                        low(c - 1)
                if xh is not None:
                    low(KC - 1)

            def tiles(name, j=None):
                n = dict((a, b) for a, b, _ in PLAN)[name]
                for a in range(n) if j is None else [j]:
                    if SPLIT_AT[name] + a + 2 < len(SPLIT):
                        make_low(dve, "dve", SPLIT_AT[name] + a + 2)

            def gate(l):
                flat = W_IN_ORDER
                dve.wait_ge(*at("border_zero", l))
                for c in range(4):
                    ju, jg = flat.index(c), flat.index(4 + c)
                    dve.wait_ge(*proj_at(("win", l), ju))
                    dve.wait_ge(*at("win_act", (l, jg)))
                    bank = ps[ju % 6]
                    if c < 2:
                        dst = vrow[:, c, :, HALF:HALF + GRID_W]
                    else:
                        dst = vcol[:, c - 2, 3:3 + ROWS, :]
                    i = tt(dst, bank[:, 0:T].rearrange("p (a b) -> p a b", a=ROWS),
                           sig[:, c % 2, 0:T].rearrange("p (a b) -> p a b", a=ROWS), ALU.mult)
                    if l < DEPTH - 1:
                        i = tt(vseq[:, c, HALF:HALF + T], bank[:, T:2 * T], sig[:, c % 2, T:2 * T], ALU.mult)
                    i.then_inc(*done("gated", (l, c)))
                dve.drain()

            def conformer(l):
                w, b = v(f"conv_w{l}"), v(f"conv_b{l}")

                def grid(c):
                    return MIX[:, c, 0:T].rearrange("p (a b) -> p a b", a=ROWS)

                first = HALF - (ROWS - 1)
                for c in range(4):
                    src = vrow[:, c, :, 0:GRID_W] if c < 2 else vcol[:, c - 2, 0:ROWS, :]
                    tap = 0 if c < 2 else first
                    ts(grid(c), src, w[:, c, tap:tap + 1], b[:, c:c + 1], ALU.mult, ALU.add)
                    if l < DEPTH - 1:
                        ts(MIX[:, c, T:2 * T], vseq[:, c, 0:T], w[:, c, 0:1], b[:, c:c + 1], ALU.mult, ALU.add)
                dve.drain()
                with dve.Fori(1, TAPS) as tap:
                    for c in range(2):
                        stt(grid(c), vrow[:, c, :, bass.ds(tap, GRID_W)], w[:, c, bass.ds(tap, 1)], grid(c), ALU.mult, ALU.add)
                    if l < DEPTH - 1:
                        for c in range(4):
                            y = MIX[:, c, T:2 * T]
                            stt(y, vseq[:, c, bass.ds(tap, T)], w[:, c, bass.ds(tap, 1)], y, ALU.mult, ALU.add)
                    dve.drain()
                for r in range(1, 2 * ROWS - 1):
                    for c in range(2, 4):
                        i = stt(grid(c), vcol[:, c - 2, r:r + ROWS, :], w[:, c, first + r:first + r + 1], grid(c), ALU.mult, ALU.add)
                    if r < 2 * ROWS - 2:
                        dve.drain()
                i.then_inc(*done("conv_y", l))

            def sconv(l):
                w, b = v(f"sconv_w{l}"), v(f"sconv_b{l}")
                dve.wait_ge(*at("win_act", (l, W_IN_ORDER.index(19))))
                dve.wait_ge(*at("dt_raw", l))
                streams = 1 if l == DEPTH - 1 else 2
                for tap in range(STAPS):
                    for c in range(8):
                        n = 2 if c < 6 else streams
                        y = HT[:, c, 0:n * T].rearrange("p (a b) -> p a b", a=n)
                        src = xbc[:, c, 0:n, tap:tap + T]
                        if tap == 0:
                            i = ts(y, src, w[:, c, 0:1], b[:, c:c + 1], ALU.mult, ALU.add)
                        else:
                            i = stt(y, src, w[:, c, tap:tap + 1], y, ALU.mult, ALU.add)
                    if tap == STAPS - 1:
                        i.then_inc(*done("sconv", l))
                    else:
                        dve.drain()

            def softplus(name, key, raw, bias, x, ab, mx, lp, res, sign):
                tt(x, raw, bias, ALU.add)
                dve.drain()
                tss(lp, x, -1.0, ALU.mult)
                ts(mx, x, sign, 0.0, ALU.mult, ALU.max)
                dve.drain()
                tt(ab, x, lp, ALU.max).then_inc(*done(name + "_abs", key))
                dve.wait_ge(*at(name + "_log", key))
                tt(res, mx, lp, ALU.add)
                dve.drain()

            def steps(l):
                dve.wait_ge(*at("dt_raw", l))
                raw = ps[6][:, 0:64].rearrange("p (a b) -> p a b", a=4)
                bias = v(f"dt_bias{l}").unsqueeze(1).to_broadcast([P, 4, 16])
                softplus("dt", l, raw, bias, dts[:, 0, :, :], dts[:, 1, :, :], dts[:, 2, :, :], dts[:, 3, :, :],
                         dts[:, 4, :, :], 1.0)
                dve.wait_ge(*at("a_exp", l))
                tss(aneg[:, 1, :], aneg[:, 0, :], -1.0, ALU.mult)
                dve.drain()
                tt(dts[:, 5, :, :], dts[:, 4, :, :], aneg[:, 1, :].unsqueeze(1).to_broadcast([P, 4, 16]), ALU.mult)\
                    .then_inc(*done("da", l))

            def ssd(l, s, full):
                o = s * T
                dt = dts[:, 4, :, :]
                dve.wait_ge(*at("acum", (l, s)))
                if s == 1:
                    tss(nacum[:], ps[7][:, 0:32].rearrange("p (a b) -> p a b", a=2), -1.0, ALU.mult)
                    dve.drain()
                    tt(wst[:, 0, :, :], nacum[:], ps[7][:, 32:48].unsqueeze(1).to_broadcast([P, 2, 16]), ALU.add)\
                        .then_inc(*done("to_end", l))
                    dve.drain()
                    dve.drain().then_inc(*done("acum_sb", (l, s)))
                    dve.wait_ge(*at("end_decay", l))
                    tt(wst[:, 0, :, :], wst[:, 1, :, :], dt[:, 2:4, :], ALU.mult)
                    dve.wait_ge(*at("x_tok_sb", (l, s, 1)))
                    dve.drain()
                    for b in range(TB):
                        for d in range(2):
                            i = tt(xw[:, b, d, :].rearrange("p (h c) -> p h c", h=HEADS),
                                   xtok[:, b, :].rearrange("p (h c) -> p h c", h=HEADS),
                                   wst[:, 0, b, 8 * d:8 * d + 8].unsqueeze(2).to_broadcast([P, HEADS, HD]), ALU.mult)
                    i.then_inc(*done("xw", l))
                else:
                    tss(nacum[:], ps[7][:, 0:32].rearrange("p (a b) -> p a b", a=2), -1.0, ALU.mult)\
                        .then_inc(*done("acum_sb", (l, s)))
                if not full:
                    return
                b0, b1 = 2 * s, 2 * s + 1

                def take(c):
                    dve.wait_ge(*at("y", (l, s, 2 * c + 1)))
                    y = MIX[:, 4 + c, o:o + T]
                    stt(y, HT[:, c, o:o + T], v(f"d_skip{l}")[:, c:c + 1], ps[4 + c % 2][:, 0:T], ALU.mult, ALU.add)\
                        .then_inc(*done("y_taken", (l, s, c)))
                    dve.drain()
                    return tt(y, y, zs[:, c, o:o + T], ALU.mult)

                dve.wait_ge(*at("scores_sb", (l, s, 1)))
                for h in range(HEADS):
                    p, g = h % 2, h // 4
                    dve.wait_ge(*at("decayed", (l, s, h)))
                    if h >= 2:
                        dve.wait_ge(*at("y", (l, s, h - 2)))
                    stt(mix0[:, p, :], dec_f0[:, p, :], dt[:, b0, h:h + 1], score[:, g, 0, :], ALU.mult, ALU.mult)
                    stt(part0[:, p, :], dec_b0[:, p, :], dt[:, b0, 8 + h:9 + h], score[:, g, 0, 0:P], ALU.mult, ALU.mult)
                    stt(mix1[:, p, :], dec_b1[:, p, :], dt[:, b1, 8 + h:9 + h], score[:, g, 1, :], ALU.mult, ALU.mult)
                    stt(part1[:, p, :], dec_f1[:, p, :], dt[:, b1, h:h + 1], score[:, g, 1, P:T], ALU.mult, ALU.mult)
                    if s == 0:
                        tt(off_f[:, p, :], off_f[:, p, :], HT[:, 6 + g, o:o + T], ALU.mult)
                        tt(off_b[:, p, :], off_b[:, p, :], HT[:, 6 + g, o:o + T], ALU.mult)
                    dve.drain()
                    tt(mix0[:, p, 0:P], mix0[:, p, 0:P], part0[:, p, :], ALU.add)
                    tt(mix1[:, p, P:T], mix1[:, p, P:T], part1[:, p, :], ALU.add).then_inc(*done("mix_sb", (l, s, h)))
                    if h >= 3 and h % 2:
                        take((h - 3) // 2)
                take(3).then_inc(*done("y_stream", (l, s)))

            def mixer_norms(l, tok):
                n = tok.stop
                dve.drain()
                dve.drain().then_inc(*done("y_done", l))
                y = MIX[:, 0:4, tok]
                dve.wait_ge(*at("mean4", ("ln_mean", l)))
                tt(y, y, ps[6][:, 0:n].unsqueeze(1).to_broadcast([P, 4, n]), ALU.subtract).then_inc(*done("centred", l))
                dve.wait_ge(*at("ln_root", l))
                nc.vector.reciprocal(rstd[:, 0:n], rms[:, 0:n]).then_inc(*done("ln_rstd", l))
                dve.drain()
                tt(y, y, rstd[:, 0:n].unsqueeze(1).to_broadcast([P, 4, n]), ALU.mult).then_inc(*done("ln_scaled", l))
                dve.wait_ge(*at("ssd_root", l))
                dve.drain()
                nc.vector.reciprocal(rstd[:, 0:n], rms[:, 0:n])
                dve.drain()
                for c in range(4):
                    y = MIX[:, 4 + c, tok]
                    stt(y, y, v(f"ssd_g{l}")[:, c:c + 1], rstd[:, 0:n], ALU.mult, ALU.mult).then_inc(*done("ssd_out", (l, c)))
                for c in range(KC):
                    dve.wait_ge(*at("mix_high", (l, c)))
                    y = MIX[:, c, tok]
                    tt(r(MIX_r[:, c, tok]), y, HT_r[:, c, tok], ALU.subtract).then_inc(*done("mixed", (l, c)))

            def residual(name, taken, gates=None, streams=1):
                for j in range(KC):
                    dve.wait_ge(*proj_at(name, j))
                    for s in range(streams):
                        x = XT[:, j, s * T:s * T + T]
                        p = ps[taken[j % len(taken)]][:, s * T:s * T + T]
                        i = tt(x, p, x, ALU.add) if gates is None else stt(x, p, gates(j, s), x, ALU.mult, ALU.add)
                    i.then_inc(*done("res_dve", (name, j)))
                    if j % 2:
                        tiles(name, j // 2)

            def first_max(hot, score_, x, mx, n):
                tt(hot, x, mx.to_broadcast([P, n, 4]), ALU.is_equal)
                dve.drain()
                tt(score_, hot, k("first4").unsqueeze(1).to_broadcast([P, n, 4]), ALU.mult)
                dve.drain()
                nc.vector.tensor_reduce(mx, score_, AX.X, ALU.max)
                dve.drain()
                tt(hot, score_, mx.to_broadcast([P, n, 4]), ALU.is_equal)
                dve.drain()

            def router(l, n):
                dve.wait_ge(*at("logits", l))
                lg = rt[:, 0, 0:n, :]
                tt(lg, ps[6][:, 0:20 * n].rearrange("p (a b) -> p a b", a=n),
                   v(f"b_rt{l}").unsqueeze(1).to_broadcast([P, n, 20]), ALU.add)
                dve.drain()
                a = lambda i: rs1[:, i, 0:n, :]
                one = lambda i: rs1[:, 12 + i // 4, 0:n, i % 4:i % 4 + 1]
                mx, gs, e2, wsum, w1, w2, m2 = (one(i) for i in range(7))
                nc.vector.tensor_reduce(mx, lg[:, :, 0:4], AX.X, ALU.max)
                dve.drain()
                tt(rt[:, 1, 0:n, 0:4], lg[:, :, 0:4], mx.to_broadcast([P, n, 4]), ALU.subtract)
                first_max(a(0), a(1), lg[:, :, 0:4], mx, n)
                tt(a(2), lg[:, :, 4:8], a(0)[:, :, 0:1].to_broadcast([P, n, 4]), ALU.mult)
                dve.drain()
                for g in range(1, 4):
                    tt(a(3), lg[:, :, 4 + 4 * g:8 + 4 * g], a(0)[:, :, g:g + 1].to_broadcast([P, n, 4]), ALU.mult)
                    dve.drain()
                    tt(a(2), a(2), a(3), ALU.add)
                    dve.drain()
                nc.vector.tensor_reduce(mx, a(2), AX.X, ALU.max)
                dve.drain()
                tt(rt[:, 1, 0:n, 4:8], a(2), mx.to_broadcast([P, n, 4]), ALU.subtract).then_inc(*done("rt_shift", l))
                first_max(a(4), a(5), a(2), mx, n)
                stt(a(6), a(4), -BIG, a(2), ALU.mult, ALU.add)
                dve.drain()
                nc.vector.tensor_reduce(m2, a(6), AX.X, ALU.max)
                dve.drain()
                first_max(a(7), a(8), a(6), m2, n)
                dve.wait_ge(*at("rt_exp", l))
                nc.vector.tensor_reduce(gs, rt[:, 2, 0:n, 0:4], AX.X, ALU.add)
                tt(a(9), rt[:, 2, 0:n, 4:8], a(4), ALU.mult)
                tt(a(10), rt[:, 2, 0:n, 4:8], a(7), ALU.mult)
                dve.drain()
                nc.vector.tensor_reduce(w1, a(9), AX.X, ALU.add)
                nc.vector.tensor_reduce(w2, a(10), AX.X, ALU.add)
                dve.drain()
                tt(wsum, w1, w2, ALU.add)
                dve.drain()
                tt(wsum, wsum, gs, ALU.mult)
                dve.drain()
                nc.vector.reciprocal(wsum, wsum)
                tt(a(9), a(9), a(10), ALU.add)
                dve.drain()
                tt(a(9), a(9), wsum.to_broadcast([P, n, 4]), ALU.mult)
                dve.drain()
                for g in range(4):
                    i = tt(comb[:, 0:n, 4 * g:4 * g + 4], a(9), a(0)[:, :, g:g + 1].to_broadcast([P, n, 4]), ALU.mult)
                i.then_inc(*done("comb", l))

            def swiglu(name, slices, weighted):
                c0, d0, act0 = SPLIT_AT[name], DOWN_AT[name], base("gate_act", name)
                loop_base("hidden", name, slices)

                def one(j, g):
                    dve.wait_ge(sem("gate_act"), act0 + j + 1 + RING * g)
                    tt(hraw, gact[:, j % 2, :], ps[4 + j % 2][:, T:2 * T], ALU.mult)
                    dve.drain()
                    if weighted:
                        e = j // 2 + RING // 2 * g
                        tt(hraw, hraw, cw[:, e, :], ALU.mult)
                        dve.drain()
                    nc.vector.tensor_copy(r(hid[:, j % 2, 0, :]), hraw)
                    dve.drain()
                    tt(r(hid[:, j % 2, 1, :]), hraw, hid[:, j % 2, 0, :], ALU.subtract).then_inc(sem("hidden"), 1)
                    if c0 + j + 2 < len(SPLIT):
                        make_low(dve, "dve", c0 + j + 2, g)
                    if j + 1 < slices:
                        make_down_low(dve, "dve", d0 + j + 1, g)
                    dve.drain()

                make_down_low(dve, "dve", d0)
                slices_loop(dve, slices, one)

            def add_sum(name, gates=None, stream=0):
                slices = SLICES if gates is not None else FFN_SLICES
                dve.wait_ge(sem("down_free"), DOWN_AT[name] + slices)
                for c in range(KC):
                    x = XT[:, c, stream * T:stream * T + T]
                    p = ps[c // 2][:, (c % 2) * T:(c % 2) * T + T]
                    i = tt(x, p, x, ALU.add) if gates is None else stt(x, p, gates(c), x, ALU.mult, ALU.add)
                    i.then_inc(*done("x_ready", (name, c)))
                dve.drain()

            def fox(i_layer):
                j_fox = i_layer // 3
                tiles(("foxin", i_layer))
                dve.wait_ge(*at("f_raw", i_layer))
                softplus("f", i_layer, ps[7][:, 256:288].rearrange("p (a b) -> p a b", a=TB),
                         v(f"fox_b{j_fox}").unsqueeze(1).to_broadcast([P, TB, 16]),
                         fx[:, 0, :, :], fx[:, 1, :, :], fx[:, 2, :, :], fx[:, 3, :, :], fx[:, 5, :, :], -1.0)
                dve.drain().then_inc(*done("f_sp", i_layer))
                for h in range(FOX_HEADS):
                    p = h % 2
                    L = ps[p]
                    dve.wait_ge(*at("att", (i_layer, h)))
                    nc.vector.reduce_max(stat[:, p, 0, 0:1], L[:, 0:P], AX.X, negate=True)
                    nc.vector.reduce_max(stat[:, p, 0, 1:2], L[:, P:384], AX.X, negate=True)\
                        .then_inc(*done("att_max", (i_layer, h)))
                    dve.wait_ge(*at("prob", (i_layer, h)))
                    nc.vector.reciprocal(stat[:, p, 2, :], stat[:, p, 1, :])
                    dve.drain()
                    tss(prob[:, p, 0:P], prob[:, p, 0:P], stat[:, p, 2, 0:1], ALU.mult)
                    tss(prob[:, p, P:384], prob[:, p, P:384], stat[:, p, 2, 1:2], ALU.mult)\
                        .then_inc(*done("prob_n", (i_layer, h)))
                for c in range(KC):
                    dve.wait_ge(*at("o_high", (i_layer, c)))
                    tt(r(O2r[:, c, :]), O2[:, c, :], H2r[:, c, :], ALU.subtract).then_inc(*done("o_split", (i_layer, c)))
                residual(("foxout", i_layer), [0, 1, 2, 3])

            def s5_rates():
                dve.wait_ge(*at("s5_dt"))
                pv = lambda i: s5p[:, i, :]
                tt(pv(1), v("a_re"), pv(0), ALU.mult)
                tt(pv(2), v("a_im"), pv(0), ALU.mult)
                dve.drain()
                tss(pv(9), pv(2), math.pi / 2, ALU.add)
                dve.drain()
                for src, dst in ((2, 4), (9, 5)):
                    tss(pv(8), pv(src), 1 / (2 * math.pi), ALU.mult)
                    dve.drain()
                    nc.vector.tensor_copy(pv(10).bitcast(I32), pv(8))
                    dve.drain()
                    nc.vector.tensor_copy(pv(8), pv(10).bitcast(I32))
                    dve.drain()
                    stt(pv(dst), pv(8), -6.28125, pv(src), ALU.mult, ALU.add)
                    dve.drain()
                    stt(pv(dst), pv(8), -(2 * math.pi - 6.28125), pv(dst), ALU.mult, ALU.add)
                    dve.drain()
                    ts(pv(dst), pv(dst), 3.1415925, -3.1415925, ALU.min, ALU.max)
                    dve.drain()
                dve.drain().then_inc(*done("s5_ang"))
                dve.wait_ge(*at("s5_trig"))
                lam_re, lam_im = pv(18), pv(19)
                tt(lam_re, pv(3), pv(7), ALU.mult)
                tt(lam_im, pv(3), pv(6), ALU.mult)
                dve.drain()
                tss(pv(11), lam_re, -1.0, ALU.add)
                tt(pv(12), v("a_re"), v("a_re"), ALU.mult)
                tt(pv(13), v("a_im"), v("a_im"), ALU.mult)
                dve.drain()
                tt(pv(12), pv(12), pv(13), ALU.add)
                dve.drain()
                nc.vector.reciprocal(pv(12), pv(12))
                tt(pv(13), pv(11), v("a_re"), ALU.mult)
                tt(pv(14), lam_im, v("a_im"), ALU.mult)
                tt(pv(15), lam_im, v("a_re"), ALU.mult)
                tt(pv(16), pv(11), v("a_im"), ALU.mult)
                dve.drain()
                tt(pv(13), pv(13), pv(14), ALU.add)
                tt(pv(15), pv(15), pv(16), ALU.subtract)
                dve.drain()
                tt(pv(13), pv(13), pv(12), ALU.mult)
                tt(pv(15), pv(15), pv(12), ALU.mult)
            def s5_powers():
                pv = lambda i: s5p[:, i, :]
                nc.vector.tensor_copy(pw[:, 0, 0, :], pv(7))
                nc.vector.tensor_copy(pw[:, 0, 1, :], pv(6))
                dve.drain()
                for n in range(1, S5_LEVELS):
                    tt(pv(16), pw[:, n - 1, 0, :], pw[:, n - 1, 0, :], ALU.mult)
                    tt(pv(17), pw[:, n - 1, 1, :], pw[:, n - 1, 1, :], ALU.mult)
                    stt(pw[:, n, 1, :], pw[:, n - 1, 0, :], 2.0, pw[:, n - 1, 1, :], ALU.mult, ALU.mult)
                    dve.drain()
                    tt(pw[:, n, 0, :], pv(16), pv(17), ALU.subtract)
                    dve.drain()

            def s5():
                pv = lambda i: s5p[:, i, :]
                dve.wait_ge(sem("s5_loaded"), 32)
                tiles(("s5in", 1))
                br, bi = bblk[:, 0, :, :], bblk[:, 1, :, :]
                f_re = pv(13).unsqueeze(2).to_broadcast([P, S5_CH, S5_CH])
                f_im = pv(15).unsqueeze(2).to_broadcast([P, S5_CH, S5_CH])
                tmp = [view(wide, i * 1024, S5_CH, S5_CH) for i in range(4)]
                tt(tmp[0], br, f_re, ALU.mult)
                tt(tmp[1], bi, f_im, ALU.mult)
                tt(tmp[2], br, f_im, ALU.mult)
                tt(tmp[3], bi, f_re, ALU.mult)
                dve.drain()
                tt(br, tmp[0], tmp[1], ALU.subtract)
                tt(bi, tmp[2], tmp[3], ALU.add).then_inc(*done("b_bar"))
                dve.drain()
                tss(cT[:, 1, :, :], cT[:, 1, :, :], -1.0, ALU.mult).then_inc(*done("c_neg"))
                tt(s5_dmat, ident.unsqueeze(1).to_broadcast([P, KC, P]), v("s5_d").unsqueeze(2).to_broadcast([P, KC, P]),
                   ALU.mult).then_inc(*done("s5_dmat"))
                dve.drain().then_inc(sem("s5_out"), 2)
                with dve.Fori(0, S5_CH // BATCH // 2) as g:
                    for j in range(2 * BATCH):
                        if j % BATCH == 0:
                            dve.wait_ge(sem("tables"), j // BATCH + 1 + 2 * g)
                        cos, sin = (table[j // BATCH][:, i, j % BATCH, :] for i in range(2))
                        cos2 = cos.unsqueeze(1).to_broadcast([P, 2, T])
                        dve.wait_ge(sem("bu"), j + 1 + 2 * BATCH * g)
                        bu = ps[j % 2][:].rearrange("p (a t) -> p a t", a=2)
                        tt(s5_a, bu, cos2, ALU.mult)
                        tt(s5_b[:, 0], bu[:, 1], sin, ALU.mult)
                        stt(s5_b[:, 1], bu[:, 0], -1.0, sin, ALU.mult, ALU.mult).then_inc(sem("bu_used"), 1)
                        dve.drain()
                        tt(s5_a, s5_a, s5_b, ALU.add)
                        dve.drain()
                        modulus = s5p[:, 3, bass.ds(j + 2 * BATCH * g, 1)].to_broadcast([P, T])
                        for i in range(2):
                            nc.vector.tensor_tensor_scan(s5_z[:, i], modulus, s5_a[:, i], 0.0, ALU.mult, ALU.add)
                        dve.drain()
                        q = s5_q[:, j % 2]
                        dve.wait_ge(sem("s5_out"), j + 1 + 2 * BATCH * g)
                        tt(q[:, 0], s5_z, cos2, ALU.mult)
                        stt(q[:, 1, 0], s5_z[:, 1], -1.0, sin, ALU.mult, ALU.mult)
                        tt(q[:, 1, 1], s5_z[:, 0], sin, ALU.mult).then_inc(sem("states_done"), 1)
                for c in range(KC):
                    dve.wait_ge(*at("gelu_high", c))
                    tt(r(O2r[:, c, :]), O2[:, c, :], H2r[:, c, :], ALU.subtract).then_inc(*done("gelu_split", c))
                for j in range(KC):
                    dve.wait_ge(*proj_at(("glu", 1), 2 * j))
                    dve.wait_ge(*at("glu_gate", j))
                    g = sig[:, j % 2, 0:T]
                    tt(g, g, ps[4 + (2 * j) % 4][:, 0:T], ALU.mult).then_inc(*done("glu_val", j))
                    dve.drain()
                    tt(XT2[:, j, :], XT2[:, j, :], g, ALU.add).then_inc(*done("res_dve", (("glu", 1), j)))
                    tiles(("glu", 1), j)

            def pooling():
                dve.wait_ge(*at("wide_zero", "pool"))
                dve.wait_ge(sem("counts_loaded"), 16)
                dve.drain()

                for half in range(2):
                    a, b = hpad
                    c0 = 4 * half
                    nc.vector.tensor_copy(a[:, :, 16:], H2[:, c0:c0 + 4, :])
                    dve.drain()
                    n, lo_c = 0, 0
                    for step in range(2 * half + 2):
                        d = 1 << step
                        if step == 2 * half + 1:
                            lo_c = 2
                        src, dst = (a, b) if n % 2 == 0 else (b, a)
                        tt(dst[:, lo_c:4, 16:], src[:, lo_c:4, 16:], src[:, lo_c:4, 16 - d:16 - d + T], ALU.add)
                        n += 1
                        dve.drain()
                        if step == 2 * half or step == 2 * half + 1:
                            g = step
                            res, r0 = dst, (0 if step == 2 * half else 2)
                            o = O2[:, 2 * g:2 * g + 2, :]
                            tt(o, res[:, r0:r0 + 2, 16:], counts[:, g, :].unsqueeze(1).to_broadcast([P, 2, T]), ALU.mult)
                            dve.drain()
                            tt(o, o, H2[:, 2 * g:2 * g + 2, :], ALU.subtract).then_inc(*done("pooled", g))
                for j in range(KC):
                    dve.wait_ge(*at("proj", (("poolw", 2), j)))
                    t = sig[:, j % 2, 0:T]
                    ts(t, ps[j % 4][:, 0:T], v("pool_b")[:, j:j + 1], v("pool_s")[:, j:j + 1], ALU.add, ALU.mult)
                    dve.drain()
                    tt(XT2[:, j, :], XT2[:, j, :], t, ALU.add).then_inc(*done("res_dve", (("poolw", 2), j)))

            s5_rates()
            ada(0)
            for l in range(DEPTH):
                last = l == DEPTH - 1
                streams = 1 if last else 2
                tok = slice(0, streams * T)
                bias = lambda which: lambda c, s: mod[l][:, 24 * which + c, s:s + 1]
                scale(("mix", l), 2, lambda c, s: gsc[l][:, 0, c, s:s + 1], bias(0), SB3)
                gate(l)
                conformer(l)
                sconv(l)
                if not last:
                    ada(l + 1)
                steps(l)
                ssd(l, 1, not last)
                ssd(l, 0, True)
                mixer_norms(l, tok)
                residual(("wout", l), [0, 1, 2, 3], lambda j, s: mod[l][:, 16 + j, s:s + 1], streams)
                dve.drain()
                scale(("ffn", l), streams, lambda c, s: gsc[l][:, 1, c, s:s + 1], bias(1), MIX_r)
                dve.drain()
                router(l, 2 * streams)
                if l == 0:
                    s5_powers()
                for s in range(streams):
                    swiglu(("moe", l, s), SLICES, True)
                    add_sum(("moe", l, s), lambda c: mod[l][:, 40 + c, s:s + 1], s)
            dve.wait_ge(*at("root", ("final1",)))
            nc.vector.reciprocal(rstd[:, 0:T], rms[:, 0:T])
            dve.drain()
            for c in range(KC):
                stt(XT2[:, c, :], XT2[:, c, :], v("g_final")[:, c:c + 1], rstd[:, 0:T], ALU.mult, ALU.mult)\
                    .then_inc(*done("x_ready", ("first", c)))
            dve.drain()
            for i_layer in range(4):
                name = (("fox", 0), ("s5",), ("pool",), ("fox", 3))[i_layer]
                scale(name, 1, lambda c, s: v(f"mix_g{i_layer}")[:, c:c + 1], None, None if i_layer == 2 else H2h)
                if i_layer in (0, 3):
                    fox(i_layer)
                elif i_layer == 1:
                    s5()
                else:
                    pooling()
                dve.drain()
                scale(("ffn2", i_layer), 1, lambda c, s: v(f"ffn_g{i_layer}")[:, c:c + 1], None, H2h)
                swiglu(("ffn", i_layer), FFN_SLICES, False)
                add_sum(("ffn", i_layer))
            scale(("final2",), 1, lambda c, s: v("fin_g")[:, c:c + 1])
            dve.drain().then_inc(*done("x_ready", "end"))

    return seen


def win_taken(l, j):
    ch = W_IN_ORDER[j]
    return ("gated", (l, ch)) if ch < 4 else ("win_act", (l, j))


def lay_out(a):
    def cols(w, idx=None):
        w = w if idx is None else w[:, idx]
        return w.reshape(KC, P, -1).transpose(1, 0, 2).reshape(P, -1)

    def chunks(ids):
        return np.concatenate([np.arange(P) + P * i for i in ids])

    def feat(x):
        return x.reshape(-1, P).T

    def rep(x):
        return np.broadcast_to(x.reshape(1, -1), (P, x.size))

    def slices(w, n):
        return [cols(w[:, TCOLS * i:TCOLS * i + TCOLS]) for i in range(n)]

    def gate_up(g, u, j):
        return cols(np.concatenate([g[:, P * j:P * j + P], u[:, P * j:P * j + P]], 1))

    d = {}
    halves = EXPERT_FF // P
    d["ada"] = np.stack([t for l in range(DEPTH) for t in slices(a["w_ada"][l], ADA_TILES)])
    d["win"] = np.stack([t for l in range(DEPTH) for t in slices(a["w_in"][l][:, chunks(W_IN_ORDER)], WIN_TILES)])
    d["wout"] = np.stack([t for l in range(DEPTH) for t in slices(a["w_out"][l], HALF_D)])
    d["moe"] = np.stack([gate_up(a["w_gate"][l, e], a["w_up"][l, e], j)
                         for l in range(DEPTH) for e in range(EXPERTS) for j in range(halves)])
    d["moe_down"] = a["w_down"].reshape(-1, P, D)
    qkv = np.concatenate([np.arange(D) + 2 * D, np.arange(2 * D)])
    d["foxin"] = np.stack([t for j in range(2) for t in slices(a["fox_w_in_2"][j][:, qkv], 3 * HALF_D)])
    d["foxout"] = np.stack([t for j in range(2) for t in slices(a["fox_w_out_2"][j], HALF_D)])
    d["s5in"] = np.stack(slices(a["s5_w_in_2"][0], HALF_D))
    pairs = chunks([i for j in range(KC) for i in (j, KC + j)])
    d["glu"] = np.stack(slices(a["s5_w_glu_2"][0][:, pairs], 2 * HALF_D))
    d["poolw"] = a["pool_w_2"][0].reshape(POOLS, 2, P, 2 * P).transpose(2, 0, 1, 3).reshape(1, P, -1)
    f = FFN_SLICES * FF
    d["ffn"] = np.stack([gate_up(a["ffn_w_gate_up_2"][i][:, :f], a["ffn_w_gate_up_2"][i][:, f:], j)
                         for i in range(4) for j in range(FFN_SLICES)])
    d["ffn_down"] = a["ffn_w_down_2"].reshape(-1, P, D)

    def by_state(re, im):
        o = np.zeros((P, 2, S5_CH, 2, 16), np.float32)
        for r, m in enumerate((re, im)):
            x = m.reshape(S5_CH, 2, 64, 16)
            for g in range(2):
                o[64 * g:64 * g + 64, r, :, g, :] = x[:, g].transpose(1, 0, 2)
        return o.reshape(P, -1)

    d["s5_b"] = by_state(a["s5_b_re_2"][0], a["s5_b_im_2"][0])
    d["s5_c"] = by_state(a["s5_c_re_2"][0].transpose(0, 2, 1), a["s5_c_im_2"][0].transpose(0, 2, 1))

    vec = {"c2": np.stack([feat(a["c"][0]), feat(a["c_ctx"])], 2)}
    two = lambda x: np.stack([feat(x), feat(x)], 2)
    state = lambda x: x.reshape(S5_CH, P).T
    for l in range(DEPTH):
        vec[f"b_ada{l}"] = two(a["b_ada"][l])
        vec[f"g_mix{l}"], vec[f"g_ffn{l}"] = two(a["g_mix"][l]), two(a["g_ffn"][l])
        vec[f"conv_w{l}"] = a["conv_w"][l].T.reshape(4, P, TAPS).transpose(1, 0, 2)
        vec[f"conv_b{l}"], vec[f"ln_g{l}"] = feat(a["conv_b"][l]), feat(a["conv_ln_g"][l])
        vec[f"ln_b{l}"], vec[f"ssd_g{l}"] = feat(a["conv_ln_b"][l]), feat(a["ssd_norm_g"][l])
        vec[f"d_skip{l}"] = feat(np.repeat(a["d_skip"][l], HD))
        vec[f"sconv_w{l}"] = a["ssd_conv_w"][l].T.reshape(8, P, STAPS).transpose(1, 0, 2)
        vec[f"sconv_b{l}"] = feat(a["ssd_conv_b"][l])
        vec[f"dt_bias{l}"], vec[f"a_log{l}"] = rep(a["dt_bias"][l]), rep(a["a_log"][l])
        vec[f"fox_b{l}"] = rep(a["fox_b_f_2"][l])
        vec[f"b_rt{l}"] = rep(np.concatenate([a["b_router_group"][l], a["b_router_expert"][l]]))
        vec[f"w_rt{l}"] = cols(np.concatenate([a["w_router_group"][l], a["w_router_expert"][l]], 1))
        vec[f"w_dt{l}"] = cols(a["w_in"][l][:, 2560:])
        vec[f"w_f{l}"] = cols(a["fox_w_in_2"][l][:, 3 * D:])
    for i in range(4):
        vec[f"mix_g{i}"], vec[f"ffn_g{i}"] = feat(a["mix_norm_g_2"][i]), feat(a["ffn_norm_g_2"][i])
    vec["g_final"], vec["fin_g"], vec["s5_d"] = feat(a["g_final"]), feat(a["final_norm_g_2"]), feat(a["s5_d_2"][0])
    vec["pool_b"], vec["pool_s"] = feat(a["pool_b_2"][0]), feat(a["pool_scale_2"][0])
    vec["a_re"], vec["a_im"] = state(a["s5_a_re_2"][0]), state(a["s5_a_im_2"][0])
    vec["log_dt"] = state(np.repeat(a["s5_log_dt_2"][0], 64))
    d["vec"] = np.concatenate([vec[n].reshape(P, -1) for n, _ in VEC_SHAPES], 1)
    xt = np.concatenate([a["x"][0], a["ctx"][0]], 0)
    d["xt"] = xt.T.reshape(KC, P, 2 * T).transpose(1, 0, 2).reshape(P, -1)
    d["con"], d["msk"], pool = const_arrays()
    d["pool_counts"] = pool.reshape(P, -1)
    return {n: np.ascontiguousarray(x) for n, x in d.items()}


def shaped(dram):
    r = dict(dram)
    r["xt"] = dram["xt"].rearrange("p (a b) -> p a b", a=KC)
    for n in ("s5_b", "s5_c"):
        r[n] = dram[n].rearrange("p (a b c) -> p a b c", a=2, b=S5_CH)
    r["pool_counts"] = dram["pool_counts"].rearrange("p (a b) -> p a b", a=POOLS)
    return r


def declare(nc, arrays):
    dram = {n: nc.dram_tensor(f"in_{n}", x.shape, mybir.dt.from_np(x.dtype), kind="ExternalInput").ap()
            for n, x in arrays.items()}
    return shaped(dram), nc.dram_tensor("out_0", (P, KC * T), F32, kind="ExternalOutput").ap()


def kernel(**inputs):
    import concourse.bacc as _bacc
    from concourse.bass_utils import run_bass_kernel_spmd as _run

    arrays = lay_out({n: np.asarray(x) for n, x in inputs.items()})
    counting = _bacc.Bacc("TRN2", target_bir_lowering=False, num_devices=1)
    known = program(counting, *declare(counting, arrays), {})
    nc = _bacc.Bacc("TRN2", target_bir_lowering=False, num_devices=1)
    program(nc, *declare(nc, arrays), known)
    r = _run(nc, [{f"in_{n}": x for n, x in arrays.items()}], core_ids=[0])
    o = np.asarray(r.results[0]["out_0"]).reshape(P, KC, T)
    return o.transpose(2, 1, 0).reshape(1, T, D)
```

```python
import math
from contextlib import ExitStack

import numpy as np

import concourse.bass as bass
import concourse.mybir as mybir

ALU = mybir.AluOpType
ACT = mybir.ActivationFunctionType
AX = mybir.AxisListType
F32 = mybir.dt.float32
BF16 = mybir.dt.bfloat16
F32R = mybir.dt.float32r
I32 = mybir.dt.int32

P = 128
D = 1024
KC = D // P
T = 256
TB = T // P
GRID_W = 64
ROWS = T // GRID_W
DEPTH = 2
TAPS = 31
HALF = TAPS // 2
STAPS = 5
HEADS = 8
HD = 64
EXPERTS = 16
FF = P
EXPERT_FF = 256
SLICES = EXPERTS * EXPERT_FF // FF
PER_BLOCK = EXPERT_FF // FF
OVER = 8
OVER_SLICES = OVER * PER_BLOCK
FFN_SLICES = 2816 // FF
FOX_HEADS = 16
S5_CH = 32
S5_LEVELS = 8
BATCH = 4
POOLS = 4
RING = 4
QUAD = 32
HIGH = 2
TCOLS = 2 * P
TILE = KC * TCOLS
BIG = 1.0e30

W_IN_ORDER = [0, 4, 1, 5, 2, 6, 3, 7, 12, 13, 14, 15, 16, 17, 18, 19, 8, 9, 10, 11]

VEC_SHAPES = (
    [("c2", (KC, 2))]
    + [(f"b_ada{l}", (48, 2)) for l in range(DEPTH)]
    + [(f"{n}{l}", (KC, 2)) for l in range(DEPTH) for n in ("g_mix", "g_ffn")]
    + [(f"conv_w{l}", (4, TAPS)) for l in range(DEPTH)]
    + [(f"{n}{l}", (4,)) for l in range(DEPTH) for n in ("conv_b", "ln_g", "ln_b", "d_skip", "ssd_g")]
    + [(f"sconv_w{l}", (8, STAPS)) for l in range(DEPTH)]
    + [(f"sconv_b{l}", (8,)) for l in range(DEPTH)]
    + [(f"{n}{l}", (16,)) for l in range(DEPTH) for n in ("dt_bias", "a_log", "fox_b")]
    + [(f"b_rt{l}", (20,)) for l in range(DEPTH)]
    + [(f"{n}{i}", (KC,)) for i in range(4) for n in ("mix_g", "ffn_g")]
    + [(n, (KC,)) for n in ("g_final", "fin_g", "s5_d", "pool_b", "pool_s")]
    + [(n, (S5_CH,)) for n in ("a_re", "a_im", "log_dt")]
)
VEC_AT = {}
_at = 0
for _n, _s in VEC_SHAPES:
    VEC_AT[_n] = (_at, _s)
    _at += int(np.prod(_s))
NVEC = _at

CONSTS = ([("ident", (P,)), ("tri", (3, P)), ("mean1024", (P,)), ("mean512", (P,)),
           ("first4", (4,)), ("first_row", (EXPERTS,)), ("over_row", (EXPERTS,)), ("expert_id", (EXPERTS,)),
           ("block_id", (OVER,)), ("partial", (2,)), ("eps6", (1,)), ("eps5", (1,)), ("halfpi", (1,))])
CON_AT = {}
_at = 0
for _n, _s in CONSTS:
    CON_AT[_n] = (_at, _s)
    _at += int(np.prod(_s))
NCON = _at


def const_arrays():
    i = np.arange(P)
    up = (i[:, None] <= i[None, :]).astype(np.float32)
    lo = (i[:, None] >= i[None, :]).astype(np.float32)
    one = np.ones((P, P), np.float32)
    c = {
        "ident": np.eye(P, dtype=np.float32),
        "tri": np.concatenate([up, one, lo], 1),
        "mean1024": one / D, "mean512": one / (D // 2),
        "first_row": np.broadcast_to(np.arange(EXPERTS, dtype=np.float32) * P - 1, (P, EXPERTS)),
        "over_row": np.broadcast_to((EXPERTS - 1 - np.arange(EXPERTS, dtype=np.float32)) * P, (P, EXPERTS)),
        "expert_id": np.broadcast_to(np.arange(EXPERTS, dtype=np.float32), (P, EXPERTS)),
        "block_id": np.broadcast_to(np.arange(OVER, dtype=np.float32), (P, OVER)),
        "partial": (i[:, None] % QUAD == np.arange(2)[None, :]).astype(np.float32),
        "first4": np.broadcast_to(np.arange(4, 0, -1, dtype=np.float32), (P, 4)),
        "eps6": np.full((P, 1), 1e-6, np.float32), "eps5": np.full((P, 1), 1e-5, np.float32),
        "halfpi": np.full((P, 1), math.pi / 2, np.float32),
    }
    con = np.concatenate([c[n].reshape(P, -1) for n, _ in CONSTS], 1).astype(np.float32)
    masks = np.concatenate([np.eye(P), (up - 1) * BIG, (lo - 1) * BIG, np.zeros((P, 512))], 1)
    counts = np.stack([1.0 / np.minimum(np.arange(1, T + 1), 2 << g) for g in range(POOLS)])
    pool = np.broadcast_to(counts.astype(np.float32)[None], (P, POOLS, T))
    return con, masks.astype(mybir.dt.np(BF16)), np.ascontiguousarray(pool)


ADA_TILES = 6 * D // TCOLS
ADA_FIRST = 2 * D // TCOLS
ADA_PARTS = (range(ADA_FIRST), range(ADA_FIRST, 3 * ADA_TILES // 2), range(3 * ADA_TILES // 2, 2 * ADA_TILES))
WIN_TILES = len(W_IN_ORDER) // 2 + 1
ROUTES = 4 + EXPERTS
LONE = {"win": len(W_IN_ORDER), "rt": 0, "foxf": 0}
HALF_D = D // TCOLS
RAW = ("ada", "poolw")
WITH_DVE = ("rt", "moe", "over", "ffn", "foxin", "foxf", "foxout", "s5in", "glu")


def tile_plan():
    plan = [(("ada", 0), len(ADA_PARTS[0]), 0)]
    for l in range(DEPTH):
        plan += [(("win", l), WIN_TILES, WIN_TILES * l)]
        plan += [(("ada", l + 1), len(ADA_PARTS[l + 1]), ADA_PARTS[l + 1][0])]
        plan += [(("wout", l), HALF_D, HALF_D * l), (("rt", l), 1, l)]
        plan += [(("moe", l), SLICES, SLICES * l), (("over", l), OVER_SLICES, SLICES * l)]
    for i in range(4):
        if i in (0, 3):
            plan += [(("foxf", i), 1, i // 3), (("foxin", i), 3 * HALF_D, 3 * HALF_D * (i // 3)), (("foxout", i), HALF_D, HALF_D * (i // 3))]
        elif i == 1:
            plan += [(("s5in", i), HALF_D, 0), (("glu", i), 2 * HALF_D, 0)]
        else:
            plan += [(("poolw", i), 1, 0)]
        plan += [(("ffn", i), FFN_SLICES, FFN_SLICES * i)]
    return plan


PLAN = tile_plan()
TILE_AT, SPLIT_AT, DOWN_AT = {}, {}, {}
SPLIT, SHARED, DOWNS = [], [], 0
_at = 0
for _n, _k, _ in PLAN:
    TILE_AT[_n], SPLIT_AT[_n] = _at, len(SPLIT)
    for _i in range(_k):
        if _n[0] not in RAW:
            SPLIT.append(_at + _i)
            SHARED.append((SHARED[-1] if SHARED else 0) + (_n[0] in WITH_DVE))
    if _n[0] in ("moe", "over", "ffn"):
        DOWN_AT[_n] = DOWNS
        DOWNS += _k
    _at += _k


def shared(c):
    return SHARED[c] > (SHARED[c - 1] if c else 0)


def program(nc, dram, out, known):
    ctx = ExitStack()
    seen, count, sems = {}, {}, {}

    def sem(name):
        if name not in sems:
            sems[name] = ctx.enter_context(nc.semaphore(name))
            count[name] = 0
        return sems[name]

    def done(name, key=None, by=1):
        s = sem(name)
        count[name] += by
        seen[name, key] = count[name]
        return s, by

    def at(name, key=None):
        return sem(name), known.get((name, key), 1)

    def loop_base(name, key, total):
        sem(name)
        seen[name, key] = count[name]
        count[name] += total
        return seen[name, key]

    def base(name, key):
        sem(name)
        return known.get((name, key), 0)

    with ctx:
        def sb(name, shape, dt=F32):
            return ctx.enter_context(nc.sbuf_tensor(name, [P] + list(shape), dt))

        def shared_sb(name, shape):
            with nc.sbuf_tensor(name + "_halves", [P] + list(shape), F32) as halves:
                pass
            return sb(name, shape), halves

        ring, ring_r = zip(*(shared_sb(f"ring{i}", [TILE]) for i in range(RING)))
        high = [sb(f"high{i}", [TILE]) for i in range(HIGH)]
        dring, dring_r = zip(*(shared_sb(f"dring{i}", [D]) for i in range(RING)))
        dhigh = [sb(f"dhigh{i}", [D]) for i in range(HIGH)]
        vec = sb("vec", [NVEC])
        con = sb("con", [NCON])
        msk = sb("msk", [3 * P + 512], BF16)
        XT = sb("XT", [KC, 2 * T])
        HT, HT_r = shared_sb("HT", [KC, 2 * T])
        MIX, MIX_r = shared_sb("MIX", [KC, 2 * T])
        wide = sb("wide", [4160])
        border, border_r = shared_sb("border", [3176])
        zs_b = sb("zs_b", [4 * 2 * T])
        ssdb, ssdb_r = shared_sb("ssdb", [KC * 2 * T])
        sig = sb("sig", [2, 2 * T])
        rms = sb("rms", [2 * T])
        rstd = sb("rstd", [2 * T])
        mod = [sb(f"mod{l}", [48, 2]) for l in range(DEPTH)]
        gsc = [sb(f"gsc{l}", [2, KC, 2]) for l in range(DEPTH)]
        sc2 = sb("sc2", [KC, QUAD])
        arow = sb("arow", [4, TCOLS])
        dts = sb("dts", [6, 4, 16])
        dar = sb("dar", [2, 4, 16])
        splr = sb("splr", [2, TB, 16])
        tri_r = sb("tri_r", [6 * P])
        aneg = sb("aneg", [2, 16])
        nacum = sb("nacum", [TB, 16])
        wst = sb("wst", [2, TB, 16])
        rt = sb("rt", [4, 4, 20])
        rs1 = sb("rs1", [16, 4, 4])
        s5p = sb("s5p", [20, S5_CH])

        ps = [ctx.enter_context(nc.psum_tensor(f"bank{b}", [P, 512], F32)) for b in range(8)]

        def v(name):
            o, s = VEC_AT[name]
            x = vec[:, o:o + int(np.prod(s))]
            return x if len(s) == 1 else x.rearrange("p (a b) -> p a b", a=s[0])

        def k(name):
            o, s = CON_AT[name]
            return con[:, o:o + int(np.prod(s))]

        up, one, lo = (k("tri")[:, i * P:i * P + P] for i in range(3))
        fw, bw = tri_r[:, 0:4 * P], tri_r[:, 2 * P:]
        identb, mask_f, mask_b, zeros = msk[:, 0:P], msk[:, P:2 * P], msk[:, 2 * P:3 * P], msk[:, 3 * P:]
        ident = k("ident")

        def view(buf, off, *shape):
            x = buf[:, off:off + int(np.prod(shape))]
            names = "abcd"[:len(shape)]
            if len(shape) == 1:
                return x
            return x.rearrange(f"p ({' '.join(names)}) -> p {' '.join(names)}",
                               **dict(zip(names[:-1], shape[:-1])))

        sq = view(wide, 0, KC, 2 * T)
        xbc = view(wide, 0, KC, 2, T + STAPS - 1)
        vrow = view(border, 0, 2, ROWS, GRID_W + 2 * HALF)
        vcol = view(border, 752, 2, ROWS + 6, GRID_W)
        vseq = view(border, 752 + 1280, 4, T + 2 * HALF)
        zs = view(zs_b, 0, 4, 2 * T)
        xw = view(border, 0, TB, 2, 512)
        dec_f0, dec_f1 = view(wide, 0, 2, T), view(wide, 512, 2, P)
        dec_b1, dec_b0 = view(wide, 768, 2, T), view(wide, 1280, 2, P)
        off_f, off_b = view(wide, 1536, 2, T), view(wide, 2048, 2, T)
        mix0, mix1 = view(wide, 2560, 2, T), view(wide, 3072, 2, T)
        part0, part1 = view(wide, 3584, 2, P), view(wide, 3840, 2, P)
        htok = view(wide, 0, 2 * TB, D)
        ytok = lambda b, i: view(wide if b < TB else MIX[:].rearrange("p a b -> p (a b)"), (b % TB * 2 + i) * D, D)
        xrows, yrows = view(zs_b, 0, 2, D), view(ssdb, 0, 2, D)
        xT = HT_r[:].rearrange("p a b -> p (a b)").rearrange("p (q h c t) -> p q h c t", q=2, h=2, c=KC)
        hrows = view(border, 1536, 2, P)
        sigf = sig[:].rearrange("p a b -> p (a b)")
        pick, picked, row = view(sigf, 0, 2, 4, EXPERTS), view(sigf, 128, 4, EXPERTS), view(sigf, 192, 4, EXPERTS)
        past, extra, prod = view(sigf, 256, 4, EXPERTS), view(sigf, 320, 4, EXPERTS), view(sigf, 384, 2, 4, EXPERTS)
        slot_f, weight = view(sigf, 512, 2, 4), view(sigf, 520, 2, 4)
        in_block, below = view(sigf, 528, OVER, EXPERTS), view(sigf, 656, OVER, EXPERTS)
        over_f = view(sigf, 784, OVER)
        slot, over_expert = view(sigf, 792, 2, 4).bitcast(I32), view(sigf, 800, OVER).bitcast(I32)
        overflow = view(sigf, 808, 1).bitcast(I32)
        x_slots = nc.dram_tensor("x_slots", ((EXPERTS + OVER) * P, D), F32, kind="Internal").ap()
        y_slots = nc.dram_tensor("y_slots", ((EXPERTS + OVER) * P, D), F32, kind="Internal").ap()
        hid = view(border_r, 0, 2, 2, T)
        gact = view(border, 1024, 2, T)
        hraw = view(border, 1536, T)
        xtok, btok = view(ssdb, 0, TB, 512), view(ssdb, 1024, TB, 2, P)
        score, h0 = view(ssdb, 1536, 2, TB, T), view(ssdb, 2560, 2, 2, T)
        narrow_sb = rms
        SB3 = view(ssdb_r, 0, KC, 2 * T)
        r = lambda x: x.bitcast(F32R)

        XT2 = XT[:, :, 0:T]
        H2r, O2r = (x[:].rearrange("p a b -> p (a b)")[:, 0:KC * T].rearrange("p (a b) -> p a b", a=KC)
                    for x in (HT_r, MIX_r))
        HTf, MIXf = HT[:].rearrange("p a b -> p (a b)"), MIX[:].rearrange("p a b -> p (a b)")
        H2, Q2 = view(HTf, 0, KC, T), view(HTf, KC * T, KC, T)
        H2h = view(ssdb_r, 0, KC, T)
        O2, K2 = view(MIXf, 0, KC, T), view(MIXf, KC * T, KC, T)
        vtok = view(zs_b, 0, TB, D)
        prob = view(wide, 0, 2, 384)
        probT = view(wide, 768, 2, 384)
        fx = view(wide, 1536, 6, TB, 16)
        stat = view(wide, 1536 + 192, 2, 4, 2)
        bT = view(MIXf, KC * T, 2, KC, P)
        cT = view(zs_b, 0, 2, S5_CH, S5_CH)
        bblk = view(MIXf, 0, 2, S5_CH, S5_CH)
        pw = view(arow[:].rearrange("p a b -> p (a b)"), 0, S5_LEVELS, 2, S5_CH)
        table = [XT[:, :, T:2 * T].rearrange("p (a b) t -> p a b t", a=2), view(ssdb, KC * T, 2, BATCH, T)]
        table_tmp = sig[:].rearrange("p a (b t) -> p a b t", b=BATCH)
        s5_a, s5_b, s5_z = (view(wide, i * 2 * T, 2, T) for i in range(3))
        s5_q = view(wide, 3 * 2 * T, 2, 2, 2, T)
        s5_dmat = view(dring[0], 0, KC, P)
        hpad = [view(wide, i * 4 * (16 + T), 4, 16 + T) for i in range(2)]
        counts = view(border, 0, POOLS, T)

        def proj_at(name, j):
            return at("proj", (name, j)) if j % 2 == 0 and LONE.get(name[0]) != j else (sem("tile_free"), TILE_AT[name] + j // 2 + 1)

        block = ctx.enter_context(nc.Block())

        def sum_at(c, stream=0):
            return ps[c // 2 if stream == 0 else 7 - c // 2], (c % 2) * T

        def low_ready(c, g=0):
            if shared(c):
                nc.tensor.wait_ge(sem("low_dve"), SHARED[c] + RING * g)
            nc.tensor.wait_ge(sem("low_pool"), c + 1 + RING * g)
            return r(high[c % HIGH][:]), r(ring_r[SPLIT[c] % RING][:])

        def make_low(eng, engine, c, g=0):
            if engine == "dve" and not shared(c):
                return
            cut = TILE // 2 if shared(c) else 0
            at_ = slice(0, cut) if engine == "dve" else slice(cut, TILE)
            w, h = ring[SPLIT[c] % RING][:, at_], high[c % HIGH][:, at_]
            eng.wait_ge(sem("high"), c + 1 + RING * g)
            low = r(ring_r[SPLIT[c] % RING][:, at_])
            eng.tensor_tensor(low, w, h, ALU.subtract).then_inc(sem(f"low_{engine}"), 1)

        def make_down_low(eng, engine, d, g=0):
            at_ = slice(0, D // 2) if engine == "dve" else slice(D // 2, D)
            w, h = dring[d % RING][:, at_], dhigh[d % HIGH][:, at_]
            eng.wait_ge(sem("down_high"), d + 1 + RING * g)
            low = r(dring_r[d % RING][:, at_])
            eng.tensor_tensor(low, w, h, ALU.subtract).then_inc(sem(f"down_low_{engine}"), 1)

        def slices_loop(eng, slices, one, apart=0):
            turns = (slices - 1) // RING
            for j in range(apart * RING):
                one(j, 0)
            with eng.Fori(apart, turns) as g:
                for j in range(RING):
                    one(j, g)
            for j in range(turns * RING, slices):
                one(j, 0)

        def rows_loaded(name, b):
            return sem(f"x_loaded{b % 2}_{name[0]}{name[1]}")

        def if_overflow(eng, l, run, else_):
            eng.wait_ge(*at("overflow", l))
            blocks_ = eng.value_load(overflow[0:1, 0:1], min_val=0, max_val=OVER)
            with eng.If(blocks_ > 0):
                run()
            with eng.Else():
                else_()

        @block.sync
        def _(sp):
            def load(t, src, g=0):
                if t >= RING:
                    sp.wait_ge(sem("tile_free"), t - RING + 1 + RING * g)
                sp.dma_start(ring[t % RING][:], src).then_inc(sem(f"tile_loaded{t % RING}"), 16)

            def load_down(d, src, g=0):
                if d >= RING:
                    sp.wait_ge(sem("down_free"), d - RING + 1 + RING * g)
                sp.dma_start(dring[d % RING][:], src).then_inc(sem(f"down_loaded{d % RING}"), 16)

            def over(name, first):
                t0, d0, l = TILE_AT[name], DOWN_AT[name], name[1]

                def run():
                    for b in range(OVER):
                        e = sp.value_load(over_expert[0:1, b:b + 1], min_val=0, max_val=EXPERTS - 1)
                        for i in range(PER_BLOCK):
                            j = PER_BLOCK * b + i
                            load(t0 + j, dram["moe"][bass.ds(first + i + PER_BLOCK * e, 1)].rearrange("a p c -> p (a c)"))
                            load_down(d0 + j, dram["moe_down"][bass.ds(first + i + PER_BLOCK * e, 1)].rearrange("a p c -> p (a c)"))

                def skip():
                    for i in range(RING):
                        sp.wait_ge(sem(f"tile_loaded{i}"), 16 * ((t0 - i + RING - 1) // RING))
                        sp.sem_inc(sem(f"tile_loaded{i}"), 16 * OVER_SLICES // RING)
                        sp.wait_ge(sem(f"down_loaded{i}"), 16 * ((d0 - i + RING - 1) // RING))
                        sp.sem_inc(sem(f"down_loaded{i}"), 16 * OVER_SLICES // RING)

                if_overflow(sp, l, run, skip)

            for name, n, first in PLAN:
                if name[0] == "over":
                    over(name, first)
                    b = (2 if name[1] == 0 else 1) * TB - 1
                    sp.wait_ge(*at(f"y_tok{b}", (name[1], b, 1)))
                    continue
                if name == ("rt", 0):
                    sp.wait_ge(sem("vec_loaded"), 32)
                    none = zeros.bitcast(F32).unsqueeze(1).to_broadcast([P, 4, D // 4])
                    for slots_, b0 in ((x_slots, 0), (y_slots, EXPERTS)):
                        rows = slots_.rearrange("(b p) (q c) -> p b q c", p=P, q=4)
                        for b in range(b0, EXPERTS + OVER):
                            sp.dma_start(rows[:, b], none).then_inc(sem("slots_cleared"), 16)
                t0, src = TILE_AT[name], dram[name[0]]
                if name in DOWN_AT:
                    downs = dram[name[0] + "_down"]
                    d0 = DOWN_AT[name]
                    if t0 + 0 < RING or d0 < RING:
                        for j in range(RING):
                            load(t0 + j, src[first + j])
                            load_down(d0 + j, downs[first + j])
                        start = 1
                    else:
                        start = 0
                    with sp.Fori(start, n // RING) as g:
                        for j in range(RING):
                            load(t0 + j, src[first + j + RING * g], g)
                            load_down(d0 + j + (RING if start else 0), downs[first + j + RING * g], g - start)
                    for j in range(n // RING * RING, n):
                        load(t0 + j, src[first + j])
                        load_down(d0 + j, downs[first + j])
                else:
                    for j in range(n):
                        load(t0 + j, src[first + j])
            sp.wait_ge(*at("x_ready", "end"))
            sp.dma_start(out.rearrange("p (a b) -> p a b", a=KC), H2).then_inc(sem("stored"), 16)
            sp.wait_ge(sem("stored"), 16)

        @block.gpsimd
        def _(pool):
            def tiles(name, before=None, late=None):
                n = dict((a, b) for a, b, _ in PLAN)[name]
                for a in range(n):
                    if before is not None and a == 0:
                        before()
                    if late is not None and a == n - 2:
                        late()
                    make_low(pool, "pool", SPLIT_AT[name] + a + 2)

            def during_ssd(l):
                if l < DEPTH - 1:
                    ln_scale(l)
                c_decayed(l)

            def ln_scale(l):
                y = MIX[:, 0:4, :]
                pool.wait_ge(*at("ln_rstd", l))
                nc.gpsimd.tensor_tensor(y, y, rstd[:].unsqueeze(1).to_broadcast([P, 4, 2 * T]), ALU.mult)\
                    .then_inc(*done("ln_scaled", l))

            def swiglu(name, slices):
                c0, d0 = SPLIT_AT[name], DOWN_AT[name]

                def one(j, g):
                    if c0 + j + 2 < len(SPLIT):
                        make_low(pool, "pool", c0 + j + 2, g)
                    if j + 1 < slices:
                        make_down_low(pool, "pool", d0 + j + 1, g)

                make_down_low(pool, "pool", d0)
                slices_loop(pool, slices, one)

            def c_decayed(l):
                for h in range(HEADS):
                    p, g = h % 2, h // 4
                    pool.wait_ge(*at("decayed", (l, 0, h)))
                    nc.gpsimd.tensor_tensor(off_f[:, p, :], off_f[:, p, :], HT[:, 6 + g, 0:T], ALU.mult)
                    nc.gpsimd.tensor_tensor(off_b[:, p, :], off_b[:, p, :], HT[:, 6 + g, 0:T], ALU.mult)\
                        .then_inc(*done("c_decayed", (l, h)))

            def scatter(l, blocks):
                pool.wait_ge(sem("slots_cleared"), 16 * (EXPERTS + 2 * OVER))
                pool.wait_ge(*at("slots", l))
                for b in range(blocks):
                    pool.wait_ge(*at("h_tok", (l, b)))
                    for i in range(2):
                        pool.indirect_dma_start(x_slots, bass.IndirectOffsetOnAxis(slot[:, i, b:b + 1], 0), htok[:, b, :], None)\
                            .then_inc(*done("x_scattered", (l, b, i), 16))
                pool.wait_ge(*at("x_scattered", (l, blocks - 1, 1)))

            def experts(name, blocks, row0):
                c0, d0, slices, turned0 = SPLIT_AT[name], DOWN_AT[name], PER_BLOCK * blocks, base("x_turned", name)
                def rows(b, g):
                    src = x_slots[bass.ds(row0 + P * b + 2 * P * g, P)] if not isinstance(g, int) else \
                        x_slots[row0 + P * b:row0 + P * b + P]
                    pool.dma_start(xrows[:, b % 2, :], src).then_inc(rows_loaded(name, b), 16)

                def one(j, g):
                    if j % 2 == 0 and j // 2 + 2 < blocks:
                        pool.wait_ge(sem("x_turned"), turned0 + j // 2 + 1 + RING // 2 * g)
                        rows(j // 2 + 2, g)
                    if j + 2 < slices:
                        make_low(pool, "pool", c0 + j + 2, g)
                    if j + 1 < slices:
                        make_down_low(pool, "pool", d0 + j + 1, g)

                if turned0:
                    pool.wait_ge(sem("x_turned"), turned0)
                for b in range(2):
                    rows(b, 0)
                if name[0] == "over":
                    for a in range(2):
                        make_low(pool, "pool", c0 + a)
                make_down_low(pool, "pool", d0)
                slices_loop(pool, slices, one)

            def moe(l, blocks):
                scatter(l, blocks)
                experts(("moe", l), EXPERTS, 0)
                name = ("over", l)

                def skip():
                    pool.drain()
                    pool.sem_inc(sem("low_pool"), OVER_SLICES)
                    pool.sem_inc(sem("down_low_pool"), OVER_SLICES)

                if_overflow(pool, l, lambda: experts(name, OVER, EXPERTS * P), skip)
                for p in range(2):
                    pool.wait_ge(sem(f"y_stored{p}"), base(f"y_stored{p}", name) + 16 * OVER // 2)
                for b in range(blocks):
                    for i in range(2):
                        pool.indirect_dma_start(ytok(b, i), None, y_slots, bass.IndirectOffsetOnAxis(slot[:, i, b:b + 1], 0))\
                            .then_inc(*done(f"y_tok{b}", (l, b, i), 16))
                for a in range(2):
                    make_low(pool, "pool", SPLIT_AT[name] + OVER_SLICES + a)

            def rotations(b, batch):
                tab = table[b]
                ptt = nc.gpsimd.tensor_tensor
                for n in range(S5_LEVELS):
                    d = 1 << n
                    low, new = tab[:, :, :, 0:d], tab[:, :, :, d:2 * d]
                    cos, sin = (pw[:, n, i, bass.ds(BATCH * batch, BATCH)].unsqueeze(1).unsqueeze(3)
                                .to_broadcast([P, 2, BATCH, d]) for i in range(2))
                    tmp = table_tmp[:, :, :, 0:d]
                    ptt(new, low, cos, ALU.mult)
                    ptt(tmp, low, sin, ALU.mult)
                    pool.drain()
                    ptt(new[:, 0], new[:, 0], tmp[:, 1], ALU.subtract)
                    i = ptt(new[:, 1], new[:, 1], tmp[:, 0], ALU.add)
                    if n == S5_LEVELS - 1:
                        i.then_inc(sem("tables"), 1)
                    pool.drain()

            def clear_wide(key, after):
                pool.wait_ge(*after)
                nc.gpsimd.memset(wide[:], 0.0).then_inc(*done("wide_zero", key))

            nc.gpsimd.memset(sc2[:, :, 2:QUAD], 0.0).then_inc(*done("c2_zero"))
            nc.gpsimd.memset(border[:], 0.0).then_inc(*done("border_zero", 0))
            make_low(pool, "pool", 0)
            make_low(pool, "pool", 1)
            for l in range(DEPTH):
                tiles(("win", l), lambda: clear_wide(l, at("mean_square", ("mix", l))),
                      lambda: during_ssd(l))
                tiles(("wout", l))
                tiles(("rt", l))
                moe(l, 2 * TB if l == 0 else TB)
                if l == 0:
                    pool.wait_ge(*at("x_ready", (("moe", 0, 1), KC - 1)))
                    nc.gpsimd.memset(border[:], 0.0).then_inc(*done("border_zero", 1))
            tiles(("foxf", 0))
            tiles(("foxin", 0))
            pool.wait_ge(*at("f_sp", 0))
            for b in range(2):
                nc.gpsimd.memset(table[b][:, 0, :, 0:1], 1.0)
                nc.gpsimd.memset(table[b][:, 1, :, 0:1], 0.0)
            pool.drain()
            for b in range(2):
                rotations(b, b)
            tiles(("foxout", 0))
            pool.wait_ge(*at("res_dve", (("foxout", 0), KC - 1)))
            pool.dma_start(bblk, dram["s5_b"]).then_inc(*done("s5_loaded", 0, 16))
            pool.dma_start(cT, dram["s5_c"]).then_inc(*done("s5_loaded", 1, 16))
            swiglu(("ffn", 0), FFN_SLICES)
            tiles(("s5in", 1))
            with pool.Fori(1, S5_CH // BATCH // 2) as g:
                for b in range(2):
                    pool.wait_ge(sem("states_done"), BATCH * (b - 1) + 2 * BATCH * g)
                    rotations(b, b + 2 * g)
            tiles(("glu", 1))
            swiglu(("ffn", 1), FFN_SLICES)
            pool.wait_ge(*at("x_ready", (("ffn", 1), KC - 1)))
            pool.dma_start(counts, dram["pool_counts"]).then_inc(*done("counts_loaded", 0, 16))
            clear_wide("pool", at("mean_square", ("pool",)))
            swiglu(("ffn", 2), FFN_SLICES)
            tiles(("foxf", 3))
            tiles(("foxin", 3))
            tiles(("foxout", 3))
            swiglu(("ffn", 3), FFN_SLICES)

        mm = nc.tensor.matmul

        @block.tensor
        def _(pe):
            def mm3(o, a, b, first, last, **kw):
                mm(o, a[0], b[0], start=first, stop=last and bool(kw), **kw)
                mm(o, a[0], b[1], start=False, stop=last and bool(kw), **kw)
                return mm(o, a[1], b[0], start=False, stop=last, **kw)

            def ada(part):
                tiles = ADA_PARTS[part]
                t0 = TILE_AT["ada", part] - tiles[0]

                def turn(q):
                    pe.wait_ge(*at("ada_row", q))
                    l, j = divmod(q, ADA_TILES)
                    for c in range(2):
                        i = mm(ps[2 + l][:, 4 * j + 2 * c:4 * j + 2 * c + 2], arow[:, q % 4, P * c:P * c + P],
                               k("partial"), start=True, stop=True)
                    i.then_inc(*done("ada_turned", q))

                for q in tiles:
                    t = t0 + q
                    pe.wait_ge(sem(f"tile_loaded{t % RING}"), 16 * (t // RING + 1))
                    w = ring[t % RING][:].rearrange("p (a b) -> p a b", a=KC)
                    if q >= 2:
                        pe.wait_ge(*at("ada_row", q - 2))
                    for c in range(KC):
                        a = QUAD * (c % 4)
                        i = mm(ps[q % 2][a:a + QUAD, 0:TCOLS], sc2[:, c, :], w[:, c, :], start=c < 4, stop=c >= 4,
                               tile_position=(0, a), skip_group_check=True)
                        if c >= KC - 4:
                            i.then_inc(sem("ada_sums"), 1)
                    pe.wait_ge(sem("ada_sums"), 4 * (q + 1))
                    pe.drain().then_inc(sem("tile_free"), 1)
                    if q > tiles[0]:
                        turn(q - 1)
                    if q == ADA_FIRST - 2:
                        mean_square(("mix", 0), slice(0, 2 * T))
                turn(tiles[-1])

            def mean_square(n, tok):
                for c in range(KC):
                    if c % 2 == 0:
                        pe.wait_ge(*at("squares", (n, c // 2)))
                    i = mm(ps[7][:, 0:tok.stop - tok.start], k("mean1024"), sq[:, c, tok],
                           start=c == 0, stop=c == KC - 1)
                i.then_inc(*done("mean_square", n))

            def project(name, groups, banks, ready, taken):
                for j, (out_ap, pairs) in enumerate(groups):
                    if j >= len(banks):
                        pe.wait_ge(*taken(j - len(banks)))
                    c0 = SPLIT_AT[name] + j // 2
                    for c, (a, b) in enumerate(pairs(*low_ready(c0))):
                        if j == 0:
                            pe.wait_ge(*ready(c))
                        i = mm3(out_ap(ps[banks[j % len(banks)]]), a, b, c == 0, c == KC - 1)
                    if j % 2 == 0 and LONE.get(name[0]) != j:
                        i.then_inc(*done("proj", (name, j)))
                    else:
                        i.then_inc(sem("tile_free"), 1)

            def by_column(xh, xl, tok, m):
                def pairs(wh, wl):
                    for c in range(KC):
                        a = slice(c * TCOLS + m * P, c * TCOLS + m * P + P)
                        yield (wh[:, a], wl[:, a]), (r(xh[:, c, tok]), r(xl[:, c, tok]))
                return pairs

            def narrow(name, xh, xl, tok, ready):
                project(name, [(lambda bank: bank[:, tok], by_column(xh, xl, tok, 0))], [5], ready, None)

            def narrow_turned(name, n, bank, off, blocks):
                pe.wait_ge(*at("narrow_sb", name))
                for b in range(blocks):
                    i = mm(ps[bank][:, off + n * b:off + n * b + n], narrow_sb[0:n, b * P:b * P + P], ident[0:n, 0:n],
                           start=True, stop=True)
                return i

            def win(l):
                groups = []
                for j, ch in enumerate(W_IN_ORDER):
                    tok = slice(0, 2 * T) if l == 0 or 12 <= ch < 18 else slice(0, T)
                    groups.append((lambda bank, tok=tok: bank[:, tok], by_column(SB3, HT_r, tok, j % 2)))
                groups.append((lambda bank: bank[:], by_column(SB3, HT_r, slice(0, 2 * T), 0)))
                project(("win", l), groups, [0, 1, 2, 3, 4, 5], lambda c: at("normed", (("mix", l), c)),
                        lambda j: at(*win_taken(l, j)))
                narrow_turned(("win", l), 16, 6, 0, 2 * TB).then_inc(*done("dt_raw", l))

            def ssd(l, s, full):
                o = s * T
                da = dts[:, 5, :, :]
                b0, b1 = 2 * s, 2 * s + 1
                for c in range(KC):
                    pe.wait_ge(*at("ssd_in", (l, c)))
                for b in range(TB):
                    for c in range(4):
                        i = nc.tensor.transpose(ps[6 + b][:, c * P:c * P + P],
                                                HT[:, c, o + b * P:o + b * P + P], ident)
                    i.then_inc(*done("x_tok", (l, s, b)))
                pe.wait_ge(*at("x_tok_sb", (l, s, 0)))
                for b in range(TB):
                    for g in range(2):
                        i = nc.tensor.transpose(ps[6][:, (2 * b + g) * P:(2 * b + g + 1) * P],
                                                HT[:, 4 + g, o + b * P:o + b * P + P], ident)
                i.then_inc(*done("b_tok", (l, s)))
                pe.wait_ge(*at("da", l))
                pe.wait_ge(*at("x_tok_sb", (l, s, 1)))
                ac = ps[7]
                mm(ac[:, 0:8], up, da[:, b0, 0:8], start=True, stop=True)
                mm(ac[:, 16:24], one, da[:, b0, 0:8], start=True, stop=False)
                mm(ac[:, 16:24], up, da[:, b1, 0:8], start=False, stop=True)
                mm(ac[:, 24:32], lo, da[:, b1, 8:16], start=True, stop=True)
                mm(ac[:, 8:16], lo, da[:, b0, 8:16], start=True, stop=False)
                mm(ac[:, 8:16], one, da[:, b1, 8:16], start=False, stop=True)
                mm(ac[:, 32:48], one, da[:, b0, :], start=True, stop=False)
                mm(ac[:, 32:48], one, da[:, b1, :], start=False, stop=True).then_inc(*done("acum", (l, s)))
                if full:
                    for g in range(2):
                        pe.wait_ge(*(at("b_tok_sb", (l, s)) if g == 0 else at("acum_sb", (l, s))))
                        for b in range(TB):
                            i = mm(ps[6 + g][:, b * T:b * T + T], HT[:, 4 + g, o + b * P:o + b * P + P],
                                   HT[:, 6 + g, o:o + T], start=True, stop=True)
                        i.then_inc(*done("scores", (l, s, g)))
                if s == 1:
                    n = slice(0, 2 * T if full else T)
                    mean4(("ln_var", l), lambda c: sq[:, c, n], 5, n, lambda c: at("ln_sq", l))
                    pe.wait_ge(*at("xw", l))
                    pe.wait_ge(*at("b_tok_sb", (l, s)))
                    for g in range(2):
                        if full:
                            pe.wait_ge(*at("scores_sb", (l, s, g)))
                        for b in range(TB):
                            i = mm(ps[6 + g][:], btok[:, b, g, :], xw[:, b, :, g * T:g * T + T],
                                   start=b == 0, stop=b == TB - 1)
                        i.then_inc(*done("states", (l, g)))
                if not full:
                    return

                def decay(h):
                    f, b = ps[2 * (h % 2)], ps[2 * (h % 2) + 1]
                    if h >= 2:
                        pe.wait_ge(*at("decayed", (l, s, h - 2)))
                    for n in range(2):
                        mm(f[:], r(dar[:, n, b0, h:h + 1]).to_broadcast([P, P]), r(fw), start=n == 0, stop=True, skip_group_check=True)
                        mm(f[:, 2 * P:], r(dar[:, n, b1, h:h + 1]).to_broadcast([P, P]), r(fw[:, 0:2 * P]), start=False, stop=True, skip_group_check=True)
                    fm = f[:].rearrange("p (a m c) -> p a m c", a=2, m=2)[:, :, 1, :]
                    mm(fm, identb, mask_f.unsqueeze(1).to_broadcast([P, 2, P]), start=False, stop=True, skip_group_check=True)
                    for n in range(2):
                        mm(b[:], r(dar[:, n, b1, 8 + h:9 + h]).to_broadcast([P, P]), r(bw), start=n == 0, stop=True, skip_group_check=True)
                        mm(b[:, 0:2 * P], r(dar[:, n, b0, 8 + h:9 + h]).to_broadcast([P, P]), r(bw[:, 2 * P:]), start=False, stop=True, skip_group_check=True)
                    bm = b[:].rearrange("p (a m c) -> p a m c", a=2, m=2)[:, :, 0, :]
                    mm(bm, identb, mask_b.unsqueeze(1).to_broadcast([P, 2, P]), start=False, stop=True, skip_group_check=True)\
                        .then_inc(*done("decay", (l, s, h)))

                def outputs(h):
                    c, q = h // 2, (h % 2) * HD
                    if h % 2 == 0 and c >= 2:
                        pe.wait_ge(*at("y_taken", (l, s, c - 2)))
                    pe.wait_ge(*at("mix_sb", (l, s, h)))
                    y = ps[4 + c % 2][q:q + HD, 0:T]
                    mm(y, xtok[:, 0, h * HD:h * HD + HD], mix0[:, h % 2, :], start=True, stop=False)
                    i = mm(y, xtok[:, 1, h * HD:h * HD + HD], mix1[:, h % 2, :], start=False, stop=s == 1)
                    if s == 0:
                        g, w = h // 4, (h % 4) * HD
                        pe.wait_ge(*at("c_decayed", (l, h)))
                        mm(y, h0[:, g, 0, w:w + HD], off_f[:, h % 2, :], start=False, stop=False)
                        i = mm(y, h0[:, g, 1, w:w + HD], off_b[:, h % 2, :], start=False, stop=True)
                    i.then_inc(*done("y", (l, s, h)))

                decay(0)
                decay(1)
                for h in range(HEADS):
                    if h + 2 < HEADS:
                        decay(h + 2)
                    outputs(h)

            def mean4(name, src, bank, tok, ready):
                for c in range(4):
                    pe.wait_ge(*ready(c))
                    i = mm(ps[bank][:, 0:tok.stop - tok.start], k("mean512"), src(c), start=c == 0, stop=c == 3)
                i.then_inc(*done("mean4", name))

            def wout(l, tok):
                groups = [(lambda bank: bank[:, 0:tok.stop], by_column(HT_r, MIX_r, tok, j % 2)) for j in range(KC)]
                project(("wout", l), groups, [0, 1, 2, 3], lambda c: at("mixed", (l, c)),
                        lambda j: at("res_dve", (("wout", l), j)))

            def router(l, blocks):
                narrow(("rt", l), MIX_r, HT_r, slice(0, blocks * P), lambda c: at("normed", (("ffn", l), c)))

            def ranks(l, blocks):
                pe.wait_ge(*at("picks", l))
                for b in range(blocks):
                    o = ps[6][:, 128 + EXPERTS * b:128 + EXPERTS * b + EXPERTS]
                    for b2 in range(b + 1):
                        mm(o, up if b2 == b else one, picked[:, b2, :], start=b2 == 0, stop=b2 == b)
                for b in range(blocks):
                    i = mm(ps[6][:, 256:256 + EXPERTS], one, picked[:, b, :], start=b == 0, stop=b == blocks - 1)
                i.then_inc(*done("ranks", l))

            def tokens(l, blocks):
                for b in range(blocks):
                    if b >= 2:
                        pe.wait_ge(*at("h_tok", (l, b - 2)))
                    t = slice(b * P, b * P + P)
                    for c in range(KC):
                        o = ps[2 * (b % 2) + c // 4][:, (c % 4) * P:(c % 4) * P + P]
                        mm(o, MIX_r[:, c, t], ident, start=True, stop=False)
                        i = mm(o, HT_r[:, c, t], ident, start=False, stop=True)
                    i.then_inc(*done("h_turned", (l, b)))
                    if b == 0:
                        narrow_turned(("rt", l), ROUTES, 6, 0, blocks).then_inc(*done("logits", l))
                    if b == 1:
                        ranks(l, blocks)

            def experts(name, blocks):
                c0, d0, slices = SPLIT_AT[name], DOWN_AT[name], PER_BLOCK * blocks
                split0, raw0, hid0, taken0 = (base(x, name) for x in ("x_split", "hid_raw", "hidden", "out_taken"))
                loop_base("x_turned", name, blocks)
                loop_base("hid_turned", name, slices)

                def turn_rows(b, g):
                    pe.wait_ge(rows_loaded(name, b), 16 * (b // 2 + 1) + 16 * g)
                    if split0 or b or not isinstance(g, int):
                        pe.wait_ge(sem("x_split"), split0 + b + RING // 2 * g)
                    for c in range(KC):
                        i = nc.tensor.transpose(ps[6 + c // 4][:, (c % 4) * P:(c % 4) * P + P],
                                                xrows[:, b % 2, c * P:c * P + P], ident)
                    i.then_inc(sem("x_turned"), 1)

                def gate_up(j, g, half):
                    b = j // 2
                    wh, wl = low_ready(c0 + j, g)
                    pe.wait_ge(sem("x_split"), split0 + b + 1 + RING // 2 * g)
                    for c in range(half * KC // 2, (half + 1) * KC // 2):
                        a = slice(c * TCOLS, c * TCOLS + TCOLS)
                        i = mm3(ps[4 + j % 2][:, 0:TCOLS], (r(xT[:, b % 2, 0, c, :]), r(xT[:, b % 2, 1, c, :])),
                                (wh[:, a], wl[:, a]), c == 0, c == KC - 1)
                    if half:
                        i.then_inc(sem("tile_free"), 1)

                def turn_hidden(j, g):
                    pe.wait_ge(sem("hid_raw"), raw0 + j + 1 + RING * g)
                    nc.tensor.transpose(ps[4 + j % 2][:, TCOLS:TCOLS + P], hrows[:, j % 2, :], ident).then_inc(sem("hid_turned"), 1)

                def down(j, g):
                    d, b = d0 + j, j // 2
                    if j % 2 == 0 and (taken0 or b >= 2 or not isinstance(g, int)):
                        pe.wait_ge(sem("out_taken"), taken0 + b - 1 + RING // 2 * g)
                    pe.wait_ge(sem("down_low_dve"), d + 1 + RING * g)
                    pe.wait_ge(sem("down_low_pool"), d + 1 + RING * g)
                    pe.wait_ge(sem("hidden"), hid0 + j + 1 + RING * g)
                    dh, dl = r(dhigh[d % HIGH][:]), r(dring_r[d % RING][:])
                    h = (r(hid[:, j % 2, 0, 0:P]), r(hid[:, j % 2, 1, 0:P]))
                    for n in range(2):
                        a = slice(n * D // 2, (n + 1) * D // 2)
                        i = mm3(ps[2 * (b % 2) + n][:], h, (dh[:, a], dl[:, a]), j % 2 == 0, j % 2 == 1)
                    i.then_inc(sem("down_free"), 1)

                def one(j, g):
                    if j % 2 == 0 and j // 2 + 1 < blocks:
                        turn_rows(j // 2 + 1, g)
                    if j + 1 < slices:
                        gate_up(j + 1, g, 0)
                    turn_hidden(j, g)
                    if j + 1 < slices:
                        gate_up(j + 1, g, 1)
                    down(j, g)

                turn_rows(0, 0)
                gate_up(0, 0, 0)
                gate_up(0, 0, 1)
                slices_loop(pe, slices, one, 0 if taken0 else 1)

            def moe(l, blocks):
                tokens(l, blocks)
                experts(("moe", l), EXPERTS)

                def skip():
                    pe.drain()
                    for name, n in (("tile_free", OVER_SLICES), ("down_free", OVER_SLICES), ("x_turned", OVER),
                                    ("hid_turned", OVER_SLICES)):
                        pe.sem_inc(sem(name), n)

                if_overflow(pe, l, lambda: experts(("over", l), OVER), skip)
                pe.wait_ge(sem("out_taken"), base("out_taken", ("over", l)) + OVER)
                for b in range(blocks):
                    pe.wait_ge(*at("y_sum", (l, b)))
                    for c in range(KC):
                        bank, col = sum_at(c, b // TB)
                        i = nc.tensor.transpose(bank[:, col + (b % TB) * P:col + (b % TB) * P + P],
                                                ytok(b, 0)[:, c * P:c * P + P], ident)
                    i.then_inc(*done("y_turned", (l, b)))

            def swiglu(name, slices, xh, xl, ready):
                c0, d0, hid0 = SPLIT_AT[name], DOWN_AT[name], base("hidden", name)
                for b in range(4):
                    mm(ps[b][:], zeros[:, 0:P], zeros, start=True, stop=True)

                def gate_up(j, g, ready=None):
                    wh, wl = low_ready(c0 + j, g)
                    for m in range(2):
                        for c in range(KC):
                            if ready and m == 0:
                                pe.wait_ge(*ready(c))
                            a = slice(c * TCOLS + m * P, c * TCOLS + m * P + P)
                            i = mm3(ps[4 + j % 2][:, m * T:m * T + T], (wh[:, a], wl[:, a]), (r(xh(c)), r(xl(c))),
                                    c == 0, c == KC - 1)
                    i.then_inc(sem("tile_free"), 1)

                def down(j, g):
                    d = d0 + j
                    pe.wait_ge(sem("down_low_dve"), d + 1 + RING * g)
                    pe.wait_ge(sem("down_low_pool"), d + 1 + RING * g)
                    pe.wait_ge(sem("hidden"), hid0 + j + 1 + RING * g)
                    dh, dl = r(dhigh[d % HIGH][:]), r(dring_r[d % RING][:])
                    for c in range(KC):
                        a = slice(c * P, c * P + P)
                        i = mm3(ps[c // 2][:, (c % 2) * T:(c % 2) * T + T], (dh[:, a], dl[:, a]),
                                (r(hid[:, j % 2, 0, :]), r(hid[:, j % 2, 1, :])), False, True, skip_group_check=True)
                    i.then_inc(sem("down_free"), 1)

                gate_up(0, 0, ready)
                turns = (slices - 1) // RING
                with pe.Fori(0, turns) as g:
                    for j in range(RING):
                        gate_up(j + 1, g)
                        down(j, g)
                for j in range(turns * RING, slices):
                    if j + 1 < slices:
                        gate_up(j + 1, 0)
                    down(j, 0)

            def fox(i_layer):
                j_fox = i_layer // 3
                name = ("fox", i_layer)
                narrow(("foxf", i_layer), H2h, H2r, slice(0, T), lambda c: at("normed", (name, c)))
                narrow_turned(("foxf", i_layer), 16, 7, 256, TB).then_inc(*done("f_raw", i_layer))
                groups = []
                for j in range(4):
                    for b in range(TB):
                        def pairs(wh, wl, b=b):
                            for c in range(KC):
                                t, a = slice(b * P, b * P + P), slice(c * TCOLS, c * TCOLS + TCOLS)
                                yield (r(H2h[:, c, t]), r(H2r[:, c, t])), (wh[:, a], wl[:, a])
                        groups.append((lambda bank: bank[:, 0:TCOLS], pairs))
                for j in range(16):
                    groups.append((lambda bank: bank[:, 0:T], by_column(H2h, H2r, slice(0, T), j % 2)))
                project(("foxin", i_layer), groups, [0, 1, 2, 3], lambda c: at("normed", (name, c)),
                        lambda j: at("fox_sb", (i_layer, j)))

                spl = fx[:, 5, :, :]

                def logits(h):
                    c, q = h // 2, (h % 2) * HD
                    L = ps[h % 2]
                    if h >= 2:
                        pe.wait_ge(*at("prob", (i_layer, h - 2)))
                    else:
                        pe.wait_ge(*at("fox_sb", (i_layer, 23)))
                        pe.wait_ge(*at("f_sp", i_layer))
                    for n in range(2):
                        mm(L[:, 0:384], r(splr[:, n, 0, h:h + 1]).to_broadcast([P, P]), r(fw[:, 0:384]), start=n == 0, stop=True, skip_group_check=True)
                    mm(L[:, 256:384], spl[:, 1, h:h + 1].to_broadcast([P, P]), up, start=False, stop=True, skip_group_check=True)
                    diag = L[:].rearrange("p (a m c) -> p a m c", a=2, m=2)[:, :, 0, :]
                    mm(diag, identb, mask_b.unsqueeze(1).to_broadcast([P, 2, P]), start=False, stop=True, skip_group_check=True)
                    mm(L[:, 0:P], Q2[q:q + HD, c, 0:P], K2[q:q + HD, c, 0:P], start=False, stop=True, skip_group_check=True)
                    mm(L[:, P:384], Q2[q:q + HD, c, P:T], K2[q:q + HD, c, 0:T], start=False, stop=True, skip_group_check=True)\
                        .then_inc(*done("att", (i_layer, h)))

                def turn(h):
                    pe.wait_ge(*at("prob_n", (i_layer, h)))
                    if h >= 2:
                        pe.wait_ge(*at("probT", (i_layer, h - 2)))
                    for blk, to in ((0, 0), (1, 1), (2, 2)):
                        i = nc.tensor.transpose(ps[2 + h % 2][:, to * P:to * P + P],
                                                prob[:, h % 2, blk * P:blk * P + P], ident)
                    i.then_inc(*done("att_turned", (i_layer, h)))

                def values(h):
                    c, q = h // 2, (h % 2) * HD
                    pe.wait_ge(*at("probT", (i_layer, h)))
                    if h % 2 == 0 and c >= 2:
                        pe.wait_ge(*at("o_high", (i_layer, c - 2)))
                    o = ps[4 + c % 2]
                    mm(o[q:q + HD, 0:T], vtok[:, 0, h * HD:h * HD + HD], probT[:, h % 2, 0:T], start=True, stop=False)
                    mm(o[q:q + HD, P:T], vtok[:, 1, h * HD:h * HD + HD], probT[:, h % 2, T:384],
                       start=False, stop=True).then_inc(*done("o", (i_layer, h)))

                for h in range(FOX_HEADS + 2):
                    if h < FOX_HEADS:
                        logits(h)
                    if 1 <= h <= FOX_HEADS:
                        turn(h - 1)
                    if h >= 2:
                        values(h - 2)
                groups = [(lambda bank: bank[:, 0:T], by_column(H2r, O2r, slice(0, T), j % 2)) for j in range(KC)]
                project(("foxout", i_layer), groups, [0, 1, 2, 3], lambda c: at("o_split", (i_layer, c)),
                        lambda j: at("res_dve", (("foxout", i_layer), j)))

            def s5_turn(n):
                if n == 3:
                    pe.wait_ge(*at("bT", 0))
                for c in (2 * n, 2 * n + 1):
                    for r in range(2):
                        i = nc.tensor.transpose(
                            ps[4 + n % 3][:, (2 * (c % 2) + r) * P:(2 * (c % 2) + r + 1) * P],
                            bblk[:, r, 4 * c:4 * c + 4, :].rearrange("p a b -> p (a b)"), ident)
                i.then_inc(*done("b_turned", n))

            def s5():
                pe.wait_ge(*at("b_bar", 1))
                for n in range(3):
                    s5_turn(n)
                groups = [(lambda bank: bank[:, 0:T], by_column(H2h, H2r, slice(0, T), j % 2)) for j in range(KC)]
                project(("s5in", 1), groups, [0, 1, 2, 3], lambda c: at("normed", (("s5",), c)),
                        lambda j: at("u_sb", j))
                s5_turn(3)
                pe.wait_ge(*at("bT", 2))
                pe.wait_ge(*at("u_sb", KC - 1))
                pe.wait_ge(*at("c_neg"))
                pe.wait_ge(*at("s5_dmat"))

                def inputs(j):
                    q, c = 32 * (j % 4), j // 4
                    if j == 24:
                        pe.wait_ge(*at("bT", 3))
                    if j >= 2:
                        pe.wait_ge(sem("bu_used"), j - 1)
                    for i in range(2):
                        mm_ = mm(ps[j % 2][:, i * T:i * T + T], bT[q:q + 32, i, c, :], Q2[q:q + 32, c, :],
                                 start=True, stop=True, tile_position=(q, 0))
                    mm_.then_inc(sem("bu"), 1)

                def outputs(j):
                    q, c = 32 * (j % 4), j // 4
                    bank = ps[2 + c % 2]
                    if j % 4 == 0:
                        if c >= 2:
                            pe.wait_ge(*at("s5_y", c - 2))
                        mm(bank[:, 0:T], s5_dmat[:, c, :], Q2[:, c, :], start=True, stop=False, skip_group_check=True)
                    pe.wait_ge(sem("states_done"), j + 1)
                    y = bank[q:q + 32, 0:T]
                    for n, (part, z) in enumerate(((0, s5_q[:, j % 2, 0, 0, :]), (0, s5_q[:, j % 2, 1, 0, :]),
                                                   (1, s5_q[:, j % 2, 0, 1, :]), (1, s5_q[:, j % 2, 1, 1, :]))):
                        i = mm(y, cT[:, part, j, :], z, start=False, stop=n == 3, skip_group_check=True, tile_position=(0, q))
                    i.then_inc(sem("s5_out"), 1)

                inputs(0)
                for j in range(S5_CH):
                    if j + 1 < S5_CH:
                        inputs(j + 1)
                    outputs(j)
                groups = [(lambda bank: bank[:, 0:T], by_column(H2r, O2r, slice(0, T), j % 2)) for j in range(2 * KC)]
                project(("glu", 1), groups, [4, 5, 6, 7], lambda c: at("gelu_split", c),
                        lambda j: at("glu_val", j // 2) if j % 2 == 0 else at("glu_gate", j // 2))

            def pooling():
                t0 = TILE_AT["poolw", 2]
                pe.wait_ge(sem(f"tile_loaded{t0 % RING}"), 16 * (t0 // RING + 1))
                w = ring[t0 % RING][:].rearrange("p (g a n) -> p g a n", g=POOLS, a=2)
                for j in range(KC):
                    g, m = j // 2, j % 2
                    if j >= 4:
                        pe.wait_ge(*at("res_dve", (("poolw", 2), j - 4)))
                    if m == 0:
                        pe.wait_ge(*at("pooled", g))
                    for a in range(2):
                        i = mm(ps[j % 4][:, 0:T], w[:, g, a, m * P:m * P + P], O2[:, 2 * g + a, :],
                               start=a == 0, stop=a == 1)
                    i.then_inc(*done("proj", (("poolw", 2), j)))
                pe.wait_ge(*at("res_dve", (("poolw", 2), KC - 1)))
                nc.tensor.sem_inc(sem("tile_free"), 1)

            pe.wait_ge(*at("c2_silu"))
            pe.wait_ge(*at("c2_zero"))
            pe.wait_ge(sem("con_loaded"), 16)
            ada(0)
            pe.wait_ge(sem("vec_loaded"), 16 * 2)
            for l in range(DEPTH):
                both, last = slice(0, 2 * T), l == DEPTH - 1
                tok = slice(0, T) if last else both
                if l:
                    mean_square(("mix", l), both)
                win(l)
                for j in (18, 19, 15, 16, 17):
                    pe.wait_ge(*at(*win_taken(l, j)))
                ada(l + 1)
                mean4(("ln_mean", l), lambda c: MIX[:, c, tok], 4, tok, lambda c: at("conv_y", l))
                ssd(l, 1, not last)
                pe.wait_ge(*at("h0", (l, 1)))
                ssd(l, 0, True)
                mean4(("ssd_ms", l), lambda c: sq[:, 4 + c, tok], 6, tok, lambda c: at("ssd_sq", l))
                wout(l, tok)
                mean_square(("ffn", l), tok)
                router(l, 2 if last else 4)
                moe(l, TB if last else 2 * TB)
            mean_square(("final1",), slice(0, T))
            for i_layer in range(4):
                name = (("fox", 0), ("s5",), ("pool",), ("fox", 3))[i_layer]
                mean_square(name, slice(0, T))
                if i_layer in (0, 3):
                    fox(i_layer)
                elif i_layer == 1:
                    s5()
                else:
                    pooling()
                mean_square(("ffn2", i_layer), slice(0, T))
                swiglu(("ffn", i_layer), FFN_SLICES, lambda c: H2h[:, c, :], lambda c: H2r[:, c, :],
                       lambda c: at("normed", (("ffn2", i_layer), c)))
            mean_square(("final2",), slice(0, T))

        act_fn = nc.scalar.activation

        @block.scalar
        def _(act):
            c2_at, c2_end = VEC_AT["c2"][0], VEC_AT["c2"][0] + 2 * KC
            act.dma_start(vec[:, c2_at:c2_end], dram["vec"][:, c2_at:c2_end]).then_inc(sem("c2_loaded"), 16)
            act.dma_start(con[:], dram["con"]).then_inc(sem("con_loaded"), 16)
            act.dma_start(XT[:], dram["xt"]).then_inc(sem("x_loaded"), 16)
            act.dma_start(vec[:, c2_end:], dram["vec"][:, c2_end:]).then_inc(sem("vec_loaded"), 16)
            act.dma_start(msk[:], dram["msk"]).then_inc(sem("vec_loaded"), 16)
            act.wait_ge(sem("c2_loaded"), 16)
            act_fn(sc2[:, :, 0:2], v("c2"), ACT.Silu).then_inc(*done("c2_silu"))

            def make_high(c, g=0):
                if c >= len(SPLIT):
                    return
                t = SPLIT[c]
                act.wait_ge(sem(f"tile_loaded{t % RING}"), 16 * (t // RING + 1) + 16 * g)
                if c >= HIGH:
                    act.wait_ge(sem("tile_free"), SPLIT[c - HIGH] + 1 + RING * g)
                nc.scalar.copy(r(high[c % HIGH][:]), ring[t % RING][:]).then_inc(sem("high"), 1)

            def make_down_high(d, g=0):
                act.wait_ge(sem(f"down_loaded{d % RING}"), 16 * (d // RING + 1) + 16 * g)
                if d >= HIGH or not isinstance(g, int):
                    act.wait_ge(sem("down_free"), d - HIGH + 1 + RING * g)
                nc.scalar.copy(r(dhigh[d % HIGH][:]), dring[d % RING][:]).then_inc(sem("down_high"), 1)

            def ada(part):
                tiles = ADA_PARTS[part]
                for q in tiles:
                    act.wait_ge(sem("tile_free"), TILE_AT["ada", part] + q - tiles[0] + 1)
                    if q >= 4:
                        act.wait_ge(*at("ada_turned", q - 4))
                    nc.scalar.copy(arow[:, q % 4, :], ps[q % 2][:, 0:TCOLS]).then_inc(*done("ada_row", q))
                    if q == ADA_FIRST - 4:
                        act.wait_ge(sem("con_loaded"), 16)
                        squares(("mix", 0), slice(0, 2 * T), lambda c: (sem("x_loaded"), 16))
                    if q == ADA_FIRST + 2:
                        act_fn(s5p[:, 0, :], v("log_dt"), ACT.Exp).then_inc(*done("s5_dt"))
                    if q == tiles[-4] and part == 1:
                        act.wait_ge(*at("s5_ang"))
                        act_fn(s5p[:, 3, :], s5p[:, 1, :], ACT.Exp)
                        act_fn(s5p[:, 6, :], s5p[:, 4, :], ACT.Sin)
                        act_fn(s5p[:, 7, :], s5p[:, 5, :], ACT.Sin).then_inc(*done("s5_trig"))

            def squares(n, tok, ready):
                for p in range(KC // 2):
                    act.wait_ge(*ready(2 * p + 1))
                    act_fn(sq[:, 2 * p:2 * p + 2, tok], XT[:, 2 * p:2 * p + 2, tok], ACT.Square)\
                        .then_inc(*done("squares", (n, p)))

            def root(n, tok):
                act.wait_ge(*at("mean_square", n))
                act_fn(rms[:, 0:tok.stop], ps[7][:, 0:tok.stop], ACT.Sqrt, bias=k("eps6")).then_inc(*done("root", n))

            def split_high(n, dst, src, bias, streams):
                for c in range(KC):
                    for s in range(streams):
                        act.wait_ge(*at("scaled", (n, c, s)))
                        o, i = r(dst[:, c, s * T:s * T + T]), src[:, c, s * T:s * T + T]
                        i = nc.scalar.copy(o, i) if bias is None else act_fn(o, i, ACT.Identity, bias=bias(c, s))
                        i.then_inc(*done("norm_high", (n, c, s)))

            def narrow(name, bank, n, tokens):
                act.wait_ge(*proj_at(name, LONE[name[0]]))
                nc.scalar.copy(narrow_sb[0:n, 0:tokens], bank[0:n, 0:tokens]).then_inc(*done("narrow_sb", name))

            def win(l):
                streams = 1 if l == DEPTH - 1 else 2
                for j, ch in enumerate(W_IN_ORDER):
                    if ch >= 4:
                        act.wait_ge(*proj_at(("win", l), j))
                    if ch < 4:
                        pass
                    elif ch < 8:
                        if ch >= 6:
                            act.wait_ge(*at("gated", (l, ch - 6)))
                        act_fn(sig[:, ch % 2, 0:streams * T], ps[j % 6][:, 0:streams * T], ACT.Sigmoid)\
                            .then_inc(*done("win_act", (l, j)))
                    elif ch < 12:
                        act_fn(zs[:, ch - 8, 0:streams * T], ps[j % 6][:, 0:streams * T], ACT.Silu)\
                            .then_inc(*done("win_act", (l, j)))
                    else:
                        if ch == 12:
                            act.wait_ge(*at("wide_zero", l))
                        n = 2 if ch < 18 else streams
                        act_fn(xbc[:, ch - 12, 0:n, 2:2 + T],
                               ps[j % 6][:, 0:n * T].rearrange("p (a b) -> p a b", a=n), ACT.Copy)\
                            .then_inc(*done("win_act", (l, j)))
                    if j % 2 and j // 2 + 2 < WIN_TILES:
                        make_high(SPLIT_AT["win", l] + j // 2 + 2)
                narrow(("win", l), ps[len(W_IN_ORDER) % 6], 16, 2 * T)

            def softplus_log(name, key, e, src):
                act.wait_ge(*at(name + "_abs", key))
                act_fn(e, src, ACT.Exp, scale=-1.0)
                act.drain()
                act_fn(e, e, ACT.Ln, bias=1.0).then_inc(*done(name + "_log", key))

            def ssd_in(l):
                streams = 1 if l == DEPTH - 1 else 2
                for c in range(8):
                    act.wait_ge(*at("sconv", l))
                    n = 2 * T if c < 6 else streams * T
                    act_fn(HT[:, c, 0:n], HT[:, c, 0:n], ACT.Silu).then_inc(*done("ssd_in", (l, c)))
                act.wait_ge(*at("centred", l))
                tok = slice(0, streams * T)
                act_fn(sq[:, 0:4, tok], MIX[:, 0:4, tok], ACT.Square).then_inc(*done("ln_sq", l))

            def ln_silu(l, n):
                for c in range(4):
                    act.wait_ge(*at("ln_scaled", l))
                    act_fn(MIX[:, c, 0:n], MIX[:, c, 0:n], ACT.Silu, bias=v(f"ln_b{l}")[:, c:c + 1],
                           scale=v(f"ln_g{l}")[:, c:c + 1])

            def ssd(l, s, full):
                last = l == DEPTH - 1
                if s == 0 and not last:
                    ln_silu(l, 2 * T)
                for b in range(TB):
                    act.wait_ge(*at("x_tok", (l, s, b)))
                    nc.scalar.copy(xtok[:, b, :], ps[6 + b][:]).then_inc(*done("x_tok_sb", (l, s, b)))
                act.wait_ge(*at("b_tok", (l, s)))
                nc.scalar.copy(btok[:].rearrange("p a b c -> p (a b c)"), ps[6][:]).then_inc(*done("b_tok_sb", (l, s)))
                if full:
                    for g in range(2):
                        act.wait_ge(*at("scores", (l, s, g)))
                        nc.scalar.copy(score[:, g, :, :].rearrange("p a b -> p (a b)"), ps[6 + g][:])\
                            .then_inc(*done("scores_sb", (l, s, g)))
                if s == 1:
                    act.wait_ge(*at("to_end", l))
                    act_fn(wst[:, 1, :, :], wst[:, 0, :, :], ACT.Exp).then_inc(*done("end_decay", l))
                    for g in range(2):
                        act.wait_ge(*at("states", (l, g)))
                        nc.scalar.copy(h0[:, g, :, :].rearrange("p a b -> p (a b)"), ps[6 + g][:]).then_inc(*done("h0", (l, g)))
                    tok = slice(0, 2 * T if full else T)
                    act.wait_ge(*at("mean4", ("ln_var", l)))
                    act_fn(rms[:, tok], ps[5][:, tok], ACT.Sqrt, bias=k("eps5")).then_inc(*done("ln_root", l))
                if not full:
                    return
                if s == 0 and last:
                    ln_silu(l, T)
                act.wait_ge(*at("acum_sb", (l, s)))
                for h in range(HEADS):
                    p = h % 2
                    f, b = ps[2 * p], ps[2 * p + 1]
                    act.wait_ge(*at("decay", (l, s, h)))
                    if h >= 2:
                        act.wait_ge(*at("mix_sb", (l, s, h - 2)))
                    act_fn(dec_f0[:, p, :], f[:, P:3 * P], ACT.Exp, bias=nacum[:, 0, h:h + 1])
                    act_fn(dec_f1[:, p, :], f[:, 3 * P:], ACT.Exp, bias=nacum[:, 1, h:h + 1])
                    act_fn(dec_b1[:, p, :], b[:, P:3 * P], ACT.Exp, bias=nacum[:, 1, 8 + h:9 + h])
                    i = act_fn(dec_b0[:, p, :], b[:, 0:P], ACT.Exp, bias=nacum[:, 0, 8 + h:9 + h])
                    if s == 0:
                        if h >= 2:
                            act.wait_ge(*at("y", (l, s, h - 2)))
                        act_fn(off_f[:, p, :].rearrange("p (a c) -> p a c", a=2),
                               f[:].rearrange("p (a m c) -> p a m c", a=2, m=2)[:, :, 0, :], ACT.Exp)
                        i = act_fn(off_b[:, p, :].rearrange("p (a c) -> p a c", a=2),
                                   b[:].rearrange("p (a m c) -> p a m c", a=2, m=2)[:, :, 1, :], ACT.Exp)
                    i.then_inc(*done("decayed", (l, s, h)))

            def mixer_norms(l, tok):
                act.wait_ge(*at("y_done", l))
                act_fn(sq[:, 4:8, tok], MIX[:, 4:8, tok], ACT.Square).then_inc(*done("ssd_sq", l))
                for c in range(KC):
                    if c == 4:
                        act.wait_ge(*at("mean4", ("ssd_ms", l)))
                        act_fn(rms[:, tok], ps[6][:, tok], ACT.Sqrt, bias=k("eps6")).then_inc(*done("ssd_root", l))
                    if c >= 4:
                        act.wait_ge(*at("ssd_out", (l, c - 4)))
                    nc.scalar.copy(r(HT_r[:, c, tok]), MIX[:, c, tok]).then_inc(*done("mix_high", (l, c)))

            def router(l, blocks):
                narrow(("rt", l), ps[5], ROUTES, blocks * P)
                make_high(SPLIT_AT["rt", l] + 2)
                act.wait_ge(*at("rt_shift", l))
                act_fn(rt[:, 2, :, 0:4], rt[:, 1, :, 0:4], ACT.Exp)
                act_fn(rt[:, 2, :, 4:8], rt[:, 1, :, 4:8], ACT.Exp).then_inc(*done("rt_exp", l))

            def experts(name, blocks, row0):
                t0, c0, d0, slices = TILE_AT[name], SPLIT_AT[name], DOWN_AT[name], PER_BLOCK * blocks
                turned0, hid_turned0 = base("x_turned", name), base("hid_turned", name)
                taken0 = loop_base("out_taken", name, blocks)
                stored0 = [loop_base(f"y_stored{p}", name, 16 * blocks // 2) for p in range(2)]
                loop_base("gate_act", name, slices)
                loop_base("x_high", name, blocks)
                loop_base("hid_high", name, slices)

                def split_rows(b, g):
                    act.wait_ge(sem("x_turned"), turned0 + b + 1 + RING // 2 * g)
                    for n in range(2):
                        i = nc.scalar.copy(r(xT[:, b % 2, 0, 4 * n:4 * n + 4, :].rearrange("p a b -> p (a b)")), ps[6 + n][:])
                    i.then_inc(sem("x_high"), 1)

                def store(b, g):
                    act.wait_ge(sem("down_free"), d0 + 2 * b + 2 + RING * g)
                    if stored0[b % 2] or b >= 2 or not isinstance(g, int):
                        act.wait_ge(sem(f"y_stored{b % 2}"), stored0[b % 2] + 16 * (b // 2) + 16 * g)
                    for n in range(2):
                        i = nc.scalar.copy(yrows[:, b % 2, n * D // 2:(n + 1) * D // 2], ps[2 * (b % 2) + n][:])
                    i.then_inc(sem("out_taken"), 1)
                    act.wait_ge(sem("out_taken"), taken0 + b + 1 + RING // 2 * g)
                    dst = y_slots[row0 + P * b:row0 + P * b + P] if isinstance(g, int) else \
                        y_slots[bass.ds(row0 + P * b + 2 * P * g, P)]
                    act.dma_start(dst, yrows[:, b % 2, :]).then_inc(sem(f"y_stored{b % 2}"), 16)

                def one(j, g):
                    act.wait_ge(sem("tile_free"), t0 + j + 1 + RING * g)
                    act_fn(gact[:, j % 2, 0:P], ps[4 + j % 2][:, 0:P], ACT.Silu).then_inc(sem("gate_act"), 1)
                    if j + 2 < slices:
                        make_high(c0 + j + 2, g)
                    act.wait_ge(sem("hid_turned"), hid_turned0 + j + 1 + RING * g)
                    nc.scalar.copy(r(hid[:, j % 2, 0, 0:P]), ps[4 + j % 2][:, TCOLS:TCOLS + P]).then_inc(sem("hid_high"), 1)
                    if j % 2 == 0 and j // 2 + 1 < blocks:
                        split_rows(j // 2 + 1, g)
                    if j + 1 < slices:
                        make_down_high(d0 + j + 1, g)
                    if j % 2:
                        store(j // 2, g)

                if name[0] == "over":
                    for a in range(2):
                        make_high(c0 + a)
                make_down_high(d0)
                split_rows(0, 0)
                slices_loop(act, slices, one, 0 if taken0 else 1)

            def moe(l, blocks):
                for b in range(blocks):
                    act.wait_ge(*at("h_turned", (l, b)))
                    for n in range(2):
                        i = nc.scalar.copy(htok[:, b, n * D // 2:(n + 1) * D // 2], ps[2 * (b % 2) + n][:])
                    i.then_inc(*done("h_tok", (l, b)))
                experts(("moe", l), EXPERTS, 0)
                name = ("over", l)

                def skip():
                    act.drain()
                    for n, by in (("high", OVER_SLICES), ("down_high", OVER_SLICES), ("gate_act", OVER_SLICES),
                                  ("hid_high", OVER_SLICES), ("x_high", OVER), ("out_taken", OVER)):
                        act.sem_inc(sem(n), by)
                    for p in range(2):
                        act.wait_ge(sem(f"y_stored{p}"), base(f"y_stored{p}", name))
                        act.sem_inc(sem(f"y_stored{p}"), 16 * OVER // 2)

                if_overflow(act, l, lambda: experts(name, OVER, EXPERTS * P), skip)
                act.wait_ge(*at("slots", l))
                for b in range(blocks):
                    act.wait_ge(*at(f"y_tok{b}", (l, b, 1)))
                    act_fn(ytok(b, 0), ytok(b, 0), ACT.Identity, scale=weight[:, 0, b:b + 1])\
                        .then_inc(*done("y_weighted", (l, b)))
            def swiglu(name, slices):
                t0, c0, d0 = TILE_AT[name], SPLIT_AT[name], DOWN_AT[name]
                loop_base("gate_act", name, slices)

                def one(j, g):
                    act.wait_ge(sem("tile_free"), t0 + j + 1 + RING * g)
                    act_fn(gact[:, j % 2, :], ps[4 + j % 2][:, 0:T], ACT.Silu).then_inc(sem("gate_act"), 1)
                    make_high(c0 + j + 2, g)
                    if j + 1 < slices:
                        make_down_high(d0 + j + 1, g)

                make_down_high(d0)
                slices_loop(act, slices, one, 1 if d0 == 0 else 0)

            def tiles_after(name, j):
                if j % 2:
                    make_high(SPLIT_AT[name] + j // 2 + 2)

            def fox(i_layer):
                narrow(("foxf", i_layer), ps[5], 16, T)
                make_high(SPLIT_AT["foxf", i_layer] + 2)
                softplus_log("f", i_layer, fx[:, 3, :, :], fx[:, 1, :, :])
                for j in range(24):
                    act.wait_ge(*proj_at(("foxin", i_layer), j))
                    bank = ps[j % 4]
                    if j < 8:
                        i = nc.scalar.copy(vtok[:, j % 2, TCOLS * (j // 2):TCOLS * (j // 2) + TCOLS], bank[:, 0:TCOLS])
                    elif j < 16:
                        i = nc.scalar.mul(Q2[:, j - 8, :], bank[:, 0:T], HD ** -0.5)
                    else:
                        i = nc.scalar.copy(K2[:, j - 16, :], bank[:, 0:T])
                    i.then_inc(*done("fox_sb", (i_layer, j)))
                    tiles_after(("foxin", i_layer), j)
                for h in range(FOX_HEADS + 2):
                    p = h % 2
                    if h < FOX_HEADS:
                        act.wait_ge(*at("att_max", (i_layer, h)))
                        if h >= 2:
                            act.wait_ge(*at("att_turned", (i_layer, h - 2)))
                        L = ps[p]
                        act_fn(prob[:, p, 0:P], L[:, 0:P], ACT.Exp, bias=stat[:, p, 0, 0:1], accum_out=stat[:, p, 1, 0:1])
                        act_fn(prob[:, p, P:384], L[:, P:384], ACT.Exp, bias=stat[:, p, 0, 1:2],
                               accum_out=stat[:, p, 1, 1:2]).then_inc(*done("prob", (i_layer, h)))
                    if 1 <= h <= FOX_HEADS:
                        q = (h - 1) % 2
                        act.wait_ge(*at("att_turned", (i_layer, h - 1)))
                        if h >= 3:
                            act.wait_ge(*at("o", (i_layer, h - 3)))
                        nc.scalar.copy(probT[:, q, :], ps[2 + q][:, 0:384]).then_inc(*done("probT", (i_layer, h - 1)))
                    if h >= 2 and h % 2 == 1:
                        c = (h - 2) // 2
                        act.wait_ge(*at("o", (i_layer, h - 2)))
                        nc.scalar.copy(O2[:, c, :], ps[4 + c % 2][:, 0:T]).then_inc(*done("o_sb", (i_layer, c)))
                        act_fn(r(H2r[:, c, :]), ps[4 + c % 2][:, 0:T], ACT.Copy).then_inc(*done("o_high", (i_layer, c)))

            def s5():
                def bT_from(n):
                    act.wait_ge(*at("b_turned", n))
                    nc.scalar.copy(bT[:, :, 2 * n:2 * n + 2, :].rearrange("p a c b -> p c a b"),
                                   ps[4 + n % 3][:].rearrange("p (c a b) -> p c a b", c=2, a=2)).then_inc(*done("bT", n))

                for n in range(3):
                    bT_from(n)
                for j in range(KC):
                    act.wait_ge(*proj_at(("s5in", 1), j))
                    nc.scalar.copy(Q2[:, j, :], ps[j % 4][:, 0:T]).then_inc(*done("u_sb", j))
                    tiles_after(("s5in", 1), j)
                bT_from(3)
                for c in range(KC):
                    act.wait_ge(sem("s5_out"), 2 + 4 * c + 4)
                    act_fn(O2[:, c, :], ps[2 + c % 2][:, 0:T], ACT.Gelu_apprx_tanh).then_inc(*done("s5_y", c))
                    act.drain()
                    nc.scalar.copy(r(H2r[:, c, :]), O2[:, c, :]).then_inc(*done("gelu_high", c))
                for j in range(KC):
                    act.wait_ge(*proj_at(("glu", 1), 2 * j + 1))
                    if j >= 2:
                        act.wait_ge(*at("res_dve", (("glu", 1), j - 2)))
                    act_fn(sig[:, j % 2, 0:T], ps[4 + (2 * j + 1) % 4][:, 0:T], ACT.Sigmoid).then_inc(*done("glu_gate", j))
                    tiles_after(("glu", 1), 2 * j + 1)

            ada(0)
            root(("mix", 0), slice(0, 2 * T))
            act.wait_ge(sem("vec_loaded"), 32)
            for l in range(DEPTH):
                last = l == DEPTH - 1
                tok = slice(0, T) if last else slice(0, 2 * T)
                bias = lambda which: lambda c, s: mod[l][:, 24 * which + c, s:s + 1]
                act_fn(aneg[:, 0, :], v(f"a_log{l}"), ACT.Exp).then_inc(*done("a_exp", l))
                if l:
                    squares(("mix", l), slice(0, 2 * T), lambda c: at("x_ready", (("moe", l - 1, 1), c)))
                    root(("mix", l), slice(0, 2 * T))
                for a in range(2):
                    make_high(SPLIT_AT["win", l] + a)
                split_high(("mix", l), SB3, HT, bias(0), 2)
                win(l)
                ada(l + 1)
                softplus_log("dt", l, dts[:, 3, :, :], dts[:, 1, :, :])
                ssd_in(l)
                ssd(l, 1, not last)
                ssd(l, 0, True)
                for j in (0, 1):
                    make_high(SPLIT_AT["wout", l] + j)
                mixer_norms(l, tok)
                for a in range(HALF_D):
                    tiles_after(("wout", l), 2 * a + 1)
                squares(("ffn", l), tok, lambda c: at("res_dve", (("wout", l), c)))
                root(("ffn", l), tok)
                split_high(("ffn", l), MIX_r, HT, bias(1), 1 if last else 2)
                router(l, TB if last else 2 * TB)
                moe(l, TB if last else 2 * TB)
            squares(("final1",), slice(0, T), lambda c: at("x_ready", (("moe", 1, 0), c)))
            root(("final1",), slice(0, T))
            for a in range(2):
                make_high(SPLIT_AT["foxf", 0] + a)
            for i_layer in range(4):
                name = (("fox", 0), ("s5",), ("pool",), ("fox", 3))[i_layer]
                squares(name, slice(0, T), lambda c: at("x_ready", (("ffn", i_layer - 1), c) if i_layer else ("first", c)))
                root(name, slice(0, T))
                if i_layer != 2:
                    split_high(name, H2h, H2, None, 1)
                last_res = (("foxout", 0), ("glu", 1), ("poolw", 2), ("foxout", 3))[i_layer]
                if i_layer in (0, 3):
                    fox(i_layer)
                    for a in range(HALF_D):
                        tiles_after(last_res, 2 * a + 1)
                elif i_layer == 1:
                    s5()
                squares(("ffn2", i_layer), slice(0, T), lambda c: at("res_dve", (last_res, c)))
                root(("ffn2", i_layer), slice(0, T))
                split_high(("ffn2", i_layer), H2h, H2, None, 1)
                swiglu(("ffn", i_layer), FFN_SLICES)
            squares(("final2",), slice(0, T), lambda c: at("x_ready", (("ffn", 3), c)))
            root(("final2",), slice(0, T))

        stt, tt, ts = nc.vector.scalar_tensor_tensor, nc.vector.tensor_tensor, nc.vector.tensor_scalar
        tss = nc.vector.tensor_single_scalar

        @block.vector
        def _(dve):
            dve.wait_ge(sem("con_loaded"), 16)
            nc.vector.tensor_copy(r(tri_r[:]).rearrange("p (a b c) -> p a b c", a=3, b=2),
                                  k("tri").rearrange("p (a c) -> p a c", a=3).unsqueeze(2).to_broadcast([P, 3, 2, P]))\
                .then_inc(*done("tri_rounded"))
            dve.wait_ge(sem("vec_loaded"), 32)
            dve.wait_ge(sem("x_loaded"), 16)

            def ada(part):
                tiles = ADA_PARTS[part]
                dve.wait_ge(*at("ada_turned", tiles[-1]))
                vectors = [(q // ADA_TILES, q % ADA_TILES // (D // TCOLS)) for q in tiles[::D // TCOLS]]
                for l in sorted({a for a, _ in vectors}):
                    own = [b for a, b in vectors if a == l]
                    x = slice(KC * own[0], KC * own[-1] + KC)
                    tt(mod[l][:, x, :], ps[2 + l][:, 2 * x.start:2 * x.stop].rearrange("p (a b) -> p a b", b=2),
                       v(f"b_ada{l}")[:, x, :], ALU.add)
                dve.drain()
                for l, i in vectors:
                    if i % 3 == 1:
                        stt(gsc[l][:, i // 3, :, :], mod[l][:, KC * i:KC * i + KC, :], 1.0,
                            v(f"{('g_mix', 'g_ffn')[i // 3]}{l}"), ALU.add, ALU.mult)
                dve.drain()

            def scale(n, streams, gain, bias=None, xh=None):
                dve.wait_ge(*at("root", n))
                nc.vector.reciprocal(rstd[:, 0:streams * T], rms[:, 0:streams * T])
                dve.drain()

                def low(c):
                    for s in range(streams):
                        h, hh = HT_(c, s), xh[:, c, s * T:s * T + T]
                        dve.wait_ge(*at("norm_high", (n, c, s)))
                        to = r(H2r[:, c, :] if bias is None else HT_r[:, c, s * T:s * T + T])
                        i = tt(to, h, hh, ALU.subtract) if bias is None else \
                            stt(to, h, bias(c, s), hh, ALU.add, ALU.subtract)
                    i.then_inc(*done("normed", (n, c)))

                HT_ = lambda c, s: HT[:, c, s * T:s * T + T] if bias is not None else H2[:, c, :]
                for c in range(KC):
                    for s in range(streams):
                        stt(HT_(c, s), XT[:, c, s * T:s * T + T], gain(c, s), rstd[:, s * T:s * T + T], ALU.mult, ALU.mult)\
                            .then_inc(*done("scaled", (n, c, s)))
                    if xh is not None and c:
                        low(c - 1)
                if xh is not None:
                    low(KC - 1)

            def tiles(name, j=None):
                n = dict((a, b) for a, b, _ in PLAN)[name]
                for a in range(n) if j is None else [j]:
                    if SPLIT_AT[name] + a + 2 < len(SPLIT):
                        make_low(dve, "dve", SPLIT_AT[name] + a + 2)

            def gate(l):
                flat = W_IN_ORDER
                dve.wait_ge(*at("border_zero", l))
                for c in range(4):
                    ju, jg = flat.index(c), flat.index(4 + c)
                    dve.wait_ge(*proj_at(("win", l), ju))
                    dve.wait_ge(*at("win_act", (l, jg)))
                    bank = ps[ju % 6]
                    if c < 2:
                        dst = vrow[:, c, :, HALF:HALF + GRID_W]
                    else:
                        dst = vcol[:, c - 2, 3:3 + ROWS, :]
                    i = tt(dst, bank[:, 0:T].rearrange("p (a b) -> p a b", a=ROWS),
                           sig[:, c % 2, 0:T].rearrange("p (a b) -> p a b", a=ROWS), ALU.mult)
                    if l < DEPTH - 1:
                        i = tt(vseq[:, c, HALF:HALF + T], bank[:, T:2 * T], sig[:, c % 2, T:2 * T], ALU.mult)
                    i.then_inc(*done("gated", (l, c)))
                dve.drain()

            def conformer(l):
                w, b = v(f"conv_w{l}"), v(f"conv_b{l}")

                def grid(c):
                    return MIX[:, c, 0:T].rearrange("p (a b) -> p a b", a=ROWS)

                first = HALF - (ROWS - 1)
                for c in range(4):
                    src = vrow[:, c, :, 0:GRID_W] if c < 2 else vcol[:, c - 2, 0:ROWS, :]
                    tap = 0 if c < 2 else first
                    ts(grid(c), src, w[:, c, tap:tap + 1], b[:, c:c + 1], ALU.mult, ALU.add)
                    if l < DEPTH - 1:
                        ts(MIX[:, c, T:2 * T], vseq[:, c, 0:T], w[:, c, 0:1], b[:, c:c + 1], ALU.mult, ALU.add)
                dve.drain()
                with dve.Fori(1, TAPS) as tap:
                    for c in range(2):
                        stt(grid(c), vrow[:, c, :, bass.ds(tap, GRID_W)], w[:, c, bass.ds(tap, 1)], grid(c), ALU.mult, ALU.add)
                    if l < DEPTH - 1:
                        for c in range(4):
                            y = MIX[:, c, T:2 * T]
                            stt(y, vseq[:, c, bass.ds(tap, T)], w[:, c, bass.ds(tap, 1)], y, ALU.mult, ALU.add)
                    dve.drain()
                for r in range(1, 2 * ROWS - 1):
                    for c in range(2, 4):
                        i = stt(grid(c), vcol[:, c - 2, r:r + ROWS, :], w[:, c, first + r:first + r + 1], grid(c), ALU.mult, ALU.add)
                    if r < 2 * ROWS - 2:
                        dve.drain()
                i.then_inc(*done("conv_y", l))

            def sconv(l):
                w, b = v(f"sconv_w{l}"), v(f"sconv_b{l}")
                dve.wait_ge(*at("win_act", (l, W_IN_ORDER.index(19))))
                dve.wait_ge(*proj_at(("win", l), LONE["win"]))
                streams = 1 if l == DEPTH - 1 else 2
                for tap in range(STAPS):
                    for c in range(8):
                        n = 2 if c < 6 else streams
                        y = HT[:, c, 0:n * T].rearrange("p (a b) -> p a b", a=n)
                        src = xbc[:, c, 0:n, tap:tap + T]
                        if tap == 0:
                            i = ts(y, src, w[:, c, 0:1], b[:, c:c + 1], ALU.mult, ALU.add)
                        else:
                            i = stt(y, src, w[:, c, tap:tap + 1], y, ALU.mult, ALU.add)
                    if tap == STAPS - 1:
                        i.then_inc(*done("sconv", l))
                    else:
                        dve.drain()

            def softplus(name, key, raw, bias, x, ab, mx, lp, res, sign):
                tt(x, raw, bias, ALU.add)
                dve.drain()
                tss(lp, x, -1.0, ALU.mult)
                ts(mx, x, sign, 0.0, ALU.mult, ALU.max)
                dve.drain()
                tt(ab, x, lp, ALU.max).then_inc(*done(name + "_abs", key))
                dve.wait_ge(*at(name + "_log", key))
                tt(res, mx, lp, ALU.add)
                dve.drain()

            def steps(l):
                dve.wait_ge(*at("dt_raw", l))
                raw = ps[6][:, 0:64].rearrange("p (a b) -> p a b", a=4)
                bias = v(f"dt_bias{l}").unsqueeze(1).to_broadcast([P, 4, 16])
                softplus("dt", l, raw, bias, dts[:, 0, :, :], dts[:, 1, :, :], dts[:, 2, :, :], dts[:, 3, :, :],
                         dts[:, 4, :, :], 1.0)
                dve.wait_ge(*at("a_exp", l))
                tss(aneg[:, 1, :], aneg[:, 0, :], -1.0, ALU.mult)
                dve.drain()
                tt(dts[:, 5, :, :], dts[:, 4, :, :], aneg[:, 1, :].unsqueeze(1).to_broadcast([P, 4, 16]), ALU.mult)
                dve.drain()
                nc.vector.tensor_copy(r(dar[:, 0]), dts[:, 5, :, :])
                dve.drain()
                tt(r(dar[:, 1]), dts[:, 5, :, :], dar[:, 0], ALU.subtract).then_inc(*done("da", l))

            def centre(l, n):
                y = MIX[:, 0:4, 0:n]
                dve.wait_ge(*at("mean4", ("ln_mean", l)))
                tt(y, y, ps[4][:, 0:n].unsqueeze(1).to_broadcast([P, 4, n]), ALU.subtract).then_inc(*done("centred", l))

            def ln_rstd(l, n):
                dve.wait_ge(*at("ln_root", l))
                nc.vector.reciprocal(rstd[:, 0:n], rms[:, 0:n]).then_inc(*done("ln_rstd", l))

            def ssd(l, s, full):
                o = s * T
                dt = dts[:, 4, :, :]
                dve.wait_ge(*at("acum", (l, s)))
                if s == 1:
                    tss(nacum[:], ps[7][:, 0:32].rearrange("p (a b) -> p a b", a=2), -1.0, ALU.mult)
                    dve.drain()
                    tt(wst[:, 0, :, :], nacum[:], ps[7][:, 32:48].unsqueeze(1).to_broadcast([P, 2, 16]), ALU.add)\
                        .then_inc(*done("to_end", l))
                    dve.drain()
                    dve.drain().then_inc(*done("acum_sb", (l, s)))
                    dve.wait_ge(*at("end_decay", l))
                    tt(wst[:, 0, :, :], wst[:, 1, :, :], dt[:, 2:4, :], ALU.mult)
                    dve.wait_ge(*at("x_tok_sb", (l, s, 1)))
                    dve.drain()
                    for b in range(TB):
                        for d in range(2):
                            i = tt(xw[:, b, d, :].rearrange("p (h c) -> p h c", h=HEADS),
                                   xtok[:, b, :].rearrange("p (h c) -> p h c", h=HEADS),
                                   wst[:, 0, b, 8 * d:8 * d + 8].unsqueeze(2).to_broadcast([P, HEADS, HD]), ALU.mult)
                    i.then_inc(*done("xw", l))
                    if not full:
                        ln_rstd(l, T)
                        dve.drain()
                        y = MIX[:, 0:4, 0:T]
                        tt(y, y, rstd[:, 0:T].unsqueeze(1).to_broadcast([P, 4, T]), ALU.mult).then_inc(*done("ln_scaled", l))
                else:
                    tss(nacum[:], ps[7][:, 0:32].rearrange("p (a b) -> p a b", a=2), -1.0, ALU.mult)\
                        .then_inc(*done("acum_sb", (l, s)))
                if not full:
                    return
                b0, b1 = 2 * s, 2 * s + 1

                def take(c):
                    dve.wait_ge(*at("y", (l, s, 2 * c + 1)))
                    y = MIX[:, 4 + c, o:o + T]
                    stt(y, HT[:, c, o:o + T], v(f"d_skip{l}")[:, c:c + 1], ps[4 + c % 2][:, 0:T], ALU.mult, ALU.add)\
                        .then_inc(*done("y_taken", (l, s, c)))
                    dve.drain()
                    return tt(y, y, zs[:, c, o:o + T], ALU.mult)

                dve.wait_ge(*at("scores_sb", (l, s, 1)))
                for h in range(HEADS):
                    p, g = h % 2, h // 4
                    dve.wait_ge(*at("decayed", (l, s, h)))
                    if h >= 2:
                        dve.wait_ge(*at("y", (l, s, h - 2)))
                    stt(mix0[:, p, :], dec_f0[:, p, :], dt[:, b0, h:h + 1], score[:, g, 0, :], ALU.mult, ALU.mult)
                    stt(part0[:, p, :], dec_b0[:, p, :], dt[:, b0, 8 + h:9 + h], score[:, g, 0, 0:P], ALU.mult, ALU.mult)
                    stt(mix1[:, p, :], dec_b1[:, p, :], dt[:, b1, 8 + h:9 + h], score[:, g, 1, :], ALU.mult, ALU.mult)
                    stt(part1[:, p, :], dec_f1[:, p, :], dt[:, b1, h:h + 1], score[:, g, 1, P:T], ALU.mult, ALU.mult)
                    dve.drain()
                    tt(mix0[:, p, 0:P], mix0[:, p, 0:P], part0[:, p, :], ALU.add)
                    tt(mix1[:, p, P:T], mix1[:, p, P:T], part1[:, p, :], ALU.add).then_inc(*done("mix_sb", (l, s, h)))
                    if s == 1 and h == 1:
                        ln_rstd(l, 2 * T)
                    if h >= 3 and h % 2:
                        take((h - 3) // 2)
                take(3).then_inc(*done("y_stream", (l, s)))

            def mixer_norms(l, tok):
                n = tok.stop
                dve.drain()
                dve.drain().then_inc(*done("y_done", l))

                def lows(chunks):
                    for c in chunks:
                        dve.wait_ge(*at("mix_high", (l, c)))
                        tt(r(MIX_r[:, c, tok]), MIX[:, c, tok], HT_r[:, c, tok], ALU.subtract).then_inc(*done("mixed", (l, c)))

                lows(range(4))
                dve.wait_ge(*at("ssd_root", l))
                dve.drain()
                nc.vector.reciprocal(rstd[:, 0:n], rms[:, 0:n])
                dve.drain()
                for c in range(4):
                    y = MIX[:, 4 + c, tok]
                    stt(y, y, v(f"ssd_g{l}")[:, c:c + 1], rstd[:, 0:n], ALU.mult, ALU.mult).then_inc(*done("ssd_out", (l, c)))
                lows(range(4, KC))

            def residual(name, taken, gates=None, streams=1):
                for j in range(KC):
                    dve.wait_ge(*proj_at(name, j))
                    for s in range(streams):
                        x = XT[:, j, s * T:s * T + T]
                        p = ps[taken[j % len(taken)]][:, s * T:s * T + T]
                        i = tt(x, p, x, ALU.add) if gates is None else stt(x, p, gates(j, s), x, ALU.mult, ALU.add)
                    i.then_inc(*done("res_dve", (name, j)))
                    if j % 2:
                        tiles(name, j // 2)

            def first_max(hot, score_, x, mx, n):
                tt(hot, x, mx.to_broadcast([P, n, 4]), ALU.is_equal)
                dve.drain()
                tt(score_, hot, k("first4").unsqueeze(1).to_broadcast([P, n, 4]), ALU.mult)
                dve.drain()
                nc.vector.tensor_reduce(mx, score_, AX.X, ALU.max)
                dve.drain()
                tt(hot, score_, mx.to_broadcast([P, n, 4]), ALU.is_equal)
                dve.drain()

            def router(l, n):
                tiles(("rt", l))
                dve.wait_ge(*at("logits", l))
                lg = rt[:, 0, 0:n, :]
                tt(lg, ps[6][:, 0:20 * n].rearrange("p (a b) -> p a b", a=n),
                   v(f"b_rt{l}").unsqueeze(1).to_broadcast([P, n, 20]), ALU.add)
                dve.drain()
                a = lambda i: rs1[:, i, 0:n, :]
                one = lambda i: rs1[:, 12 + i // 4, 0:n, i % 4:i % 4 + 1]
                mx, gs, e2, wsum, w1, w2, m2 = (one(i) for i in range(7))
                nc.vector.tensor_reduce(mx, lg[:, :, 0:4], AX.X, ALU.max)
                dve.drain()
                tt(rt[:, 1, 0:n, 0:4], lg[:, :, 0:4], mx.to_broadcast([P, n, 4]), ALU.subtract)
                first_max(a(0), a(1), lg[:, :, 0:4], mx, n)
                tt(a(2), lg[:, :, 4:8], a(0)[:, :, 0:1].to_broadcast([P, n, 4]), ALU.mult)
                dve.drain()
                for g in range(1, 4):
                    tt(a(3), lg[:, :, 4 + 4 * g:8 + 4 * g], a(0)[:, :, g:g + 1].to_broadcast([P, n, 4]), ALU.mult)
                    dve.drain()
                    tt(a(2), a(2), a(3), ALU.add)
                    dve.drain()
                nc.vector.tensor_reduce(mx, a(2), AX.X, ALU.max)
                dve.drain()
                tt(rt[:, 1, 0:n, 4:8], a(2), mx.to_broadcast([P, n, 4]), ALU.subtract).then_inc(*done("rt_shift", l))
                first_max(a(4), a(5), a(2), mx, n)
                stt(a(6), a(4), -BIG, a(2), ALU.mult, ALU.add)
                dve.drain()
                nc.vector.tensor_reduce(m2, a(6), AX.X, ALU.max)
                dve.drain()
                first_max(a(7), a(8), a(6), m2, n)
                for g in range(4):
                    for i, hot in enumerate((a(4), a(7))):
                        tt(pick[:, i, 0:n, 4 * g:4 * g + 4], hot, a(0)[:, :, g:g + 1].to_broadcast([P, n, 4]), ALU.mult)
                dve.drain()
                tt(picked[:, 0:n, :], pick[:, 0, 0:n, :], pick[:, 1, 0:n, :], ALU.add).then_inc(*done("picks", l))
                dve.wait_ge(*at("rt_exp", l))
                nc.vector.tensor_reduce(gs, rt[:, 2, 0:n, 0:4], AX.X, ALU.add)
                tt(a(9), rt[:, 2, 0:n, 4:8], a(4), ALU.mult)
                tt(a(10), rt[:, 2, 0:n, 4:8], a(7), ALU.mult)
                dve.drain()
                nc.vector.tensor_reduce(w1, a(9), AX.X, ALU.add)
                nc.vector.tensor_reduce(w2, a(10), AX.X, ALU.add)
                dve.drain()
                tt(wsum, w1, w2, ALU.add)
                dve.drain()
                tt(wsum, wsum, gs, ALU.mult)
                dve.drain()
                nc.vector.reciprocal(wsum, wsum)
                dve.drain()
                for i, w in enumerate((w1, w2)):
                    tt(weight[:, i, 0:n].unsqueeze(2), w, wsum, ALU.mult)
                dve.wait_ge(*at("ranks", l))
                rank = ps[6][:, 128:128 + EXPERTS * n].rearrange("p (a b) -> p a b", a=n)
                total = ps[6][:, 256:256 + EXPERTS]
                blocks_, upto, before, shift = (extra[:, i, :] for i in range(4))
                tss(past[:, 0:n, :], rank, P + 0.5, ALU.is_gt)
                tss(blocks_, total, P + 0.5, ALU.is_gt)
                for m in (2, 3):
                    dve.drain()
                    stt(blocks_, total, m * P + 0.5, blocks_, ALU.is_gt, ALU.add)
                dve.drain()
                nc.vector.tensor_tensor_scan(upto, k("tri")[:, P:P + EXPERTS], blocks_, 0.0, ALU.mult, ALU.add)
                dve.drain()
                tt(before, upto, blocks_, ALU.subtract)
                dve.drain()
                stt(shift, before, float(P), k("over_row"), ALU.mult, ALU.add)
                dve.drain()
                per = lambda x: x.unsqueeze(1).to_broadcast([P, n, EXPERTS])
                tt(row[:, 0:n, :], past[:, 0:n, :], per(shift), ALU.mult)
                dve.drain()
                tt(row[:, 0:n, :], row[:, 0:n, :], rank, ALU.add)
                dve.drain()
                tt(row[:, 0:n, :], row[:, 0:n, :], per(k("first_row")), ALU.add)
                dve.drain()
                for i in range(2):
                    tt(prod[:, i, 0:n, :], pick[:, i, 0:n, :], row[:, 0:n, :], ALU.mult)
                dve.drain()
                nc.vector.tensor_reduce(slot_f[:, :, 0:n], prod[:, :, 0:n, :], AX.X, ALU.add)
                dve.drain()
                nc.vector.tensor_copy(slot[:, :, 0:n], slot_f[:, :, 0:n]).then_inc(*done("slots", l))
                ids, by_e = k("block_id").unsqueeze(2).to_broadcast([P, OVER, EXPERTS]), \
                    lambda x: x.unsqueeze(1).to_broadcast([P, OVER, EXPERTS])
                tt(in_block, ids, by_e(before), ALU.is_ge)
                tt(below, ids, by_e(upto), ALU.is_lt)
                dve.drain()
                tt(in_block, in_block, below, ALU.mult)
                dve.drain()
                tt(in_block, in_block, by_e(k("expert_id")), ALU.mult)
                dve.drain()
                nc.vector.tensor_reduce(over_f, in_block, AX.X, ALU.add)
                dve.drain()
                nc.vector.tensor_copy(over_expert, over_f)
                nc.vector.tensor_copy(overflow, upto[:, EXPERTS - 1:EXPERTS])
                dve.drain().then_inc(*done("overflow", l))

            def experts(name, blocks):
                c0, d0, slices = SPLIT_AT[name], DOWN_AT[name], PER_BLOCK * blocks
                act0, high0, hid_high0 = (base(x, name) for x in ("gate_act", "x_high", "hid_high"))
                for n, total in (("x_split", blocks), ("hid_raw", slices), ("hidden", slices)):
                    loop_base(n, name, total)

                def split_rows(b, g):
                    dve.wait_ge(sem("x_high"), high0 + b + 1 + RING // 2 * g)
                    for n in range(2):
                        hi, lo = (xT[:, b % 2, i, 4 * n:4 * n + 4, :].rearrange("p a b -> p (a b)") for i in range(2))
                        i = tt(r(lo), ps[6 + n][:], hi, ALU.subtract)
                    i.then_inc(sem("x_split"), 1)

                def one(j, g):
                    dve.wait_ge(sem("gate_act"), act0 + j + 1 + RING * g)
                    tt(hrows[:, j % 2, :], gact[:, j % 2, 0:P], ps[4 + j % 2][:, P:TCOLS], ALU.mult).then_inc(sem("hid_raw"), 1)
                    if j + 2 < slices:
                        make_low(dve, "dve", c0 + j + 2, g)
                    dve.wait_ge(sem("hid_high"), hid_high0 + j + 1 + RING * g)
                    tt(r(hid[:, j % 2, 1, 0:P]), ps[4 + j % 2][:, TCOLS:TCOLS + P], hid[:, j % 2, 0, 0:P], ALU.subtract)\
                        .then_inc(sem("hidden"), 1)
                    if j % 2 == 0 and j // 2 + 1 < blocks:
                        split_rows(j // 2 + 1, g)
                    if j + 1 < slices:
                        make_down_low(dve, "dve", d0 + j + 1, g)

                if name[0] == "over":
                    for a in range(2):
                        make_low(dve, "dve", c0 + a)
                make_down_low(dve, "dve", d0)
                split_rows(0, 0)
                slices_loop(dve, slices, one)

            def moe(l, blocks):
                experts(("moe", l), EXPERTS)
                name = ("over", l)

                def skip():
                    dve.drain()
                    for n, by in (("low_dve", OVER_SLICES), ("down_low_dve", OVER_SLICES), ("x_split", OVER),
                                  ("hid_raw", OVER_SLICES), ("hidden", OVER_SLICES)):
                        dve.sem_inc(sem(n), by)

                if_overflow(dve, l, lambda: experts(name, OVER), skip)
                for b in range(blocks):
                    dve.wait_ge(*at(f"y_tok{b}", (l, b, 1)))
                    y1, y2 = ytok(b, 0), ytok(b, 1)
                    dve.wait_ge(*at("y_weighted", (l, b)))
                    stt(y1, y2, weight[:, 1, b:b + 1], y1, ALU.mult, ALU.add).then_inc(*done("y_sum", (l, b)))

            def swiglu(name, slices, between=None):
                c0, d0, act0 = SPLIT_AT[name], DOWN_AT[name], base("gate_act", name)
                loop_base("hidden", name, slices)

                def one(j, g):
                    dve.wait_ge(sem("gate_act"), act0 + j + 1 + RING * g)
                    tt(hraw, gact[:, j % 2, :], ps[4 + j % 2][:, T:2 * T], ALU.mult)
                    dve.drain()
                    nc.vector.tensor_copy(r(hid[:, j % 2, 0, :]), hraw)
                    dve.drain()
                    tt(r(hid[:, j % 2, 1, :]), hraw, hid[:, j % 2, 0, :], ALU.subtract).then_inc(sem("hidden"), 1)
                    if c0 + j + 2 < len(SPLIT):
                        make_low(dve, "dve", c0 + j + 2, g)
                    if j + 1 < slices:
                        make_down_low(dve, "dve", d0 + j + 1, g)
                    if between is not None and isinstance(g, int) and 1 <= j < RING:
                        between(j - 1)
                    dve.drain()

                make_down_low(dve, "dve", d0)
                slices_loop(dve, slices, one, 0 if between is None else 1)

            def add_sum(name, gates=None, stream=0):
                if gates is None:
                    dve.wait_ge(sem("down_free"), DOWN_AT[name] + FFN_SLICES)
                else:
                    dve.wait_ge(*at("y_turned", (name[1], TB * stream + TB - 1)))
                for c in range(KC):
                    x = XT[:, c, stream * T:stream * T + T]
                    bank, col = sum_at(c, stream)
                    p = bank[:, col:col + T]
                    i = tt(x, p, x, ALU.add) if gates is None else stt(x, p, gates(c), x, ALU.mult, ALU.add)
                    i.then_inc(*done("x_ready", (name, c)))
                dve.drain()

            def fox(i_layer):
                j_fox = i_layer // 3
                tiles(("foxf", i_layer))
                dve.wait_ge(*at("f_raw", i_layer))
                softplus("f", i_layer, ps[7][:, 256:288].rearrange("p (a b) -> p a b", a=TB),
                         v(f"fox_b{j_fox}").unsqueeze(1).to_broadcast([P, TB, 16]),
                         fx[:, 0, :, :], fx[:, 1, :, :], fx[:, 2, :, :], fx[:, 3, :, :], fx[:, 5, :, :], -1.0)
                dve.drain()
                nc.vector.tensor_copy(r(splr[:, 0]), fx[:, 5, :, :])
                dve.drain()
                tt(r(splr[:, 1]), fx[:, 5, :, :], splr[:, 0], ALU.subtract)
                dve.drain().then_inc(*done("f_sp", i_layer))
                tiles(("foxin", i_layer))
                for h in range(FOX_HEADS):
                    p = h % 2
                    L = ps[p]
                    dve.wait_ge(*at("att", (i_layer, h)))
                    nc.vector.reduce_max(stat[:, p, 0, 0:1], L[:, 0:P], AX.X, negate=True)
                    nc.vector.reduce_max(stat[:, p, 0, 1:2], L[:, P:384], AX.X, negate=True)\
                        .then_inc(*done("att_max", (i_layer, h)))
                    dve.wait_ge(*at("prob", (i_layer, h)))
                    nc.vector.reciprocal(stat[:, p, 2, :], stat[:, p, 1, :])
                    dve.drain()
                    tss(prob[:, p, 0:P], prob[:, p, 0:P], stat[:, p, 2, 0:1], ALU.mult)
                    tss(prob[:, p, P:384], prob[:, p, P:384], stat[:, p, 2, 1:2], ALU.mult)\
                        .then_inc(*done("prob_n", (i_layer, h)))
                for c in range(KC):
                    dve.wait_ge(*at("o_high", (i_layer, c)))
                    tt(r(O2r[:, c, :]), O2[:, c, :], H2r[:, c, :], ALU.subtract).then_inc(*done("o_split", (i_layer, c)))
                residual(("foxout", i_layer), [0, 1, 2, 3])

            def s5_rates():
                dve.wait_ge(*at("s5_dt"))
                pv = lambda i: s5p[:, i, :]
                tt(pv(1), v("a_re"), pv(0), ALU.mult)
                tt(pv(2), v("a_im"), pv(0), ALU.mult)
                dve.drain()
                tss(pv(9), pv(2), math.pi / 2, ALU.add)
                dve.drain()
                for src, dst in ((2, 4), (9, 5)):
                    tss(pv(8), pv(src), 1 / (2 * math.pi), ALU.mult)
                    dve.drain()
                    nc.vector.tensor_copy(pv(10).bitcast(I32), pv(8))
                    dve.drain()
                    nc.vector.tensor_copy(pv(8), pv(10).bitcast(I32))
                    dve.drain()
                    stt(pv(dst), pv(8), -6.28125, pv(src), ALU.mult, ALU.add)
                    dve.drain()
                    stt(pv(dst), pv(8), -(2 * math.pi - 6.28125), pv(dst), ALU.mult, ALU.add)
                    dve.drain()
                    ts(pv(dst), pv(dst), 3.1415925, -3.1415925, ALU.min, ALU.max)
                    dve.drain()
                dve.drain().then_inc(*done("s5_ang"))
                dve.wait_ge(*at("s5_trig"))
                lam_re, lam_im = pv(18), pv(19)
                tt(lam_re, pv(3), pv(7), ALU.mult)
                tt(lam_im, pv(3), pv(6), ALU.mult)
                dve.drain()
                tss(pv(11), lam_re, -1.0, ALU.add)
                tt(pv(12), v("a_re"), v("a_re"), ALU.mult)
                tt(pv(13), v("a_im"), v("a_im"), ALU.mult)
                dve.drain()
                tt(pv(12), pv(12), pv(13), ALU.add)
                dve.drain()
                nc.vector.reciprocal(pv(12), pv(12))
                tt(pv(13), pv(11), v("a_re"), ALU.mult)
                tt(pv(14), lam_im, v("a_im"), ALU.mult)
                tt(pv(15), lam_im, v("a_re"), ALU.mult)
                tt(pv(16), pv(11), v("a_im"), ALU.mult)
                dve.drain()
                tt(pv(13), pv(13), pv(14), ALU.add)
                tt(pv(15), pv(15), pv(16), ALU.subtract)
                dve.drain()
                tt(pv(13), pv(13), pv(12), ALU.mult)
                tt(pv(15), pv(15), pv(12), ALU.mult)
            def s5_powers():
                pv = lambda i: s5p[:, i, :]
                nc.vector.tensor_copy(pw[:, 0, 0, :], pv(7))
                nc.vector.tensor_copy(pw[:, 0, 1, :], pv(6))
                dve.drain()
                for n in range(1, S5_LEVELS):
                    tt(pv(16), pw[:, n - 1, 0, :], pw[:, n - 1, 0, :], ALU.mult)
                    tt(pv(17), pw[:, n - 1, 1, :], pw[:, n - 1, 1, :], ALU.mult)
                    stt(pw[:, n, 1, :], pw[:, n - 1, 0, :], 2.0, pw[:, n - 1, 1, :], ALU.mult, ALU.mult)
                    dve.drain()
                    tt(pw[:, n, 0, :], pv(16), pv(17), ALU.subtract)
                    dve.drain()

            def s5_matrices(part):
                pv = lambda i: s5p[:, i, :]
                if part == 0:
                    dve.wait_ge(sem("s5_loaded"), 32)
                if part == 2:
                    tss(cT[:, 1, :, :], cT[:, 1, :, :], -1.0, ALU.mult).then_inc(*done("c_neg"))
                    return
                n = S5_CH // 2
                own = slice(part * n, part * n + n)
                br, bi = bblk[:, 0, own, :], bblk[:, 1, own, :]
                f_re = pv(13)[:, own].unsqueeze(2).to_broadcast([P, n, S5_CH])
                f_im = pv(15)[:, own].unsqueeze(2).to_broadcast([P, n, S5_CH])
                tmp = [view(wide, i * n * S5_CH, n, S5_CH) for i in range(4)]
                tt(tmp[0], br, f_re, ALU.mult)
                tt(tmp[1], bi, f_im, ALU.mult)
                tt(tmp[2], br, f_im, ALU.mult)
                tt(tmp[3], bi, f_re, ALU.mult)
                dve.drain()
                tt(br, tmp[0], tmp[1], ALU.subtract)
                tt(bi, tmp[2], tmp[3], ALU.add).then_inc(*done("b_bar", part))

            def s5():
                tiles(("s5in", 1))
                tt(s5_dmat, ident.unsqueeze(1).to_broadcast([P, KC, P]), v("s5_d").unsqueeze(2).to_broadcast([P, KC, P]),
                   ALU.mult).then_inc(*done("s5_dmat"))
                dve.drain().then_inc(sem("s5_out"), 2)
                with dve.Fori(0, S5_CH // BATCH // 2) as g:
                    for j in range(2 * BATCH):
                        if j % BATCH == 0:
                            dve.wait_ge(sem("tables"), j // BATCH + 1 + 2 * g)
                        cos, sin = (table[j // BATCH][:, i, j % BATCH, :] for i in range(2))
                        cos2 = cos.unsqueeze(1).to_broadcast([P, 2, T])
                        dve.wait_ge(sem("bu"), j + 1 + 2 * BATCH * g)
                        bu = ps[j % 2][:].rearrange("p (a t) -> p a t", a=2)
                        tt(s5_a, bu, cos2, ALU.mult)
                        tt(s5_b[:, 0], bu[:, 1], sin, ALU.mult)
                        stt(s5_b[:, 1], bu[:, 0], -1.0, sin, ALU.mult, ALU.mult).then_inc(sem("bu_used"), 1)
                        dve.drain()
                        tt(s5_a, s5_a, s5_b, ALU.add)
                        dve.drain()
                        modulus = s5p[:, 3, bass.ds(j + 2 * BATCH * g, 1)].to_broadcast([P, T])
                        for i in range(2):
                            nc.vector.tensor_tensor_scan(s5_z[:, i], modulus, s5_a[:, i], 0.0, ALU.mult, ALU.add)
                        dve.drain()
                        q = s5_q[:, j % 2]
                        dve.wait_ge(sem("s5_out"), j + 1 + 2 * BATCH * g)
                        tt(q[:, 0], s5_z, cos2, ALU.mult)
                        stt(q[:, 1, 0], s5_z[:, 1], -1.0, sin, ALU.mult, ALU.mult)
                        tt(q[:, 1, 1], s5_z[:, 0], sin, ALU.mult).then_inc(sem("states_done"), 1)
                for c in range(KC):
                    dve.wait_ge(*at("gelu_high", c))
                    tt(r(O2r[:, c, :]), O2[:, c, :], H2r[:, c, :], ALU.subtract).then_inc(*done("gelu_split", c))
                for j in range(KC):
                    dve.wait_ge(*proj_at(("glu", 1), 2 * j))
                    dve.wait_ge(*at("glu_gate", j))
                    g = sig[:, j % 2, 0:T]
                    tt(g, g, ps[4 + (2 * j) % 4][:, 0:T], ALU.mult).then_inc(*done("glu_val", j))
                    dve.drain()
                    tt(XT2[:, j, :], XT2[:, j, :], g, ALU.add).then_inc(*done("res_dve", (("glu", 1), j)))
                    tiles(("glu", 1), j)

            def pooling():
                dve.wait_ge(*at("wide_zero", "pool"))
                dve.wait_ge(sem("counts_loaded"), 16)
                dve.drain()

                for half in range(2):
                    a, b = hpad
                    c0 = 4 * half
                    nc.vector.tensor_copy(a[:, :, 16:], H2[:, c0:c0 + 4, :])
                    dve.drain()
                    n, lo_c = 0, 0
                    for step in range(2 * half + 2):
                        d = 1 << step
                        if step == 2 * half + 1:
                            lo_c = 2
                        src, dst = (a, b) if n % 2 == 0 else (b, a)
                        tt(dst[:, lo_c:4, 16:], src[:, lo_c:4, 16:], src[:, lo_c:4, 16 - d:16 - d + T], ALU.add)
                        n += 1
                        dve.drain()
                        if step == 2 * half or step == 2 * half + 1:
                            g = step
                            res, r0 = dst, (0 if step == 2 * half else 2)
                            o = O2[:, 2 * g:2 * g + 2, :]
                            tt(o, res[:, r0:r0 + 2, 16:], counts[:, g, :].unsqueeze(1).to_broadcast([P, 2, T]), ALU.mult)
                            dve.drain()
                            tt(o, o, H2[:, 2 * g:2 * g + 2, :], ALU.subtract).then_inc(*done("pooled", g))
                for j in range(KC):
                    dve.wait_ge(*at("proj", (("poolw", 2), j)))
                    t = sig[:, j % 2, 0:T]
                    ts(t, ps[j % 4][:, 0:T], v("pool_b")[:, j:j + 1], v("pool_s")[:, j:j + 1], ALU.add, ALU.mult)
                    dve.drain()
                    tt(XT2[:, j, :], XT2[:, j, :], t, ALU.add).then_inc(*done("res_dve", (("poolw", 2), j)))

            ada(0)
            for l in range(DEPTH):
                last = l == DEPTH - 1
                streams = 1 if last else 2
                tok = slice(0, streams * T)
                bias = lambda which: lambda c, s: mod[l][:, 24 * which + c, s:s + 1]
                scale(("mix", l), 2, lambda c, s: gsc[l][:, 0, c, s:s + 1], bias(0), SB3)
                gate(l)
                conformer(l)
                sconv(l)
                if l == 0:
                    s5_rates()
                ada(l + 1)
                steps(l)
                centre(l, streams * T)
                ssd(l, 1, not last)
                ssd(l, 0, True)
                mixer_norms(l, tok)
                residual(("wout", l), [0, 1, 2, 3], lambda j, s: mod[l][:, 16 + j, s:s + 1], streams)
                dve.drain()
                scale(("ffn", l), streams, lambda c, s: gsc[l][:, 1, c, s:s + 1], bias(1), MIX_r)
                dve.drain()
                router(l, 2 * streams)
                if last:
                    s5_powers()
                moe(l, TB * streams)
                for s in range(streams):
                    add_sum(("moe", l, s), lambda c: mod[l][:, 40 + c, s:s + 1], s)
            dve.wait_ge(*at("root", ("final1",)))
            nc.vector.reciprocal(rstd[:, 0:T], rms[:, 0:T])
            dve.drain()
            for c in range(KC):
                stt(XT2[:, c, :], XT2[:, c, :], v("g_final")[:, c:c + 1], rstd[:, 0:T], ALU.mult, ALU.mult)\
                    .then_inc(*done("x_ready", ("first", c)))
            dve.drain()
            for a in range(2):
                make_low(dve, "dve", SPLIT_AT["foxf", 0] + a)
            for i_layer in range(4):
                name = (("fox", 0), ("s5",), ("pool",), ("fox", 3))[i_layer]
                scale(name, 1, lambda c, s: v(f"mix_g{i_layer}")[:, c:c + 1], None, None if i_layer == 2 else H2h)
                if i_layer in (0, 3):
                    fox(i_layer)
                elif i_layer == 1:
                    s5()
                else:
                    pooling()
                dve.drain()
                scale(("ffn2", i_layer), 1, lambda c, s: v(f"ffn_g{i_layer}")[:, c:c + 1], None, H2h)
                swiglu(("ffn", i_layer), FFN_SLICES, s5_matrices if i_layer == 0 else None)
                add_sum(("ffn", i_layer))
            scale(("final2",), 1, lambda c, s: v("fin_g")[:, c:c + 1])
            dve.drain().then_inc(*done("x_ready", "end"))

    return seen


def win_taken(l, j):
    ch = W_IN_ORDER[j]
    return ("gated", (l, ch)) if ch < 4 else ("win_act", (l, j))


def lay_out(a):
    def cols(w, idx=None):
        w = w if idx is None else w[:, idx]
        return w.reshape(KC, P, -1).transpose(1, 0, 2).reshape(P, -1)

    def chunks(ids):
        return np.concatenate([np.arange(P) + P * i for i in ids])

    def feat(x):
        return x.reshape(-1, P).T

    def rep(x):
        return np.broadcast_to(x.reshape(1, -1), (P, x.size))

    def slices(w, n):
        return [cols(w[:, TCOLS * i:TCOLS * i + TCOLS]) for i in range(n)]

    def padded(w):
        return np.pad(w, ((0, 0), (0, -w.shape[1] % TCOLS)))

    def gate_up(g, u, j):
        return cols(np.concatenate([g[:, P * j:P * j + P], u[:, P * j:P * j + P]], 1))

    d = {}
    halves = EXPERT_FF // P
    d["ada"] = np.stack([t for l in range(DEPTH) for t in slices(a["w_ada"][l], ADA_TILES)])
    d["win"] = np.stack([t for l in range(DEPTH) for t in slices(padded(a["w_in"][l][:, np.concatenate([chunks(W_IN_ORDER), np.arange(2560, 2576)])]), WIN_TILES)])
    d["rt"] = np.stack([cols(padded(np.concatenate([a["w_router_group"][l], a["w_router_expert"][l]], 1))) for l in range(DEPTH)])
    d["foxf"] = np.stack([cols(padded(a["fox_w_in_2"][j][:, 3 * D:])) for j in range(2)])
    d["wout"] = np.stack([t for l in range(DEPTH) for t in slices(a["w_out"][l], HALF_D)])
    d["moe"] = np.stack([gate_up(a["w_gate"][l, e], a["w_up"][l, e], j)
                         for l in range(DEPTH) for e in range(EXPERTS) for j in range(halves)])
    d["moe_down"] = a["w_down"].reshape(-1, P, D)
    qkv = np.concatenate([np.arange(D) + 2 * D, np.arange(2 * D)])
    d["foxin"] = np.stack([t for j in range(2) for t in slices(a["fox_w_in_2"][j][:, qkv], 3 * HALF_D)])
    d["foxout"] = np.stack([t for j in range(2) for t in slices(a["fox_w_out_2"][j], HALF_D)])
    d["s5in"] = np.stack(slices(a["s5_w_in_2"][0], HALF_D))
    pairs = chunks([i for j in range(KC) for i in (j, KC + j)])
    d["glu"] = np.stack(slices(a["s5_w_glu_2"][0][:, pairs], 2 * HALF_D))
    d["poolw"] = a["pool_w_2"][0].reshape(POOLS, 2, P, 2 * P).transpose(2, 0, 1, 3).reshape(1, P, -1)
    f = FFN_SLICES * FF
    d["ffn"] = np.stack([gate_up(a["ffn_w_gate_up_2"][i][:, :f], a["ffn_w_gate_up_2"][i][:, f:], j)
                         for i in range(4) for j in range(FFN_SLICES)])
    d["ffn_down"] = a["ffn_w_down_2"].reshape(-1, P, D)

    def by_state(re, im):
        o = np.zeros((P, 2, S5_CH, 2, 16), np.float32)
        for r, m in enumerate((re, im)):
            x = m.reshape(S5_CH, 2, 64, 16)
            for g in range(2):
                o[64 * g:64 * g + 64, r, :, g, :] = x[:, g].transpose(1, 0, 2)
        return o.reshape(P, -1)

    d["s5_b"] = by_state(a["s5_b_re_2"][0], a["s5_b_im_2"][0])
    d["s5_c"] = by_state(a["s5_c_re_2"][0].transpose(0, 2, 1), a["s5_c_im_2"][0].transpose(0, 2, 1))

    vec = {"c2": np.stack([feat(a["c"][0]), feat(a["c_ctx"])], 2)}
    two = lambda x: np.stack([feat(x), feat(x)], 2)
    state = lambda x: x.reshape(S5_CH, P).T
    for l in range(DEPTH):
        vec[f"b_ada{l}"] = two(a["b_ada"][l])
        vec[f"g_mix{l}"], vec[f"g_ffn{l}"] = two(a["g_mix"][l]), two(a["g_ffn"][l])
        vec[f"conv_w{l}"] = a["conv_w"][l].T.reshape(4, P, TAPS).transpose(1, 0, 2)
        vec[f"conv_b{l}"], vec[f"ln_g{l}"] = feat(a["conv_b"][l]), feat(a["conv_ln_g"][l])
        vec[f"ln_b{l}"], vec[f"ssd_g{l}"] = feat(a["conv_ln_b"][l]), feat(a["ssd_norm_g"][l])
        vec[f"d_skip{l}"] = feat(np.repeat(a["d_skip"][l], HD))
        vec[f"sconv_w{l}"] = a["ssd_conv_w"][l].T.reshape(8, P, STAPS).transpose(1, 0, 2)
        vec[f"sconv_b{l}"] = feat(a["ssd_conv_b"][l])
        vec[f"dt_bias{l}"], vec[f"a_log{l}"] = rep(a["dt_bias"][l]), rep(a["a_log"][l])
        vec[f"fox_b{l}"] = rep(a["fox_b_f_2"][l])
        vec[f"b_rt{l}"] = rep(np.concatenate([a["b_router_group"][l], a["b_router_expert"][l]]))
    for i in range(4):
        vec[f"mix_g{i}"], vec[f"ffn_g{i}"] = feat(a["mix_norm_g_2"][i]), feat(a["ffn_norm_g_2"][i])
    vec["g_final"], vec["fin_g"], vec["s5_d"] = feat(a["g_final"]), feat(a["final_norm_g_2"]), feat(a["s5_d_2"][0])
    vec["pool_b"], vec["pool_s"] = feat(a["pool_b_2"][0]), feat(a["pool_scale_2"][0])
    vec["a_re"], vec["a_im"] = state(a["s5_a_re_2"][0]), state(a["s5_a_im_2"][0])
    vec["log_dt"] = state(np.repeat(a["s5_log_dt_2"][0], 64))
    d["vec"] = np.concatenate([vec[n].reshape(P, -1) for n, _ in VEC_SHAPES], 1)
    xt = np.concatenate([a["x"][0], a["ctx"][0]], 0)
    d["xt"] = xt.T.reshape(KC, P, 2 * T).transpose(1, 0, 2).reshape(P, -1)
    d["con"], d["msk"], pool = const_arrays()
    d["pool_counts"] = pool.reshape(P, -1)
    return {n: np.ascontiguousarray(x) for n, x in d.items()}


def shaped(dram):
    r = dict(dram)
    r["xt"] = dram["xt"].rearrange("p (a b) -> p a b", a=KC)
    for n in ("s5_b", "s5_c"):
        r[n] = dram[n].rearrange("p (a b c) -> p a b c", a=2, b=S5_CH)
    r["pool_counts"] = dram["pool_counts"].rearrange("p (a b) -> p a b", a=POOLS)
    return r


def declare(nc, arrays):
    dram = {n: nc.dram_tensor(f"in_{n}", x.shape, mybir.dt.from_np(x.dtype), kind="ExternalInput").ap()
            for n, x in arrays.items()}
    return shaped(dram), nc.dram_tensor("out_0", (P, KC * T), F32, kind="ExternalOutput").ap()


def kernel(**inputs):
    import concourse.bacc as _bacc
    from concourse.bass_utils import run_bass_kernel_spmd as _run

    arrays = lay_out({n: np.asarray(x) for n, x in inputs.items()})
    counting = _bacc.Bacc("TRN2", target_bir_lowering=False, num_devices=1)
    known = program(counting, *declare(counting, arrays), {})
    nc = _bacc.Bacc("TRN2", target_bir_lowering=False, num_devices=1)
    program(nc, *declare(nc, arrays), known)
    r = _run(nc, [{f"in_{n}": x for n, x in arrays.items()}], core_ids=[0])
    o = np.asarray(r.results[0]["out_0"]).reshape(P, KC, T)
    return o.transpose(2, 1, 0).reshape(1, T, D)
```
